# Optimizing a Trainium2 kernel written in Bass

```python
import math
import jax, jax.numpy as jnp
from jax import lax
import numpy as np

D_MODEL = 1024
BATCH = 1
SEQ = 256
DEPTH = 1
DEC_BATCH = 1
DEC_SEQ = 1024
PAST_LEN = 128

HEAD_DIM = 64
A_HEADS = 8
B_Q_HEADS = 8
B_KV_HEADS = 2
B_GROUP = B_Q_HEADS // B_KV_HEADS
A_WIDTH = A_HEADS * HEAD_DIM
B_WIDTH = B_Q_HEADS * HEAD_DIM
KV_B_WIDTH = B_KV_HEADS * HEAD_DIM
MIX_WIDTH = A_WIDTH + B_WIDTH
IN_WIDTH = 3 * A_WIDTH + B_WIDTH + 2 * KV_B_WIDTH
DILATION_PAIRS = ((128, 1), (512, 4), (2048, 16))
B_RADIUS = 128
ROT_DIM = HEAD_DIM // 4
ROPE_THETA = 500000.0
N_KEYS = 128
N_EXPERTS = N_KEYS * N_KEYS
PEER_HEADS = 8
PEER_TOPK = 16
KEY_HALF = 128
QUERY_DIM = 2 * KEY_HALF
PEER_CHUNK = 128
LN_EPS = 1e-5
RMS_EPS = 1e-6
DN_ALPHA = (2 * DEPTH) ** 0.25
DN_BETA = (8 * DEPTH) ** -0.25

kernel_name = 'hymba_dilated_swa_peer_encoder'

def _layer_norm(x, g, b):
    xf = x.astype(jnp.float32)
    mu = jnp.mean(xf, axis=-1, keepdims=True)
    var = jnp.mean(jnp.square(xf - mu), axis=-1, keepdims=True)
    y = (xf - mu) * lax.rsqrt(var + LN_EPS) * g.astype(jnp.float32) + b.astype(jnp.float32)
    return y.astype(x.dtype)

def _rms_norm(x, g):
    xf = x.astype(jnp.float32)
    y = xf * lax.rsqrt(jnp.mean(jnp.square(xf), axis=-1, keepdims=True) + RMS_EPS)
    return y * g.astype(jnp.float32)

def _rope_partial(t, pos):
    half = ROT_DIM // 2
    inv = ROPE_THETA ** (-jnp.arange(half, dtype=jnp.float32) * 2.0 / ROT_DIM)
    ang = pos.astype(jnp.float32)[:, None] * inv[None, :]
    cos = jnp.cos(ang)[None, :, None, :]
    sin = jnp.sin(ang)[None, :, None, :]
    t1 = t[..., :half].astype(jnp.float32)
    t2 = t[..., half:ROT_DIM].astype(jnp.float32)
    rot = jnp.concatenate([t1 * cos - t2 * sin, t2 * cos + t1 * sin], axis=-1).astype(t.dtype)
    return jnp.concatenate([rot, t[..., ROT_DIM:]], axis=-1)

def _banded_attention(q, k, v, radius, block, sink=None):
    n, L, hk, g, dh = q.shape
    nb = -(-L // block)
    lp = nb * block
    qp = jnp.pad(q, ((0, 0), (0, lp - L), (0, 0), (0, 0), (0, 0)))
    kp = jnp.pad(k, ((0, 0), (block, lp - L + block), (0, 0), (0, 0)))
    vp = jnp.pad(v, ((0, 0), (block, lp - L + block), (0, 0), (0, 0)))
    qb = qp.reshape(n, nb, block, hk, g, dh)

    def key_blocks(t):
        return jnp.concatenate(
            [t[:, j * block:j * block + lp].reshape(n, nb, block, hk, dh) for j in range(3)], axis=2)

    kb = key_blocks(kp)
    vb = key_blocks(vp)
    starts = jnp.arange(nb)[:, None] * block
    qpos = starts + jnp.arange(block)[None, :]
    kpos = starts + jnp.arange(3 * block)[None, :] - block
    valid = (jnp.abs(kpos[:, None, :] - qpos[:, :, None]) <= radius) \
        & (kpos >= 0)[:, None, :] & (kpos < L)[:, None, :]
    s = jnp.einsum('nbqhgd,nbkhd->nbhgqk', qb, kb).astype(jnp.float32) * (dh ** -0.5)
    s = jnp.where(valid[None, :, None, None], s, -jnp.inf)
    m = jnp.max(s, axis=-1)
    if sink is not None:
        sk = sink.astype(jnp.float32)[None, None, :, :, None]
        m = jnp.maximum(m, sk)
    p = jnp.exp(s - m[..., None])
    den = jnp.sum(p, axis=-1)
    if sink is not None:
        den = den + jnp.exp(sk - m)
    o = jnp.einsum('nbhgqk,nbkhd->nbqhgd', (p / den[..., None]).astype(v.dtype), vb)
    o = o.reshape(n, lp, hk, g, dh)[:, :L]
    lse = (m + jnp.log(den)).transpose(0, 1, 4, 2, 3).reshape(n, lp, hk, g)[:, :L]
    return o, lse

def _dilated_branch(q, k, v, window, dilation):
    b, s, h, dh = q.shape
    L = s // dilation
    radius = window // (2 * dilation)

    def split(t):
        return t.reshape(b, L, dilation, h, dh).transpose(0, 2, 1, 3, 4).reshape(b * dilation, L, h, dh)

    o, lse = _banded_attention(split(q)[:, :, :, None], split(k), split(v), radius, radius)
    o = o[:, :, :, 0].reshape(b, dilation, L, h, dh).transpose(0, 2, 1, 3, 4).reshape(b, s, h, dh)
    lse = lse[..., 0].reshape(b, dilation, L, h).transpose(0, 2, 1, 3).reshape(b, s, h)
    return o, lse

def _token_mixer(h, w_in, attn_sink, gn_a, gn_b, w_out):
    b, s, _ = h.shape
    pos = jnp.arange(s)
    proj = h @ w_in
    cuts = [A_WIDTH, 2 * A_WIDTH, 3 * A_WIDTH, 3 * A_WIDTH + B_WIDTH, 3 * A_WIDTH + B_WIDTH + KV_B_WIDTH]
    qa, ka, va, qb, kb, vb = jnp.split(proj, cuts, axis=-1)
    qa = _rope_partial(qa.reshape(b, s, A_HEADS, HEAD_DIM), pos)
    ka = _rope_partial(ka.reshape(b, s, A_HEADS, HEAD_DIM), pos)
    va = va.reshape(b, s, A_HEADS, HEAD_DIM)
    qb = _rope_partial(qb.reshape(b, s, B_Q_HEADS, HEAD_DIM), pos)
    kb = _rope_partial(kb.reshape(b, s, B_KV_HEADS, HEAD_DIM), pos)
    vb = vb.reshape(b, s, B_KV_HEADS, HEAD_DIM)

    outs, lses = [], []
    for window, dilation in DILATION_PAIRS:
        o, l = _dilated_branch(qa, ka, va, window, dilation)
        outs.append(o.astype(jnp.float32))
        lses.append(l)
    wts = jax.nn.softmax(jnp.stack(lses), axis=0)
    oa = jnp.einsum('rbsh,rbshd->bshd', wts, jnp.stack(outs)).reshape(b, s, A_WIDTH)

    ob, _ = _banded_attention(qb.reshape(b, s, B_KV_HEADS, B_GROUP, HEAD_DIM), kb, vb,
                              B_RADIUS, B_RADIUS, attn_sink.reshape(B_KV_HEADS, B_GROUP))
    ob = ob.reshape(b, s, B_WIDTH)

    merged = jnp.concatenate([_rms_norm(oa, gn_a), _rms_norm(ob, gn_b)], axis=-1).astype(h.dtype)
    return merged @ w_out

def _peer(h, w_query, sub_keys, expert_down, expert_up):
    b, s, d = h.shape
    chunks = h.reshape(b * s // PEER_CHUNK, PEER_CHUNK, d)
    keys = sub_keys.astype(jnp.float32)

    def retrieve(hc):
        t = hc.shape[0]
        q = (hc @ w_query).reshape(t, PEER_HEADS, 2, KEY_HALF).astype(jnp.float32)
        sh = jnp.einsum('thpd,hpkd->thpk', q, keys)
        top_s, top_i = lax.top_k(sh, PEER_TOPK)
        cand = (top_s[:, :, 0, :, None] + top_s[:, :, 1, None, :]).reshape(t, PEER_HEADS, PEER_TOPK * PEER_TOPK)
        best_s, best = lax.top_k(cand, PEER_TOPK)
        i1 = jnp.take_along_axis(top_i[:, :, 0], best // PEER_TOPK, axis=-1)
        i2 = jnp.take_along_axis(top_i[:, :, 1], best % PEER_TOPK, axis=-1)
        idx = i1 * N_KEYS + i2
        gate = jax.nn.softmax(best_s, axis=-1)
        u = expert_down[idx]
        act = jax.nn.gelu(jnp.einsum('thkd,td->thk', u, hc).astype(jnp.float32), approximate=False)
        wgt = (gate * act).astype(hc.dtype)
        return jnp.einsum('thk,thkd->td', wgt, expert_up[idx])

    return lax.map(retrieve, chunks).reshape(b, s, d)

def _encoder_layer(x, c, w_mod, b_mod, w_in, attn_sink, gn_a, gn_b, w_out, ln1_g, ln1_b,
                   w_query, sub_keys, expert_down, expert_up, ln2_g, ln2_b):
    mod = (jax.nn.silu(c) @ w_mod + b_mod)[:, None, :]
    sh1, sc1, gt1, sh2, sc2, gt2 = jnp.split(mod, 6, axis=-1)
    h = x * (1 + sc1) + sh1
    x = _layer_norm(DN_ALPHA * x + (1 + gt1) * _token_mixer(h, w_in, attn_sink, gn_a, gn_b, w_out), ln1_g, ln1_b)
    h = x * (1 + sc2) + sh2
    x = _layer_norm(DN_ALPHA * x + (1 + gt2) * _peer(h, w_query, sub_keys, expert_down, expert_up), ln2_g, ln2_b)
    return x

def setup_inputs(seed: int = 0) -> dict:
    key = jax.random.key(seed)
    ks = jax.random.split(key, 20)

    def nrm(k, shape, scale):
        return jax.random.normal(k, shape, jnp.float32) * scale

    D = D_MODEL
    return {
        'x_prompt': nrm(ks[0], (BATCH, SEQ, D), 1.0),
        'x_sample': nrm(ks[1], (DEC_BATCH, DEC_SEQ, D), 1.0),
        'c_prompt': nrm(ks[2], (BATCH, D), 1.0),
        'c_sample': nrm(ks[3], (DEC_BATCH, D), 1.0),
        'w_mod': nrm(ks[4], (DEPTH, D, 6 * D), 0.5 * D ** -0.5),
        'b_mod': nrm(ks[5], (DEPTH, 6 * D), 0.01),
        'w_in': nrm(ks[6], (DEPTH, D, IN_WIDTH), D ** -0.5),
        'attn_sink': nrm(ks[7], (DEPTH, B_Q_HEADS), 1.0),
        'gn_a': 1.0 + nrm(ks[8], (DEPTH, A_WIDTH), 0.02),
        'gn_b': 1.0 + nrm(ks[9], (DEPTH, B_WIDTH), 0.02),
        'w_out': nrm(ks[10], (DEPTH, MIX_WIDTH, D), DN_BETA * MIX_WIDTH ** -0.5),
        'ln1_g': 1.0 + nrm(ks[11], (DEPTH, D), 0.02),
        'ln1_b': nrm(ks[12], (DEPTH, D), 0.02),
        'w_query': nrm(ks[13], (DEPTH, D, PEER_HEADS * QUERY_DIM), D ** -0.5),
        'sub_keys': nrm(ks[14], (DEPTH, PEER_HEADS, 2, N_KEYS, KEY_HALF), KEY_HALF ** -0.5),
        'expert_down': nrm(ks[15], (DEPTH, N_EXPERTS, D), D ** -0.5),
        'expert_up': nrm(ks[16], (DEPTH, N_EXPERTS, D), DN_BETA),
        'ln2_g': 1.0 + nrm(ks[17], (DEPTH, D), 0.02),
        'ln2_b': nrm(ks[18], (DEPTH, D), 0.02),
    }

def reference(x_prompt, x_sample, c_prompt, c_sample, w_mod, b_mod, w_in, attn_sink, gn_a, gn_b, w_out,
              ln1_g, ln1_b, w_query, sub_keys, expert_down, expert_up, ln2_g, ln2_b):
    def trunk(x, c):
        for l in range(DEPTH):
            x = _encoder_layer(x, c, w_mod[l], b_mod[l], w_in[l], attn_sink[l], gn_a[l], gn_b[l], w_out[l],
                               ln1_g[l], ln1_b[l], w_query[l], sub_keys[l], expert_down[l], expert_up[l],
                               ln2_g[l], ln2_b[l])
        return x

    y_prompt = trunk(x_prompt, c_prompt)
    y_sample = trunk(x_sample, c_sample)
    return (y_prompt, y_sample)


_drawn_inputs = setup_inputs


def setup_inputs(seed=0):
    import zlib

    import numpy as np

    out = dict(_drawn_inputs(seed))
    spreads = {}
    factors = {'attn_sink': 7.083, 'ln2_g': 2.837, 'ln2_b': 2.901}
    for name, (base, spread) in spreads.items():
        noise = np.random.default_rng([zlib.crc32(name.encode()), seed]).standard_normal(out[name].shape)
        drawn = base * np.exp(spread * noise) if base else spread * noise
        out[name] = __import__('jax').numpy.asarray(drawn.astype(out[name].dtype))
    for name, factor in factors.items():
        out[name] = (out[name] * factor).astype(out[name].dtype)
    return out
```

```python
from contextlib import ExitStack

import numpy as np

import concourse.bass as bass
from concourse import mybir

P = 128
D = 1024
DC = D // P
SEQS = ((0, 2), (2, 8))
TILES = 10
HD = 64
HALF = 8
AH, BH, BKV = 8, 8, 2
HEADS = AH + BH
QA, KA, VA, QB, KVB = 0, 512, 1024, 1536, 2048
INW = 2304
N_KEYS = 128
PH = 8
TOPK = 16
SLOTS = 14
BIG = 1.0e30
ALPHA = 2.0 ** 0.25
LN_EPS = 1e-5
RMS_EPS = 1e-6

ALU = mybir.AluOpType
ACT = mybir.ActivationFunctionType
F32 = mybir.dt.float32
U32 = mybir.dt.uint32
AX_X = mybir.AxisListType.X


def first_slot(tile0):
    return 1 if tile0 == 0 else 5


def b_head(j):
    return j // 2 + (BH // BKV) * (j % 2)


def hold(eng):
    eng.nop(nofuse=True)


class Chain:

    def __init__(self, eng, sem):
        self.eng, self.sem, self.n = eng, sem, 0

    def __call__(self, ins):
        ins.then_inc(self.sem, 1)
        self.n += 1
        return self.n

    def wait(self, n=None):
        self.eng.wait_ge(self.sem, self.n if n is None else n)

    def then(self, ins):
        self(ins)
        self.wait()

    def close(self):
        if self.n:
            self.wait()
            self.eng.sem_clear(self.sem)
        self.n = 0



def modulation(nc, io, keep):
    CH, BUFS = 512, 4
    NCH = 6 * D // CH
    with ExitStack() as ctx:
        def sb(name, shape, dt=F32):
            return ctx.enter_context(nc.sbuf_tensor(name, shape, dt))

        def sem(name):
            return ctx.enter_context(nc.semaphore(name))

        wm = [sb(f"wm{b}", [P, DC, CH]) for b in range(BUFS)]
        c_t = sb("c_t", [P, 2 * DC])
        neg_e = sb("neg_e", [P, 2 * DC])
        sig = sb("sig", [P, 2 * DC])
        silu = sb("silu", [P, 2 * DC])
        bias = sb("bias", [2, 6 * D])
        mod = sb("mod", [2, 6 * D])
        zeros = sb("zeros", [P, P])
        rows = [ctx.enter_context(nc.psum_tensor(f"rows{b}", [P, CH], F32)) for b in range(2)]
        cols = ctx.enter_context(nc.psum_tensor("cols", [P, 512], F32))

        small_in = sem("m_small_in")
        w_in_sem = [sem(f"m_w{b}") for b in range(BUFS)]
        exped = sem("m_exped")
        silu_ready = sem("m_silu_ready")
        row_done = sem("m_row_done")
        row_copied = sem("m_row_copied")
        mod_ready = sem("m_mod_ready")
        cols_done = sem("m_cols_done")
        zeroed = sem("m_zeroed")
        stored = sem("m_stored")
        block = ctx.enter_context(nc.Block())
        w_mod = io["w_mod"].rearrange("(c p) n -> p c n", p=P)

        @block.sync
        def _(sp):
            sp.dma_start(keep["ident"][:], io["ident"]).then_inc(keep["ident_loaded"], 16)
            sp.dma_start(c_t[:], io["c_t"]).then_inc(small_in, 16)
            sp.dma_start(bias[:], io["b_mod"].partition_broadcast(2)).then_inc(small_in, 16)
            for b in range(BUFS):
                sp.dma_start(wm[b][:], w_mod[:, :, b * CH:(b + 1) * CH]).then_inc(w_in_sem[b], 16)
            with sp.Fori(1, NCH // BUFS) as r:
                for b in range(BUFS):
                    sp.wait_ge(row_done, (r - 1) * BUFS + b + 1)
                    hold(sp)
                    sp.dma_start(wm[b][:], w_mod[:, :, bass.ds((r * BUFS + b) * CH, CH)]).then_inc(
                        w_in_sem[b], 16)
            sp.dma_start(keep["w_in_a"][:], io["w_in"].rearrange("(c p) n -> p c n", p=P)[:, :, 0:2048]
                         ).then_inc(keep["w_in_loaded"], 16)
            sp.dma_start(keep["w_in_b"][:], io["w_in"].rearrange("(c p) n -> p c n", p=P)[:, :, 2048:INW]
                         ).then_inc(keep["w_in_loaded"], 16)
            sp.wait_ge(mod_ready, 1)
            sp.dma_start(io["mod_rows"], mod[:, 2 * D:6 * D]).then_inc(stored, 16)
            sp.wait_ge(zeroed, 1)
            for slot in (0, 3, 4, 13):
                sp.dma_start(io["kb"][slot], zeros[:]).then_inc(stored, 16)
                sp.dma_start(io["vb"][slot], zeros[:]).then_inc(stored, 16)
            sp.wait_ge(stored, 16 * 9)
            for seq, (tile0, tiles) in enumerate(SEQS):
                sp.dma_start(io["gate2"][tile0:tile0 + tiles],
                             io["mod_rows"][seq:seq + 1, 3 * D:4 * D].rearrange("a n -> (a n)").partition_broadcast(tiles)
                             ).then_inc(stored, 16)
            sp.wait_ge(stored, 16 * 11)

        @block.scalar
        def _(act):
            act.wait_ge(small_in, 32)
            nc.scalar.activation(neg_e[:], c_t[:], ACT.Exp, scale=-1.0).then_inc(exped, 1)

        @block.vector
        def _(dve):
            chain = Chain(dve, keep["vector_chain"])
            dve.sem_inc(row_copied, 2)
            nc.vector.memset(zeros[:], 0.0).then_inc(zeroed, 1)
            dve.wait_ge(exped, 1)
            chain.then(nc.vector.tensor_scalar(neg_e[:], neg_e[:], 1.0, None, ALU.add))
            chain.then(nc.vector.reciprocal(sig[:], neg_e[:]))
            nc.vector.tensor_tensor(silu[:], c_t[:], sig[:], ALU.mult).then_inc(silu_ready, 1)
            with dve.Fori(0, NCH // 2) as r:
                for b in range(2):
                    j = r * 2 + b
                    dve.wait_ge(row_done, j + 1)
                    nc.vector.tensor_tensor(mod[:, bass.ds(j * CH, CH)], rows[b][0:2, :],
                                            bias[:, bass.ds(j * CH, CH)], ALU.add).then_inc(row_copied, 1)
            dve.wait_ge(row_copied, 2 + NCH)
            chain(nc.vector.tensor_scalar(mod[:, D:3 * D], mod[:, D:3 * D], 1.0, None, ALU.add))
            chain.then(nc.vector.tensor_scalar(mod[:, 4 * D:6 * D], mod[:, 4 * D:6 * D], 1.0, None, ALU.add))
            dve.sem_inc(mod_ready, 1)
            dve.wait_ge(cols_done, 1)
            chain(nc.vector.tensor_copy(keep["mod_cols"][:], cols[:, 0:4 * DC]))
            chain.close()

        @block.tensor
        def _(pe):
            pe.wait_ge(silu_ready, 1)
            with pe.Fori(0, NCH // BUFS) as r:
                for b in range(BUFS):
                    pe.wait_ge(w_in_sem[b], (r + 1) * 16)
                    pe.wait_ge(row_copied, r * BUFS + b + 1)
                    for c in range(DC):
                        mm = nc.tensor.matmul(rows[b % 2][0:2, :], silu[:, 2 * c:2 * c + 2], wm[b][:, c, :],
                                              start=(c == 0), stop=(c == DC - 1))
                    mm.then_inc(row_done, 1)
            pe.wait_ge(mod_ready, 1)
            pe.wait_ge(keep["ident_loaded"], 16)
            for c in range(2 * DC):
                mm = nc.tensor.transpose(cols[:, 2 * c:2 * c + 2], mod[:, c * P:(c + 1) * P],
                                         keep["ident"][0:2, 0:2])
            mm.then_inc(cols_done, 1)



def projection(nc, io, keep):
    ORDER = (0, 1, 3, 4, 2)
    WIDTH = (512, 512, 512, 512, 256)
    with ExitStack() as ctx:
        def sb(name, shape, dt=F32):
            return ctx.enter_context(nc.sbuf_tensor(name, shape, dt))

        def sem(name):
            return ctx.enter_context(nc.semaphore(name))

        xt = [sb(f"xt{b}", [P, DC, P]) for b in range(2)]
        h1t = [sb(f"h1t{b}", [P, DC, P]) for b in range(2)]
        proj = [sb(f"proj{b}", [P, INW]) for b in range(2)]
        trig = [sb(f"trig{b}", [P, 2 * HALF]) for b in range(2)]
        rot_c = sb("rot_c", [P, 16, 2, HALF])
        rot_s = sb("rot_s", [P, 16, 2, HALF])
        qk_t = [sb(f"qk_t{b}", [P, 13, P]) for b in range(2)]
        acc = [ctx.enter_context(nc.psum_tensor(f"acc{c}", [P, 512], F32)) for c in range(5)]
        tr = [ctx.enter_context(nc.psum_tensor(f"tr{c}", [P, 4, P], F32)) for c in range(2)]

        x_loaded = [sem(f"p_x{b}") for b in range(2)]
        h1_ready = sem("p_h1_ready")
        proj_done = sem("p_proj_done")
        proj_copied = sem("p_proj_copied")
        rotated = sem("p_rotated")
        turned = sem("p_turned")
        q_copied = sem("p_q_copied")
        k_copied = sem("p_k_copied")
        stored = [sem(f"p_stored{b}") for b in range(2)]
        block = ctx.enter_context(nc.Block())
        STORES = 5

        def pairs(eng, emit):
            for seq, (tile0, tiles) in enumerate(SEQS):
                with eng.Fori(tile0 // 2, (tile0 + tiles) // 2) as i:
                    for b in range(2):
                        emit(seq, tile0, i, b)

        @block.sync
        def _(sp):
            def emit(seq, tile0, i, b):
                sp.wait_ge(h1_ready, i * 2 + b + 2)
                hold(sp)
                sp.dma_start(xt[b][:], io["x_t"][i * 2 + b]).then_inc(x_loaded[b], 16)
                sp.dma_start(trig[b][:], io["trig"][i * 2 + b]).then_inc(x_loaded[b], 16)
            pairs(sp, emit)

        @block.scalar
        def _(act):
            for b in range(2):
                act.sem_inc(stored[b], 16)
            act.sem_inc(proj_copied, 5)
            act.sem_inc(q_copied, 1)

            def emit(seq, tile0, i, b):
                t = i * 2 + b
                act.wait_ge(stored[b], (i * STORES + 1) * 16)
                for o, c in enumerate(ORDER):
                    act.wait_ge(proj_done, t * 5 + o + 1)
                    w = WIDTH[c]
                    nc.scalar.mul(proj[b][:, c * 512:c * 512 + w], acc[c][:, 0:w],
                                  HD ** -0.5 if c in (0, 3) else 1.0).then_inc(proj_copied, 1)
                for g in range(2):
                    act.wait_ge(turned, t * 4 + 2 * g + 1)
                    nc.scalar.mul(qk_t[b][:, 4 * g:4 * g + 4, :], tr[0][:], 1.0).then_inc(q_copied, 1)
                act.wait_ge(proj_copied, t * 5 + 10)
                act.wait_ge(q_copied, t * 2 + 3)
                act.wait_ge(k_copied, t * 2 + 3)
                hold(act)
                slot = t + first_slot(tile0) - tile0
                act.dma_start(io["qt"][t], qk_t[b][:, 0:8, :]).then_inc(stored[b], 16)
                act.dma_start(io["kt"][seq][:, :, bass.ds((t - tile0) * P, P)], qk_t[b][:, 8:12, :]
                              ).then_inc(stored[b], 16)
                act.dma_start(io["kb"][slot], qk_t[b][:, 12, :]).then_inc(stored[b], 16)
                act.dma_start(io["vb"][slot], proj[b][:, KVB + P:INW]).then_inc(stored[b], 16)
                act.dma_start(io["va"][seq][t - tile0], proj[b][:, VA:QB]).then_inc(stored[b], 16)
            pairs(act, emit)
            for b in range(2):
                act.wait_ge(stored[b], 16 * (STORES * TILES // 2 + 1))

        @block.vector
        def _(dve):
            chain = Chain(dve, keep["vector_chain"])
            dve.sem_inc(h1_ready, 2)
            dve.sem_inc(k_copied, 1)

            def emit(seq, tile0, i, b):
                t = i * 2 + b
                dve.wait_ge(x_loaded[b], (i + 1) * 32)
                dve.wait_ge(proj_copied, t * 5 + 1)
                for c in range(DC):
                    mc = keep["mod_cols"]
                    n = chain(nc.vector.tensor_scalar(
                        h1t[b][:, c, :], xt[b][:, c, :], mc[:, 2 * (DC + c) + seq:2 * (DC + c) + seq + 1],
                        mc[:, 2 * c + seq:2 * c + seq + 1], ALU.mult, ALU.add))
                chain.wait()
                dve.sem_inc(h1_ready, 1)
                for g, (first, heads, pieces) in enumerate(((QA, 16, 2), (QB, 10, 4))):
                    dve.wait_ge(proj_copied, t * 5 + 5 + pieces)
                    v = proj[b][:, first:first + heads * HD].rearrange("p (h d) -> p h d", d=HD)
                    v = v[:, :, 0:2 * HALF].rearrange("p h (e d) -> p h e d", e=2)
                    cos = trig[b][:, 0:HALF].unsqueeze(1).unsqueeze(1).to_broadcast([P, heads, 2, HALF])
                    sin = trig[b][:, HALF:2 * HALF].unsqueeze(1).to_broadcast([P, heads, HALF])
                    rc, rs = rot_c[:, 0:heads], rot_s[:, 0:heads]
                    chain(nc.vector.tensor_tensor(rc, v, cos, ALU.mult))
                    chain(nc.vector.tensor_tensor(rs[:, :, 0, :], v[:, :, 1, :], sin, ALU.mult))
                    chain(nc.vector.tensor_tensor(rs[:, :, 1, :], v[:, :, 0, :], sin, ALU.mult))
                    chain.wait()
                    chain(nc.vector.tensor_tensor(v[:, :, 0, :], rc[:, :, 0, :], rs[:, :, 0, :], ALU.subtract))
                    chain(nc.vector.tensor_tensor(v[:, :, 1, :], rc[:, :, 1, :], rs[:, :, 1, :], ALU.add))
                    chain.wait()
                    dve.sem_inc(rotated, 1)
                for g in range(2):
                    dve.wait_ge(turned, t * 4 + 2 * g + 2)
                    w = 4 if g == 0 else 1
                    nc.vector.tensor_copy(qk_t[b][:, 8 + 4 * g:8 + 4 * g + w, :], tr[1][:, 0:w, :]
                                          ).then_inc(k_copied, 1)
                chain.close()
            pairs(dve, emit)

        @block.tensor
        def _(pe):
            pe.wait_ge(keep["w_in_loaded"], 32)

            def emit(seq, tile0, i, b):
                t = i * 2 + b
                pe.wait_ge(h1_ready, t + 3)
                for o, c in enumerate(ORDER):
                    pe.wait_ge(proj_copied, t * 5 + o + 1)
                    w = WIDTH[c]
                    for k in range(DC):
                        rhs = (keep["w_in_a"][:, k, c * 512:c * 512 + w] if c < 4
                               else keep["w_in_b"][:, k, :])
                        mm = nc.tensor.matmul(acc[c][:, 0:w], h1t[b][:, k, :], rhs,
                                              start=(k == 0), stop=(k == DC - 1))
                    mm.then_inc(proj_done, 1)
                for g, (col, chunks, bank) in enumerate(((QA, 4, 0), (KA, 4, 1), (QB, 4, 0), (KVB, 1, 1))):
                    pe.wait_ge(rotated, t * 2 + 1 + g // 2)
                    pe.wait_ge((q_copied, k_copied)[bank], t * 2 + 1 + g // 2)
                    for k in range(chunks):
                        mm = nc.tensor.transpose(tr[bank][:, k, :], proj[b][:, col + k * P:col + (k + 1) * P],
                                                 keep["ident"][:])
                    mm.then_inc(turned, 1)
            pairs(pe, emit)



def attention(nc, io, keep, seq):
    tile0, tiles = SEQS[seq]
    S = tiles * P
    KT = S // P
    side = seq == 1
    DOWN, UP = 8, 4
    PER = 2 * TOPK
    M_AT, MIX_AT, LN_AT, H2_AT = 1, 3, 6, 10
    with ExitStack() as ctx:
        def sb(name, shape, dt=F32):
            return ctx.enter_context(nc.sbuf_tensor(f"a{seq}_{name}", shape, dt))

        def sem(name):
            return ctx.enter_context(nc.semaphore(f"a{seq}_{name}"))

        def ps(name, shape):
            return ctx.enter_context(nc.psum_tensor(f"a{seq}_{name}", shape, F32))

        k_t = sb("k_t", [P, 4, S])
        v_a = sb("v_a", [P, KT, 512])
        q_t = sb("q_t", [P, 8, P])
        mask_a = sb("mask_a", [P, S])
        mask_b = sb("mask_b", [P, 3 * P])
        k_b = sb("k_b", [P, 3, P])
        v_b = sb("v_b", [P, 3, P])
        rows = sb("rows", [P, 3, D])
        ln = sb("ln", [P, 2, D])
        sink = sb("sink", [P, BH])
        prob = [sb(f"prob{b}", [P, S if S > 384 else 384]) for b in range(2)]
        prob_t = [sb(f"prob_t{b}", [P, max(KT, 3), P]) for b in range(2)]
        heads_out = sb("heads_out", [P, D])
        merged = sb("merged", [P, D])
        merged_t = sb("merged_t", [P, DC, P])
        if side:
            free = keep["w_in_a"][:].rearrange("p c n -> p (c n)").rearrange("p (s d) -> p s d", d=D)
            down, up = free[:, 0:DOWN, :], free[:, DOWN:DOWN + UP, :]
            h2_p = [free[:, DOWN + UP + t, :] for t in range(2)]
            x_in, z = free[:, DOWN + UP + 2, :], free[:, DOWN + UP + 3, :]
            idx_down = [sb(f"idx_down{t}", [P, TOPK], U32) for t in range(2)]
            idx_up = [sb(f"idx_up{t}", [P, TOPK], U32) for t in range(2)]
            dots = [sb(f"dots{t}", [P, TOPK]) for t in range(2)]
            acts = [sb(f"acts{t}", [P, TOPK]) for t in range(2)]
            wgt = [sb(f"wgt{t}", [P, TOPK]) for t in range(2)]
            down_in = [sem(f"down_in{k}") for k in range(DOWN)]
            up_in = [sem(f"up_in{k}") for k in range(UP)]
            h2p_in, dotted, upped, activated = sem("h2p_in"), sem("dotted"), sem("upped"), sem("activated")
        else:
            x_in, z = sb("x_in", [P, D])[:], sb("z", [P, D])[:]
            gn = sb("gn", [P, DC])
        x2 = sb("x2", [P, D])
        h2 = merged
        mx = sb("mx", [P, HEADS])
        neg_m = sb("neg_m", [P, HEADS])
        den = sb("den", [P, HEADS])
        sink_e = sb("sink_e", [P, BH])
        r_den = sb("r_den", [P, HEADS])
        sq = sb("sq", [P, 8])
        rr = sb("rr", [P, 4])
        stats = sb("stats", [P, 12])
        mv = sb("mv", [P, 2])
        lr = sb("lr", [P, 4])
        eps = sb("eps", [P, 2])

        score = [ps(f"score{b}", [P, 1024]) for b in range(2)]
        turn = ps("turn", [P, 8, P])
        out_ps = [ps(f"out{b}", [P, 512]) for b in range(2)]

        const_in = sem("const_in")
        kv_in = sem("kv_in")
        qa_in, qb_in, win_in, mask_in, x_sem = sem("qa_in"), sem("qb_in"), sem("win_in"), sem("mask_in"), sem("x_in_s")
        scored, masked, exped = sem("scored"), sem("masked"), sem("exped")
        turned, copied = sem("turned"), sem("copied")
        summed, head_done = sem("summed"), sem("head_done")
        squared, merged_ready, merged_turned = sem("squared"), sem("merged_ready"), sem("merged_turned")
        merged_copied, den_ready = sem("merged_copied"), sem("den_ready")
        mixed, mix_read, stat_ready, rooted = sem("mixed"), sem("mix_read"), sem("stat_ready"), sem("rooted")
        x2_ready, h2_ready, h2_turned, h2_copied = (sem("x2_ready"), sem("h2_ready"), sem("h2_turned"),
                                                    sem("h2_copied"))
        x2a_ready, stored = sem("x2a_ready"), sem("stored")
        eps_ready = sem("eps_ready")
        block = ctx.enter_context(nc.Block())

        def keys_of(h):
            return KT if h < AH else 3

        def tiled(eng, body):
            body(0, True)
            with eng.Fori(1, tiles) as i:
                body(i, False)

        @block.sync
        def _(sp):
            sp.dma_start(k_t[:], io["kt"][seq]).then_inc(kv_in, 16)
            sp.dma_start(v_a[:], io["va"][seq].rearrange("n p c -> p n c")).then_inc(kv_in, 16)

            def wait(semaphore, value):
                sp.wait_ge(semaphore, value)
                hold(sp)

            def load(i, first):
                t = i + tile0
                slot = i + first_slot(tile0)
                if not first:
                    wait(scored, i * HEADS - AH)
                sp.dma_start(q_t[:, 0:4, :], io["qt"][t][:, 0:4, :]).then_inc(qa_in, 16)
                if not first:
                    wait(masked, i * HEADS - AH + 2)
                sp.dma_start(mask_a[:], io["mask_a"][i][:, 0:S]).then_inc(mask_in, 16)
                if not first:
                    wait(scored, i * HEADS)
                sp.dma_start(q_t[:, 4:8, :], io["qt"][t][:, 4:8, :]).then_inc(qb_in, 16)
                sp.dma_start(k_b[:], io["kb"][bass.ds(slot - 1, 3)].rearrange("s p k -> p s k")
                             ).then_inc(win_in, 16)
                if not first:
                    wait(masked, i * HEADS + 2)
                sp.dma_start(mask_b[:], io["mask_b"][t]).then_inc(mask_in, 16)
                if not first:
                    wait(summed, i * HEADS + 2)
                sp.dma_start(v_b[:], io["vb"][bass.ds(slot - 1, 3)].rearrange("s p k -> p s k")
                             ).then_inc(win_in, 16)
                if not first:
                    wait(x2_ready, i)
                    sp.dma_start(x_in, io["x"][t - 1]).then_inc(x_sem, 16)
                    return
                rows_dram = io["mod_rows"][seq:seq + 1, 0:3 * D].rearrange("a n -> (a n)")
                sp.dma_start(rows[:].rearrange("p a d -> p (a d)"), rows_dram.partition_broadcast(P)
                             ).then_inc(const_in, 16)
                for j in range(2):
                    sp.dma_start(ln[:, j, :], io["ln1"][j].partition_broadcast(P)).then_inc(const_in, 16)
                sp.dma_start(sink[:], io["attn_sink"].partition_broadcast(P)).then_inc(const_in, 16)
                if side:
                    for p in range(2):
                        sp.dma_start(h2_p[p], io["h2"][p]).then_inc(h2p_in, 16)
                else:
                    sp.dma_start(gn[:], io["gn"]).then_inc(keep["w_out_loaded"], 16)
                    sp.dma_start(keep["w_out"][:], io["w_out"].rearrange("(c p) n -> p c n", p=P)
                                 ).then_inc(keep["w_out_loaded"], 16)
                    sp.dma_start(keep["w_in_a"][:], io["w_query"].rearrange("(c p) n -> p c n", p=P)
                                 ).then_inc(keep["w_query_loaded"], 16)

            tiled(sp, load)
            sp.wait_ge(x2_ready, tiles)
            sp.dma_start(x_in, io["x"][tile0 + tiles - 1]).then_inc(x_sem, 16)

        @block.gpsimd
        def _(pool):
            chain = Chain(pool, keep["gpsimd_chain"])

            def tail(j):
                pool.wait_ge(x2_ready, j + 2)
                pool.wait_ge(h2_turned, j + 1)
                pool.wait_ge(stored, (j + 1) * 48)
                chain.then(nc.gpsimd.tensor_tensor(h2[:], x2[:], rows[:, 2, :], ALU.mult))
                chain.then(nc.gpsimd.tensor_tensor(h2[:], h2[:], rows[:, 1, :], ALU.add))
                pool.sem_inc(h2_ready, 1)

            def take_idx(dst, i, p):
                chain.then(nc.gpsimd.tensor_copy(dst[p][:], keep["idx_all"][:, bass.ds((i * 2 + p) * TOPK, TOPK)]))

            def gather(ring, table, index, landed):
                hold(pool)
                pool.indirect_dma_start(ring, None, table, bass.IndirectOffsetOnAxis(ap=index, axis=0)
                                        ).then_inc(landed, 16)

            def gather_down(i, h):
                for k in range(2 * h, 2 * h + 2):
                    pool.wait_ge(dotted, i * PER + k + 1)
                    gather(down[:, k % DOWN, :], io["down"], idx_down[h // 8][:, k % TOPK:k % TOPK + 1],
                           down_in[k % DOWN])

            def gather_up(i, h):
                for k in range(2 * h, 2 * h + 2):
                    pool.wait_ge(upped, i * PER + k - TOPK + 1)
                    gather(up[:, k % UP, :], io["up"], idx_up[1 - h // 8][:, k % TOPK:k % TOPK + 1],
                           up_in[k % UP])

            def body(i, first):
                for h in range(HEADS):
                    if h == 4:
                        take_idx(idx_down, i, 1)
                        take_idx(idx_up, i, 0)
                    gather_down(i, h)
                    if not (first and h < 8):
                        gather_up(i, h)
                    if h == 12:
                        take_idx(idx_up, i, 1)
                        if i is not None:
                            take_next(i)
                    if not first and h == H2_AT:
                        tail(i - 1)
                chain.close()

            def take_next(i):
                if not (isinstance(i, int) and i == tiles - 1):
                    take_idx(idx_down, i + 1, 0)

            pool.wait_ge(const_in, 64)
            if side:
                take_idx(idx_down, 0, 0)
                chain.close()
                body(0, True)
                with pool.Fori(1, tiles - 1) as i:
                    body(i, False)
                body(tiles - 1, False)
                for h in range(8):
                    gather_up(tiles, h)
                tail(tiles - 1)
            else:
                with pool.Fori(0, tiles - 1) as j:
                    tail(j)
                    chain.close()
                tail(tiles - 1)
            chain.close()

        @block.scalar
        def _(act):
            act.wait_ge(const_in, 64)
            act.wait_ge(eps_ready, 1)
            act.sem_inc(copied, 1)
            act.sem_inc(stored, 48)

            def copy_probs(i, h):
                g = i * HEADS + h
                n = keys_of(h)
                act.wait_ge(turned, g + 1)
                act.wait_ge(summed, g + 1)
                nc.scalar.copy(prob_t[h % 2][:, 0:n, :], turn[:, 0:n, :]).then_inc(copied, 1)

            def copy_turned(count, n, j, dst_sem):
                act.wait_ge(count, n)
                act.wait_ge(stored, (j + 1) * 48)
                nc.scalar.copy(merged_t[:], turn[:]).then_inc(dst_sem, 1)

            def finish_head(i, h):
                g = i * HEADS + h
                col = (h if h < AH else AH + b_head(h - AH)) * HD
                act.wait_ge(den_ready, g + 1)
                act.wait_ge(summed, g + 3)
                nc.scalar.activation(heads_out[:, col:col + HD], out_ps[h % 2][:, 0:HD], ACT.Copy,
                                     scale=r_den[:, h:h + 1]).then_inc(head_done, 1)

            def activate(i, p):
                act.wait_ge(dotted, i * PER + (p + 1) * TOPK + DOWN)
                nc.scalar.activation(acts[p][:], dots[p][:], ACT.Gelu).then_inc(activated, 1)

            def body(i, first):
                if side and not first:
                    activate(i - 1, 1)
                if not first:
                    act.wait_ge(head_done, i * HEADS)
                    act.wait_ge(stored, i * 48)
                    for b in range(2):
                        nc.scalar.activation(merged[:, b * 512:(b + 1) * 512],
                                             heads_out[:, b * 512:(b + 1) * 512], ACT.Square,
                                             accum_out=sq[:, b:b + 1]).then_inc(squared, 1)
                    act.wait_ge(squared, i * 3 - 1)
                    nc.scalar.activation(sq[:, 2:4], sq[:, 0:2], ACT.Sqrt, bias=eps[:, 0:1], scale=1.0 / 512
                                         ).then_inc(squared, 1)
                for h in range(HEADS):
                    g = i * HEADS + h
                    if side and h == 8:
                        activate(i, 0)
                    act.wait_ge(masked, g + 3)
                    w = keys_of(h) * P
                    if h >= AH:
                        s_at = b_head(h - AH)
                        nc.scalar.activation(sink_e[:, h - AH:h - AH + 1], sink[:, s_at:s_at + 1], ACT.Exp,
                                             bias=neg_m[:, h:h + 1])
                    nc.scalar.activation(prob[h % 2][:, 0:w], prob[h % 2][:, 0:w], ACT.Exp,
                                         bias=neg_m[:, h:h + 1], accum_out=den[:, h:h + 1]).then_inc(exped, 1)
                    if h >= 1:
                        copy_probs(i, h - 1)
                    if not first and h == M_AT + 1:
                        copy_turned(merged_turned, i, i - 1, merged_copied)
                    if h >= 2:
                        finish_head(i, h - 2)
                    if not first and h == LN_AT:
                        root(i - 1)
                    if not first and h == H2_AT + 1:
                        after_h2(i - 1)
                copy_probs(i, HEADS - 1)
                finish_head(i, HEADS - 2)
                finish_head(i, HEADS - 1)

            def root(j):
                act.wait_ge(stat_ready, j + 1)
                nc.scalar.activation(lr[:, 0:1], mv[:, 1:2], ACT.Sqrt, bias=eps[:, 1:2], scale=1.0
                                     ).then_inc(rooted, 1)

            def after_h2(j):
                copy_turned(h2_turned, j + 2, j, h2_copied)
                act.wait_ge(h2_ready, j + 1)
                nc.scalar.mul(x2[:], x2[:], ALPHA).then_inc(x2a_ready, 1)
                act.wait_ge(x2a_ready, j + 1)
                act.wait_ge(h2_copied, j + 1)
                hold(act)
                act.dma_start(io["h2"][j + tile0], h2[:]).then_inc(stored, 16)
                act.dma_start(io["x2a"][j + tile0], x2[:]).then_inc(stored, 16)
                act.dma_start(io["h2t"][j + tile0], merged_t[:]).then_inc(stored, 16)

            tiled(act, body)
            last = tiles - 1
            act.wait_ge(head_done, tiles * HEADS)
            act.wait_ge(stored, tiles * 48)
            for b in range(2):
                nc.scalar.activation(merged[:, b * 512:(b + 1) * 512], heads_out[:, b * 512:(b + 1) * 512],
                                     ACT.Square, accum_out=sq[:, b:b + 1]).then_inc(squared, 1)
            act.wait_ge(squared, tiles * 3 - 1)
            nc.scalar.activation(sq[:, 2:4], sq[:, 0:2], ACT.Sqrt, bias=eps[:, 0:1], scale=1.0 / 512
                                 ).then_inc(squared, 1)
            if side:
                activate(last, 1)
            copy_turned(merged_turned, last + 1, last, merged_copied)
            root(last)
            after_h2(last)
            act.wait_ge(stored, 48 * (tiles + 1))

        @block.vector
        def _(dve):
            chain = Chain(dve, keep["vector_chain"])
            chain(nc.vector.memset(eps[:, 0:1], RMS_EPS))
            chain(nc.vector.memset(eps[:, 1:2], LN_EPS))
            chain.wait()
            dve.sem_inc(eps_ready, 1)
            dve.sem_inc(masked, 2)
            if side:
                dve.sem_inc(dotted, DOWN)
                dve.sem_inc(upped, UP)
                for p in range(2):
                    chain(nc.vector.memset(keep["sums"][p][:], 0.0))
            dve.sem_inc(x2_ready, 1)
            dve.wait_ge(const_in, 64)

            def newton(dst, root, var, tmp):
                chain.then(nc.vector.reciprocal(dst, root))
                chain.then(nc.vector.tensor_tensor(tmp, dst, dst, ALU.mult))
                chain.then(nc.vector.tensor_tensor(tmp, tmp, var, ALU.mult))
                chain.then(nc.vector.tensor_scalar(tmp, tmp, -0.5, 1.5, ALU.mult, ALU.add))
                chain.then(nc.vector.tensor_tensor(dst, dst, tmp, ALU.mult))

            def mask(i, h):
                g = i * HEADS + h
                w = keys_of(h) * P
                dve.wait_ge(scored, g + 1)
                if h == 0:
                    dve.wait_ge(mask_in, (i + 1) * 32)
                if h < AH:
                    m, least = mask_a[:], -3.0e38
                else:
                    m, least = mask_b[:], sink[:, b_head(h - AH):b_head(h - AH) + 1]
                hold(dve)
                chain.then(nc.vector.tensor_tensor_reduce(
                    prob[h % 2][:, 0:w], score[h % 2][:, 0:w], m, 1.0, least, ALU.add, ALU.max,
                    mx[:, h:h + 1]))
                nc.vector.tensor_scalar(neg_m[:, h:h + 1], mx[:, h:h + 1], -1.0, None, ALU.mult
                                        ).then_inc(masked, 1)

            def denominator(i, h):
                g = i * HEADS + h
                dve.wait_ge(exped, g + 1)
                if h >= AH:
                    chain.then(nc.vector.tensor_tensor(den[:, h:h + 1], den[:, h:h + 1],
                                                       sink_e[:, h - AH:h - AH + 1], ALU.add))
                nc.vector.reciprocal(r_den[:, h:h + 1], den[:, h:h + 1]).then_inc(den_ready, 1)

            def dot_row(i, k):
                row, p = down[:, k % DOWN, :], k // TOPK
                dve.wait_ge(down_in[k % DOWN], (i * (PER // DOWN) + k // DOWN + 1) * 16)
                nc.vector.tensor_tensor_reduce(row, row, h2_p[p], 1.0, 0.0, ALU.mult, ALU.add,
                                               dots[p][:, k % TOPK:k % TOPK + 1]).then_inc(dotted, 1)

            def add_row(i, k):
                p = 1 - k // TOPK
                n = i * PER + k - TOPK
                total = keep["sums"][p][:]
                dve.wait_ge(up_in[k % UP], (i * (PER // UP) + (k - TOPK) // UP + 1) * 16)
                dve.wait_ge(upped, n + UP)
                nc.vector.scalar_tensor_tensor(out=total, in0=up[:, k % UP, :],
                                               scalar=wgt[p][:, k % TOPK:k % TOPK + 1], in1=total,
                                               op0=ALU.mult, op1=ALU.add).then_inc(upped, 1)

            def weigh(i, p):
                dve.wait_ge(activated, i * 2 + p + 1)
                chain.then(nc.vector.tensor_tensor(
                    wgt[p][:], acts[p][:], keep["gate_all"][:, bass.ds((i * 2 + p) * TOPK, TOPK)], ALU.mult))

            def merge(j):
                dve.wait_ge(squared, j * 3 + 3)
                chain.then(nc.vector.tensor_scalar(sq[:, 4:6], sq[:, 0:2], 1.0 / 512, RMS_EPS,
                                                   ALU.mult, ALU.add))
                newton(rr[:, 0:2], sq[:, 2:4], sq[:, 4:6], rr[:, 2:4])
                for b in range(2):
                    chain(nc.vector.tensor_scalar(merged[:, b * 512:(b + 1) * 512],
                                                  heads_out[:, b * 512:(b + 1) * 512], rr[:, b:b + 1], None,
                                                  ALU.mult))
                chain.wait()
                dve.sem_inc(merged_ready, 1)

            def weigh_w_out(k):
                dve.wait_ge(keep["w_out_loaded"], 32)
                nc.vector.tensor_scalar(keep["w_out"][:, k, :], keep["w_out"][:, k, :], gn[:, k:k + 1], None,
                                        ALU.mult).then_inc(keep["w_out_weighed"], 1)

            def mix(j):
                dve.wait_ge(mixed, j + 1)
                buf = MIX_AT % 2
                chain(nc.vector.tensor_tensor(z, score[buf][:], rows[:, 0, :], ALU.mult))
                chain.wait()
                dve.sem_inc(mix_read, 1)
                dve.wait_ge(x_sem, (j + 1) * 16)
                chain.then(nc.vector.scalar_tensor_tensor(out=z, in0=x_in, scalar=ALPHA, in1=z,
                                                          op0=ALU.mult, op1=ALU.add))
                for b in range(2):
                    chain(nc.vector.bn_stats(stats[:, 6 * b:6 * b + 6], z[:, b * 512:(b + 1) * 512]))
                chain.wait()
                nc.vector.bn_aggr(mv[:], stats[:]).then_inc(stat_ready, 1)

            def layer_norm(j):
                dve.wait_ge(rooted, j + 1)
                dve.wait_ge(stat_ready, j + 1)
                chain.then(nc.vector.tensor_scalar(lr[:, 1:2], mv[:, 1:2], LN_EPS, None, ALU.add))
                newton(lr[:, 2:3], lr[:, 0:1], lr[:, 1:2], lr[:, 3:4])
                dve.wait_ge(stored, (j + 1) * 48)
                chain.then(nc.vector.tensor_scalar(x2[:], z, mv[:, 0:1], lr[:, 2:3],
                                                   ALU.subtract, ALU.mult))
                chain.then(nc.vector.tensor_tensor(x2[:], x2[:], ln[:, 0, :], ALU.mult))
                nc.vector.tensor_tensor(x2[:], x2[:], ln[:, 1, :], ALU.add).then_inc(x2_ready, 1)

            def body(i, first):
                for h in range(HEADS):
                    mask(i, h)
                    if side and not first and h == 0:
                        weigh(i - 1, 1)
                    if side and h == 8:
                        weigh(i, 0)
                    if not first and h == 0:
                        merge(i - 1)
                    if h >= 1:
                        denominator(i, h - 1)
                    for k in range(2 * h, 2 * h + 2) if side else ():
                        if not (first and h < 8):
                            add_row(i, k)
                        dot_row(i, k)
                    if seq == 0 and first and h >= 8:
                        weigh_w_out(h - 8)
                    if not first and h == MIX_AT + 1:
                        mix(i - 1)
                    if not first and h == LN_AT + 1:
                        layer_norm(i - 1)
                denominator(i, HEADS - 1)
                chain.close()

            if side:
                dve.wait_ge(h2p_in, 32)
                chain.close()
            tiled(dve, body)
            last = tiles - 1
            if side:
                weigh(last, 1)
            merge(last)
            mix(last)
            layer_norm(last)
            for k in range(TOPK) if side else ():
                add_row(tiles, k)
            if side:
                dve.wait_ge(upped, tiles * PER + UP)
            chain.close()

        @block.tensor
        def _(pe):
            ident = keep["ident"]
            pe.sem_inc(summed, 2)
            pe.sem_inc(h2_turned, 1)
            pe.wait_ge(kv_in, 32)

            def scores(i, h):
                g = i * HEADS + h
                pe.wait_ge(masked, g + 1)
                lo = (h % 2) * HD
                w = keys_of(h) * P
                q = q_t[lo:lo + HD, h // 2, :]
                if h == 0:
                    pe.wait_ge(qa_in, (i + 1) * 16)
                if h == AH:
                    pe.wait_ge(qb_in, (i + 1) * 16)
                    pe.wait_ge(win_in, (i + 1) * 32)
                for c in range(0, w, 512):
                    n = min(512, w - c)
                    rhs = k_t[lo:lo + HD, h // 2, c:c + n] if h < AH else \
                        k_b[lo:lo + HD].rearrange("p j k -> p (j k)")
                    mm = nc.tensor.matmul(score[h % 2][:, c:c + n], q, rhs, start=True, stop=True)
                mm.then_inc(scored, 1)

            def turn_probs(i, h):
                g = i * HEADS + h
                pe.wait_ge(exped, g + 1)
                pe.wait_ge(copied, g + 1)
                for k in range(keys_of(h)):
                    mm = nc.tensor.transpose(turn[:, k, :], prob[h % 2][:, k * P:(k + 1) * P], ident[:])
                mm.then_inc(turned, 1)

            def sum_values(i, h):
                g = i * HEADS + h
                pe.wait_ge(copied, g + 2)
                if h >= 2:
                    pe.wait_ge(head_done, g - 1)
                elif not isinstance(i, int):
                    pe.wait_ge(head_done, g - 1)
                n = keys_of(h)
                for k in range(n):
                    if h < AH:
                        v = v_a[:, k, h * HD:(h + 1) * HD]
                    else:
                        kv = (h - AH) % 2
                        v = v_b[:, k, kv * HD:(kv + 1) * HD]
                    mm = nc.tensor.matmul(out_ps[h % 2][:, 0:HD], prob_t[h % 2][:, k, :], v,
                                          start=(k == 0), stop=(k == n - 1))
                mm.then_inc(summed, 1)

            def turn_rows(src, count):
                for k in range(DC):
                    mm = nc.tensor.transpose(turn[:, k, :], src[:, k * P:(k + 1) * P], ident[:])
                mm.then_inc(count, 1)

            def turn_merged(j, g):
                pe.wait_ge(merged_ready, j + 1)
                pe.wait_ge(copied, g)
                turn_rows(merged, merged_turned)

            def mix(j):
                pe.wait_ge(merged_copied, j + 1)
                pe.wait_ge(keep["w_out_weighed"], DC)
                for c in range(2):
                    for k in range(DC):
                        mm = nc.tensor.matmul(score[MIX_AT % 2][:, c * 512:(c + 1) * 512], merged_t[:, k, :],
                                              keep["w_out"][:, k, c * 512:(c + 1) * 512],
                                              start=(k == 0), stop=(k == DC - 1))
                mm.then_inc(mixed, 1)

            def turn_h2(j, g):
                pe.wait_ge(h2_ready, j + 1)
                pe.wait_ge(mixed, j + 1)
                pe.wait_ge(copied, g)
                turn_rows(h2, h2_turned)

            def body(i, first):
                g0 = i * HEADS
                scores(i, 0)
                for h in range(HEADS):
                    if h + 1 < HEADS:
                        if not first and h + 1 == MIX_AT + 2:
                            pe.wait_ge(mix_read, i)
                        scores(i, h + 1)
                    if not first and h == M_AT + 1:
                        pe.wait_ge(merged_copied, i)
                    if not first and h == H2_AT + 1:
                        pe.wait_ge(h2_copied, i)
                    turn_probs(i, h)
                    if h >= 1:
                        sum_values(i, h - 1)
                    if not first and h == M_AT:
                        turn_merged(i - 1, g0 + h + 2)
                    if not first and h == MIX_AT:
                        mix(i - 1)
                    if not first and h == H2_AT:
                        turn_h2(i - 1, g0 + h + 2)
                sum_values(i, HEADS - 1)

            tiled(pe, body)
            last = tiles - 1
            turn_merged(last, tiles * HEADS + 1)
            pe.wait_ge(masked, tiles * HEADS + 2)
            mix(last)
            turn_h2(last, tiles * HEADS + 1)



class Retrieval:

    QW = 2 * N_KEYS
    LOW = -3.0e38

    def __init__(self, nc, keep, prefix, sb, sem, ps):
        self.nc, self.keep = nc, keep
        self.keys = sb("keys", [P, PH * self.QW])
        self.iota = sb("iota", [P, TOPK])
        self.h2t = sb("h2t", [P, DC, P])
        self.q, self.q_t = sb("q", [P, self.QW]), sb("q_t", [P, 2, P])
        self.sc = sb("sc", [P, 2, N_KEYS])
        self.sc2 = sb("sc2", [P, 2, N_KEYS])
        self.top = sb("top", [P, 2, TOPK])
        self.top_i, self.top_f = sb("top_i", [P, 2, TOPK], U32), sb("top_f", [P, 2, TOPK])
        self.cand, self.cand2 = sb("cand", [P, TOPK, TOPK]), sb("cand2", [P, TOPK, TOPK])
        self.best = [sb(f"best{b}", [P, TOPK]) for b in range(2)]
        self.best_i = sb("best_i", [P, TOPK], U32)
        self.pair_i, self.pair_f = sb("pair_i", [P, 2, TOPK], U32), sb("pair_f", [P, 2, TOPK])
        self.hot, self.hot2 = sb("hot", [P, 2, TOPK, TOPK]), sb("hot2", [P, 2, TOPK, TOPK])
        self.key_f = sb("key_f", [P, 2, TOPK])
        self.neg_b = [sb(f"neg_b{b}", [P, 1]) for b in range(2)]
        self.gate_e = [sb(f"gate_e{b}", [P, TOPK]) for b in range(2)]
        self.gate_s = [sb(f"gate_s{b}", [P, 1]) for b in range(2)]
        self.gate_r = sb("gate_r", [P, 1])
        self.q_ps, self.qt_ps, self.sc_ps = ps("q_ps", [P, 512]), ps("qt_ps", [P, 4, P]), ps("sc_ps", [P, 4, P])
        self.const_in, self.h2t_in = sem("r_const_in"), sem("h2t_in")
        self.q_done, self.q_copied = sem("q_done"), sem("q_copied")
        self.qt_done, self.qt_copied = sem("qt_done"), sem("qt_copied")
        self.sc_done, self.sc_copied = sem("sc_done"), sem("sc_copied")
        self.best_ready, self.gated, self.idx_ready = sem("best_ready"), sem("gated"), sem("idx_ready")

    def load(self, sp, io, tile):
        sp.dma_start(self.h2t[:], io["h2t"][tile]).then_inc(self.h2t_in, 16)
        sp.dma_start(self.keys[:], io["keys_t"]).then_inc(self.const_in, 16)
        sp.dma_start(self.iota[:], io["iota"]).then_inc(self.const_in, 16)

    def query(self, pe, m, e, tiles_in):
        nc, w_query = self.nc, self.keep["w_in_a"]
        pe.wait_ge(self.h2t_in, tiles_in * 16)
        pe.wait_ge(self.q_copied, m + 1)
        for k in range(DC):
            mm = nc.tensor.matmul(self.q_ps[:, 0:self.QW], self.h2t[:, k, :],
                                  w_query[:, k, bass.ds(e * self.QW, self.QW)],
                                  start=(k == 0), stop=(k == DC - 1))
        mm.then_inc(self.q_done, 1)
        pe.wait_ge(self.q_copied, m + 2)
        for h in range(2):
            mm = nc.tensor.transpose(self.qt_ps[:, h, :], self.q[:, h * P:(h + 1) * P], self.keep["ident"][:])
        mm.then_inc(self.qt_done, 1)
        pe.wait_ge(self.qt_copied, m + 1)
        pe.wait_ge(self.sc_copied, m + 1)
        for h in range(2):
            mm = nc.tensor.matmul(self.sc_ps[:, h, :], self.q_t[:, h, :],
                                  self.keys[:, bass.ds(e * self.QW + h * N_KEYS, N_KEYS)], start=True, stop=True)
        mm.then_inc(self.sc_done, 1)

    def start_act(self, act):
        act.sem_inc(self.q_copied, 1)
        act.sem_inc(self.sc_copied, 1)

    def move_query(self, act, m):
        nc = self.nc
        act.wait_ge(self.q_done, m + 1)
        nc.scalar.copy(self.q[:], self.q_ps[:, 0:self.QW]).then_inc(self.q_copied, 1)
        act.wait_ge(self.qt_done, m + 1)
        nc.scalar.copy(self.q_t[:], self.qt_ps[:, 0:2, :]).then_inc(self.qt_copied, 1)
        act.wait_ge(self.sc_done, m + 1)
        act.wait_ge(self.idx_ready, m + 1)
        nc.scalar.copy(self.sc[:], self.sc_ps[:, 0:2, :]).then_inc(self.sc_copied, 1)

    def gates(self, act, m, b):
        act.wait_ge(self.best_ready, m + 1)
        self.nc.scalar.activation(self.gate_e[b][:], self.best[b][:], ACT.Exp, bias=self.neg_b[b][:, 0:1],
                                  accum_out=self.gate_s[b][:, 0:1]).then_inc(self.gated, 1)

    def pick(self, dve, chain, m, b, idx, idx_free=None):
        nc, sc, sc2, top, top_i = self.nc, self.sc, self.sc2, self.top, self.top_i
        best, best_i, LOW = self.best[b], self.best_i, self.LOW
        dve.wait_ge(self.sc_copied, m + 2)
        hold(dve)
        for h in range(2):
            chain(nc.vector.max(top[:, h, 0:8], sc[:, h, :]))
        chain.wait()
        for h in range(2):
            chain(nc.vector.match_replace(sc2[:, h, :], top[:, h, 0:8], sc[:, h, :], LOW))
        chain.wait()
        for h in range(2):
            chain(nc.vector.max(top[:, h, 8:16], sc2[:, h, :]))
        for h in range(2):
            chain(nc.vector.max_index(top_i[:, h, 0:8], top[:, h, 0:8], sc[:, h, :]))
        chain.wait()
        chain(nc.vector.tensor_tensor(self.cand[:], top[:, 0, :].unsqueeze(2).to_broadcast([P, TOPK, TOPK]),
                                      top[:, 1, :].unsqueeze(1).to_broadcast([P, TOPK, TOPK]), ALU.add))
        for h in range(2):
            chain(nc.vector.max_index(top_i[:, h, 8:16], top[:, h, 8:16], sc2[:, h, :]))
        chain.wait()
        flat, flat2 = (v[:].rearrange("p a b -> p (a b)") for v in (self.cand, self.cand2))
        chain(nc.vector.max(best[:, 0:8], flat))
        chain(nc.vector.tensor_copy(self.top_f[:], top_i[:]))
        chain.wait()
        chain(nc.vector.match_replace(flat2, best[:, 0:8], flat, LOW))
        chain(nc.vector.max_index(best_i[:, 0:8], best[:, 0:8], flat))
        chain(nc.vector.tensor_scalar(self.neg_b[b][:, 0:1], best[:, 0:1], -1.0, None, ALU.mult))
        chain.wait()
        chain.then(nc.vector.max(best[:, 8:16], flat2))
        dve.sem_inc(self.best_ready, 1)
        chain.then(nc.vector.max_index(best_i[:, 8:16], best[:, 8:16], flat2))
        chain(nc.vector.tensor_scalar(self.pair_i[:, 0, :], best_i[:], 4, None, ALU.logical_shift_right))
        chain(nc.vector.tensor_scalar(self.pair_i[:, 1, :], best_i[:], TOPK - 1, None, ALU.bitwise_and))
        chain.wait()
        chain.then(nc.vector.tensor_copy(self.pair_f[:], self.pair_i[:]))
        shape = [P, 2, TOPK, TOPK]
        chain.then(nc.vector.tensor_tensor(
            self.hot[:], self.pair_f[:].unsqueeze(3).to_broadcast(shape),
            self.iota[:].unsqueeze(1).unsqueeze(1).to_broadcast(shape), ALU.is_equal))
        chain.then(nc.vector.tensor_tensor(self.hot2[:], self.hot[:],
                                           self.top_f[:].unsqueeze(2).to_broadcast(shape), ALU.mult))
        chain.then(nc.vector.tensor_reduce(self.key_f[:], self.hot2[:], AX_X, ALU.add))
        if idx_free:
            idx_free()
        nc.vector.scalar_tensor_tensor(out=idx, in0=self.key_f[:, 0, :], scalar=float(N_KEYS),
                                       in1=self.key_f[:, 1, :], op0=ALU.mult, op1=ALU.add
                                       ).then_inc(self.idx_ready, 1)


def prompt_retrieval(nc, io, keep):
    tiles = SEQS[0][1]
    with ExitStack() as ctx:
        def sb(name, shape, dt=F32):
            return ctx.enter_context(nc.sbuf_tensor(f"r_{name}", shape, dt))

        def sem(name):
            return ctx.enter_context(nc.semaphore(f"r_{name}"))

        def ps(name, shape):
            return ctx.enter_context(nc.psum_tensor(f"r_{name}", shape, F32))

        rt = Retrieval(nc, keep, "r", sb, sem, ps)
        idx = sb("idx", [P, TOPK], U32)
        block = ctx.enter_context(nc.Block())

        def each(eng, step):
            for t in range(tiles):
                with eng.Fori(0, PH // 2) as p:
                    for b in range(2):
                        step(p * 2 + b + t * PH, b, p * 2 + b, t)

        @block.sync
        def _(sp):
            rt.load(sp, io, 0)
            sp.wait_ge(rt.q_done, PH)
            sp.dma_start(rt.h2t[:], io["h2t"][1]).then_inc(rt.h2t_in, 16)

        @block.tensor
        def _(pe):
            pe.wait_ge(rt.const_in, 32)
            pe.wait_ge(keep["w_query_loaded"], 16)
            each(pe, lambda m, b, e, t: rt.query(pe, m, e, t + 1))

        @block.scalar
        def _(act):
            rt.start_act(act)

            def step(m, b, e, t):
                rt.move_query(act, m)
                rt.gates(act, m, b)
            each(act, step)

        @block.vector
        def _(dve):
            chain = Chain(dve, keep["vector_chain"])
            dve.sem_inc(rt.idx_ready, 1)
            dve.wait_ge(rt.const_in, 32)

            def step(m, b, e, t):
                rt.pick(dve, chain, m, b, idx[:])
                dve.wait_ge(rt.idx_ready, m + 2)
                at = (e * tiles + t) * TOPK
                chain(nc.vector.tensor_copy(keep["idx_all"][:, bass.ds(at, TOPK)], idx[:]))
                dve.wait_ge(rt.gated, m + 1)
                chain.then(nc.vector.reciprocal(rt.gate_r[:], rt.gate_s[b][:, 0:1]))
                chain(nc.vector.tensor_scalar(keep["gate_all"][:, bass.ds(at, TOPK)], rt.gate_e[b][:],
                                              rt.gate_r[:, 0:1], None, ALU.mult))
                chain.close()
            each(dve, step)



def experts(nc, io, keep):
    RING = 8
    tile0, tiles = SEQS[1]
    prompt_tiles = SEQS[0][1]
    with ExitStack() as ctx:
        def sb(name, shape, dt=F32):
            return ctx.enter_context(nc.sbuf_tensor(f"e_{name}", shape, dt))

        def sem(name):
            return ctx.enter_context(nc.semaphore(f"e_{name}"))

        def ps(name, shape):
            return ctx.enter_context(nc.psum_tensor(f"e_{name}", shape, F32))

        ident = keep["ident"]
        rt = Retrieval(nc, keep, "e", sb, sem, ps)
        ln = sb("ln", [P, 2, D])
        eps = sb("eps", [P, 1])
        h2 = sb("h2", [P, D])
        x2a = sb("x2a", [P, D])
        gate2 = sb("gate2", [P, D])
        z = sb("z", [P, D])
        y = sb("y", [P, D])
        down = sb("down", [P, RING, D])
        up = sb("up", [P, RING, D])
        idx = [sb(f"idx{b}", [P, TOPK], U32) for b in range(2)]
        dots = [sb(f"dots{b}", [P, TOPK]) for b in range(2)]
        acts = [sb(f"acts{b}", [P, TOPK]) for b in range(2)]
        wgt = sb("wgt", [P, TOPK])
        diag = [sb(f"diag{b}", [P, TOPK, P]) for b in range(2)]
        stats, mv, lr = sb("stats", [P, 12]), sb("mv", [P, 2]), sb("lr", [P, 4])

        acc = ps("acc", [P, D])

        const_in = sem("const_in")
        h2_in, res_in = sem("h2_in"), sem("res_in")
        down_in = [sem(f"down_in{s}") for s in range(RING)]
        up_in = [sem(f"up_in{s}") for s in range(RING)]
        dotted, activated = sem("dotted"), sem("activated")
        diag_ready, upped = sem("diag_ready"), sem("upped")
        stat_ready, rooted, y_ready, y_stored = sem("stat_ready"), sem("rooted"), sem("y_ready"), sem("y_stored")
        set_up = sem("set_up")
        block = ctx.enter_context(nc.Block())

        def first(n):
            return isinstance(n, int) and n == 0

        def steps(eng, step):
            step(0, 0, 0, 1, 0, True)

            def heads(t, last):
                with eng.Fori(0, PH // 2 - 1) as p:
                    for e in range(2):
                        step(t * PH + p * 2 + e + 1, 1 - e, t, p * 2 + e + 2, t, False)
                step(t * PH + PH - 1, 1, t, None if last else 0, t + 1, False)

            with eng.Fori(0, tiles - 1) as t:
                heads(t, False)
                step(t * PH + PH, 0, t + 1, 1, t + 1, True)
            heads(tiles - 1, True)

        @block.sync
        def _(sp):
            rt.load(sp, io, tile0)
            sp.dma_start(keep["w_in_a"][:], io["w_query"].rearrange("(c p) n -> p c n", p=P)
                         ).then_inc(keep["w_query_loaded"], 16)
            sp.dma_start(h2[:], io["h2"][tile0]).then_inc(h2_in, 16)
            for j in range(2):
                sp.dma_start(ln[:, j, :], io["ln2"][j].partition_broadcast(P)).then_inc(const_in, 16)

            for j in range(prompt_tiles + 1):
                if j:
                    sp.wait_ge(stat_ready, j)
                sp.dma_start(x2a[:], io["x2a"][j]).then_inc(res_in, 16)
                sp.dma_start(gate2[:], io["gate2"][j].partition_broadcast(P)).then_inc(res_in, 16)
                if j:
                    sp.wait_ge(y_ready, j)
                    sp.dma_start(io["y"][j - 1], y[:]).then_inc(y_stored, 16)

            def tile(t, last):
                if not last:
                    sp.wait_ge(rt.q_done, t * PH + PH)
                    hold(sp)
                    sp.dma_start(rt.h2t[:], io["h2t"][t + tile0 + 1]).then_inc(rt.h2t_in, 16)
                    sp.wait_ge(dotted, (t * PH + PH) * TOPK + RING)
                    hold(sp)
                    sp.dma_start(h2[:], io["h2"][t + tile0 + 1]).then_inc(h2_in, 16)
                    sp.wait_ge(stat_ready, t + tile0 + 1)
                    hold(sp)
                    sp.dma_start(x2a[:], io["x2a"][t + tile0 + 1]).then_inc(res_in, 16)
                    sp.dma_start(gate2[:], io["gate2"][t + tile0 + 1].partition_broadcast(P)).then_inc(res_in, 16)
                sp.wait_ge(y_ready, t + tile0 + 1)
                hold(sp)
                sp.dma_start(io["y"][t + tile0], y[:]).then_inc(y_stored, 16)

            with sp.Fori(0, tiles - 1) as t:
                tile(t, False)
            tile(tiles - 1, True)
            sp.wait_ge(y_stored, 16 * (TILES + 1))

        @block.gpsimd
        def _(pool):
            def gather(ring, table, index, landed):
                pool.indirect_dma_start(ring, None, table, bass.IndirectOffsetOnAxis(ap=index, axis=0)
                                        ).then_inc(landed, 16)

            def step(n, b, t, e_next, t_next, start):
                pool.wait_ge(rt.idx_ready, n + 2)
                hold(pool)
                for s in range(TOPK):
                    pool.wait_ge(dotted, n * TOPK + s + 1)
                    hold(pool)
                    gather(down[:, s % RING, :], io["down"], idx[b][:, s:s + 1], down_in[s % RING])
                for s in range(TOPK):
                    pool.wait_ge(upped, n * TOPK + s + 1 + 2 * TOPK - RING)
                    hold(pool)
                    gather(up[:, s % RING, :], io["up"], idx[b][:, s:s + 1], up_in[s % RING])
            steps(pool, step)

        @block.scalar
        def _(act):
            rt.start_act(act)
            act.wait_ge(set_up, 1)

            def step(n, b, t, e_next, t_next, start):
                if e_next is not None:
                    rt.move_query(act, n + 1)
                act.wait_ge(dotted, (n + 1) * TOPK + RING)
                nc.scalar.activation(acts[b][:], dots[b][:], ACT.Gelu).then_inc(activated, 1)
                if e_next is not None:
                    rt.gates(act, n + 1, 1 - b)
                if start and not first(n):
                    root(t + tile0 - 1)

            def root(t):
                act.wait_ge(stat_ready, t + 1)
                nc.scalar.activation(lr[:, 0:1], mv[:, 1:2], ACT.Sqrt, bias=eps[:, 0:1], scale=1.0
                                     ).then_inc(rooted, 1)

            rt.move_query(act, 0)
            rt.gates(act, 0, 0)
            for t in range(prompt_tiles):
                root(t)
            steps(act, step)
            root(TILES - 1)

        @block.vector
        def _(dve):
            chain = Chain(dve, keep["vector_chain"])
            chain(nc.vector.memset(eps[:], LN_EPS))
            chain.close()
            dve.sem_inc(set_up, 1)
            dve.sem_inc(dotted, RING)
            dve.sem_inc(rt.idx_ready, 1)
            dve.wait_ge(const_in, 32)
            dve.wait_ge(rt.const_in, 32)

            def retrieve(m, b):
                rt.pick(dve, chain, m, b, idx[b][:], lambda: dve.wait_ge(upped, (m + 1) * TOPK))

            def step(n, b, t, e_next, t_next, start):
                dve.wait_ge(h2_in, (t + 1) * 16)
                for s in range(TOPK):
                    row = down[:, s % RING, :]
                    dve.wait_ge(down_in[s % RING], (n * 2 + s // RING + 1) * 16)
                    nc.vector.tensor_tensor_reduce(row, row, h2[:], 1.0, 0.0, ALU.mult, ALU.add,
                                                   dots[b][:, s:s + 1]).then_inc(dotted, 1)
                if start and not first(n):
                    summed_in_psum(t - 1)
                    residual(t + tile0 - 1, acc[:])
                dve.wait_ge(rt.gated, n + 1)
                chain.then(nc.vector.reciprocal(rt.gate_r[:], rt.gate_s[b][:, 0:1]))
                dve.wait_ge(activated, n + 1)
                dve.wait_ge(upped, (n + 1) * TOPK)
                chain.then(nc.vector.scalar_tensor_tensor(out=wgt[:], in0=rt.gate_e[b][:], scalar=rt.gate_r[:, 0:1],
                                                          in1=acts[b][:], op0=ALU.mult, op1=ALU.mult))
                chain.then(nc.vector.tensor_tensor(
                    diag[b][:], ident[:].unsqueeze(1).to_broadcast([P, TOPK, P]),
                    wgt[:].unsqueeze(2).to_broadcast([P, TOPK, P]), ALU.mult))
                dve.sem_inc(diag_ready, 1)
                if e_next is not None:
                    retrieve(n + 1, 1 - b)
                if start and not first(n):
                    layer_norm(t + tile0 - 1)
                chain.close()

            def summed_in_psum(t):
                dve.wait_ge(upped, (t * PH + PH) * TOPK + 2 * TOPK)

            def residual(t, experts_sum):
                dve.wait_ge(res_in, (t + 1) * 32)
                chain.then(nc.vector.tensor_tensor(z[:], experts_sum, gate2[:], ALU.mult))
                chain.then(nc.vector.tensor_tensor(z[:], z[:], x2a[:], ALU.add))
                for h in range(2):
                    chain(nc.vector.bn_stats(stats[:, 6 * h:6 * h + 6], z[:, h * 512:(h + 1) * 512]))
                chain.wait()
                chain.then(nc.vector.bn_aggr(mv[:], stats[:]))
                dve.sem_inc(stat_ready, 1)

            def layer_norm(t):
                chain(nc.vector.tensor_scalar(lr[:, 1:2], mv[:, 1:2], LN_EPS, None, ALU.add))
                chain.wait()
                dve.wait_ge(rooted, t + 1)
                r, tmp = lr[:, 2:3], lr[:, 3:4]
                chain.then(nc.vector.reciprocal(r, lr[:, 0:1]))
                chain.then(nc.vector.tensor_tensor(tmp, r, r, ALU.mult))
                chain.then(nc.vector.tensor_tensor(tmp, tmp, lr[:, 1:2], ALU.mult))
                chain.then(nc.vector.tensor_scalar(tmp, tmp, -0.5, 1.5, ALU.mult, ALU.add))
                chain.then(nc.vector.tensor_tensor(r, r, tmp, ALU.mult))
                chain.then(nc.vector.tensor_scalar(z[:], z[:], mv[:, 0:1], r, ALU.subtract, ALU.mult))
                chain.then(nc.vector.tensor_tensor(z[:], z[:], ln[:, 0, :], ALU.mult))
                dve.wait_ge(y_stored, (t + 1) * 16)
                chain.then(nc.vector.tensor_tensor(y[:], z[:], ln[:, 1, :], ALU.add))
                dve.sem_inc(y_ready, 1)

            dve.sem_inc(y_stored, 16)
            retrieve(0, 0)
            for t in range(prompt_tiles):
                residual(t, keep["sums"][t][:])
                layer_norm(t)
            chain.close()
            steps(dve, step)
            summed_in_psum(tiles - 1)
            residual(TILES - 1, acc[:])
            layer_norm(TILES - 1)
            chain.close()

        @block.tensor
        def _(pe):
            pe.sem_inc(upped, 2 * TOPK)
            pe.wait_ge(rt.const_in, 32)
            pe.wait_ge(keep["w_query_loaded"], 32)

            def step(n, b, t, e_next, t_next, start):
                if e_next is not None:
                    rt.query(pe, n + 1, e_next, t_next + 1)
                pe.wait_ge(diag_ready, n + 1)
                for s in range(TOPK):
                    pe.wait_ge(up_in[s % RING], (n * 2 + s // RING + 1) * 16)
                    for c in range(2):
                        mm = nc.tensor.matmul(acc[:, c * 512:(c + 1) * 512], diag[b][:, s, :],
                                              up[:, s % RING, c * 512:(c + 1) * 512], start=start and s == 0,
                                              stop=e_next is None and s == TOPK - 1,
                                              skip_group_check=True)
                    mm.then_inc(upped, 1)

            rt.query(pe, 0, 0, 1)
            steps(pe, step)



def program(nc, io):
    with ExitStack() as outer:
        def sb(name, shape, stack=outer):
            return stack.enter_context(nc.sbuf_tensor(name, shape, F32))

        keep = {n: outer.enter_context(nc.semaphore(n)) for n in
                ("ident_loaded", "w_in_loaded", "w_out_loaded", "w_out_weighed", "w_query_loaded",
                 "vector_chain", "gpsimd_chain")}
        keep["ident"] = sb("ident_sb", [P, P])
        keep["mod_cols"] = sb("mod_cols", [P, 4 * DC])
        keep["sums"] = [sb(f"sums{t}", [P, D]) for t in range(2)]
        keep["w_in_a"] = sb("w_in_a", [P, DC, 2048])
        with ExitStack() as early:
            with ExitStack() as first:
                keep["w_in_b"] = sb("w_in_b", [P, DC, INW - 2048], first)
                modulation(nc, io, keep)
                projection(nc, io, keep)
            keep["w_out"] = sb("w_out_sb", [P, DC, D], early)
            keep["idx_all"] = early.enter_context(nc.sbuf_tensor("idx_all", [P, 2 * PH * TOPK], U32))
            keep["gate_all"] = sb("gate_all", [P, 2 * PH * TOPK], early)
            attention(nc, io, keep, 0)
            prompt_retrieval(nc, io, keep)
            attention(nc, io, keep, 1)
        experts(nc, io, keep)



def shape_constants():
    i = np.arange(1024)[:, None]
    j = np.arange(1024)[None, :]
    off = np.abs(i - j)
    count = (off <= 64).astype(np.float64) + ((off <= 256) & (off % 4 == 0)) + (off % 16 == 0)
    mask_a = np.where(count > 0, np.log(np.maximum(count, 1)), -BIG).astype(np.float32).reshape(8, P, 1024)
    mask_b = np.full((TILES, P, 3 * P), -BIG, np.float32)
    trig = np.zeros((TILES, P, 2 * HALF), np.float32)
    inv = (np.float32(500000.0) ** (-np.arange(HALF, dtype=np.float32) * np.float32(2.0) / np.float32(16))
           ).astype(np.float32)
    for tile0, tiles in SEQS:
        for t in range(tiles):
            q = t * P + np.arange(P)[:, None]
            k = (t - 1) * P + np.arange(3 * P)[None, :]
            mask_b[tile0 + t][(np.abs(q - k) <= 128) & (k >= 0) & (k < tiles * P)] = 0.0
            ang = (q.astype(np.float32) * inv[None, :]).astype(np.float64)
            trig[tile0 + t] = np.concatenate([np.cos(ang), np.sin(ang)], 1).astype(np.float32)
    return {"mask_a": mask_a, "mask_b": mask_b, "trig": trig, "ident": np.eye(P, dtype=np.float32),
            "iota": np.tile(np.arange(TOPK, dtype=np.float32), (P, 1))}


def lay_out(x_prompt, x_sample, c_prompt, c_sample, w_mod, b_mod, w_in, attn_sink, gn_a, gn_b, w_out,
            ln1_g, ln1_b, w_query, sub_keys, expert_down, expert_up, ln2_g, ln2_b):
    x = np.concatenate([np.asarray(x_prompt)[0], np.asarray(x_sample)[0]], 0).reshape(TILES, P, D)
    c = np.stack([np.asarray(c_prompt)[0], np.asarray(c_sample)[0]])
    w = np.array(w_in[0])
    q_b = w[:, QB:KVB].reshape(D, BH, HD)[:, [b_head(j) for j in range(BH)]].reshape(D, BH * HD)
    w = np.concatenate([w[:, :QB], q_b, w[:, KVB:]], 1)
    data = {
        "x": x,
        "x_t": x.reshape(TILES, P, DC, P).transpose(0, 3, 2, 1),
        "c_t": c.reshape(2, DC, P).transpose(2, 1, 0).reshape(P, 2 * DC),
        "w_mod": w_mod[0], "b_mod": b_mod[0], "w_in": w, "attn_sink": attn_sink[0],
        "gn": np.concatenate([gn_a[0], gn_b[0]]).reshape(DC, P).T, "w_out": w_out[0],
        "ln1": np.stack([ln1_g[0], ln1_b[0]]), "w_query": w_query[0],
        "keys_t": np.asarray(sub_keys)[0].transpose(3, 0, 1, 2).reshape(P, PH * 2 * N_KEYS),
        "down": expert_down[0], "up": expert_up[0], "ln2": np.stack([ln2_g[0], ln2_b[0]]),
    }
    data.update(shape_constants())
    return {"in_" + n: np.ascontiguousarray(a) for n, a in data.items()}


SCRATCH = {
    "mod_rows": (2, 4 * D), "qt": (TILES, P, 8, P), "kt0": (P, 4, 256), "kt1": (P, 4, 1024),
    "va0": (2, P, 512), "va1": (8, P, 512), "kb": (SLOTS, P, P), "vb": (SLOTS, P, P),
    "gate2": (TILES, D), "h2": (TILES, P, D), "x2a": (TILES, P, D), "h2t": (TILES, P, DC, P),
}


def declare_and_program(nc, arrays):
    io = {n[3:]: nc.dram_tensor(n, a.shape, F32, kind="ExternalInput").ap() for n, a in arrays.items()}
    for n, shape in SCRATCH.items():
        io[n] = nc.dram_tensor("scratch_" + n, shape, F32, kind="Internal").ap()
    io["kt"], io["va"] = (io["kt0"], io["kt1"]), (io["va0"], io["va1"])
    io["y"] = nc.dram_tensor("y", (TILES, P, D), F32, kind="ExternalOutput").ap()
    program(nc, io)


def kernel(**inputs):
    import concourse.bacc as bacc
    from concourse.bass_utils import run_bass_kernel_spmd

    arrays = lay_out(**inputs)
    nc = bacc.Bacc("TRN2", target_bir_lowering=False, num_devices=1)
    declare_and_program(nc, arrays)
    r = run_bass_kernel_spmd(nc, [arrays], core_ids=[0])
    y = r.results[0]["y"].reshape(TILES * P, D)
    return y[:2 * P].reshape(1, 2 * P, D), y[2 * P:].reshape(1, 8 * P, D)
```

```python
from contextlib import ExitStack

import numpy as np

import concourse.bass as bass
from concourse import mybir

P = 128
D = 1024
DC = D // P
SEQS = ((0, 2), (2, 8))
TILES = 10
HD = 64
HALF = 8
AH, BH, BKV = 8, 8, 2
HEADS = AH + BH
QA, KA, VA, QB, KVB = 0, 512, 1024, 1536, 2048
INW = 2304
N_KEYS = 128
PH = 8
TOPK = 16
SLOTS = 14
BIG = 1.0e30
ALPHA = 2.0 ** 0.25
LN_EPS = 1e-5
RMS_EPS = 1e-6

ALU = mybir.AluOpType
ACT = mybir.ActivationFunctionType
F32 = mybir.dt.float32
U32 = mybir.dt.uint32
AX_X = mybir.AxisListType.X


def first_slot(tile0):
    return 1 if tile0 == 0 else 5


def b_head(j):
    return j // 2 + (BH // BKV) * (j % 2)


def hold(eng):
    eng.nop(nofuse=True)


class Chain:

    def __init__(self, eng, sem):
        self.eng, self.sem, self.n = eng, sem, 0

    def __call__(self, ins):
        ins.then_inc(self.sem, 1)
        self.n += 1
        return self.n

    def wait(self, n=None):
        self.eng.wait_ge(self.sem, self.n if n is None else n)

    def then(self, ins):
        self(ins)
        self.wait()

    def close(self):
        if self.n:
            self.wait()
            self.eng.sem_clear(self.sem)
        self.n = 0



def modulation(nc, io, keep):
    CH, BUFS = 512, 4
    NCH = 6 * D // CH
    with ExitStack() as ctx:
        def sb(name, shape, dt=F32):
            return ctx.enter_context(nc.sbuf_tensor(name, shape, dt))

        def sem(name):
            return ctx.enter_context(nc.semaphore(name))

        wm = [sb(f"wm{b}", [P, DC, CH]) for b in range(BUFS)]
        c_t = sb("c_t", [P, 2 * DC])
        neg_e = sb("neg_e", [P, 2 * DC])
        sig = sb("sig", [P, 2 * DC])
        silu = sb("silu", [P, 2 * DC])
        bias = sb("bias", [2, 6 * D])
        mod = sb("mod", [2, 6 * D])
        zeros = sb("zeros", [P, P])
        rows = [ctx.enter_context(nc.psum_tensor(f"rows{b}", [P, CH], F32)) for b in range(2)]
        cols = ctx.enter_context(nc.psum_tensor("cols", [P, 512], F32))

        small_in = sem("m_small_in")
        w_in_sem = [sem(f"m_w{b}") for b in range(BUFS)]
        exped = sem("m_exped")
        silu_ready = sem("m_silu_ready")
        row_done = sem("m_row_done")
        row_copied = sem("m_row_copied")
        mod_ready = sem("m_mod_ready")
        cols_done = sem("m_cols_done")
        zeroed = sem("m_zeroed")
        stored = sem("m_stored")
        block = ctx.enter_context(nc.Block())
        w_mod = io["w_mod"].rearrange("(c p) n -> p c n", p=P)

        @block.sync
        def _(sp):
            sp.dma_start(keep["ident"][:], io["ident"]).then_inc(keep["ident_loaded"], 16)
            sp.dma_start(c_t[:], io["c_t"]).then_inc(small_in, 16)
            sp.dma_start(bias[:], io["b_mod"].partition_broadcast(2)).then_inc(small_in, 16)
            for b in range(BUFS):
                sp.dma_start(wm[b][:], w_mod[:, :, b * CH:(b + 1) * CH]).then_inc(w_in_sem[b], 16)
            with sp.Fori(1, NCH // BUFS) as r:
                for b in range(BUFS):
                    sp.wait_ge(row_done, (r - 1) * BUFS + b + 1)
                    hold(sp)
                    sp.dma_start(wm[b][:], w_mod[:, :, bass.ds((r * BUFS + b) * CH, CH)]).then_inc(
                        w_in_sem[b], 16)
            sp.dma_start(keep["w_in_a"][:], io["w_in"].rearrange("(c p) n -> p c n", p=P)[:, :, 0:2048]
                         ).then_inc(keep["w_in_loaded"], 16)
            sp.dma_start(keep["w_in_b"][:], io["w_in"].rearrange("(c p) n -> p c n", p=P)[:, :, 2048:INW]
                         ).then_inc(keep["w_in_loaded"], 16)
            sp.wait_ge(mod_ready, 1)
            sp.dma_start(io["mod_rows"], mod[:, 2 * D:6 * D]).then_inc(stored, 16)
            sp.wait_ge(zeroed, 1)
            for slot in (0, 3, 4, 13):
                sp.dma_start(io["kb"][slot], zeros[:]).then_inc(stored, 16)
                sp.dma_start(io["vb"][slot], zeros[:]).then_inc(stored, 16)
            sp.wait_ge(stored, 16 * 9)
            for seq, (tile0, tiles) in enumerate(SEQS):
                sp.dma_start(io["gate2"][tile0:tile0 + tiles],
                             io["mod_rows"][seq:seq + 1, 3 * D:4 * D].rearrange("a n -> (a n)").partition_broadcast(tiles)
                             ).then_inc(stored, 16)
            sp.wait_ge(stored, 16 * 11)

        @block.scalar
        def _(act):
            act.wait_ge(small_in, 32)
            nc.scalar.activation(neg_e[:], c_t[:], ACT.Exp, scale=-1.0).then_inc(exped, 1)

        @block.vector
        def _(dve):
            chain = Chain(dve, keep["vector_chain"])
            dve.sem_inc(row_copied, 2)
            nc.vector.memset(zeros[:], 0.0).then_inc(zeroed, 1)
            dve.wait_ge(exped, 1)
            chain.then(nc.vector.tensor_scalar(neg_e[:], neg_e[:], 1.0, None, ALU.add))
            chain.then(nc.vector.reciprocal(sig[:], neg_e[:]))
            nc.vector.tensor_tensor(silu[:], c_t[:], sig[:], ALU.mult).then_inc(silu_ready, 1)
            with dve.Fori(0, NCH // 2) as r:
                for b in range(2):
                    j = r * 2 + b
                    dve.wait_ge(row_done, j + 1)
                    nc.vector.tensor_tensor(mod[:, bass.ds(j * CH, CH)], rows[b][0:2, :],
                                            bias[:, bass.ds(j * CH, CH)], ALU.add).then_inc(row_copied, 1)
            dve.wait_ge(row_copied, 2 + NCH)
            chain(nc.vector.tensor_scalar(mod[:, D:3 * D], mod[:, D:3 * D], 1.0, None, ALU.add))
            chain.then(nc.vector.tensor_scalar(mod[:, 4 * D:6 * D], mod[:, 4 * D:6 * D], 1.0, None, ALU.add))
            dve.sem_inc(mod_ready, 1)
            dve.wait_ge(cols_done, 1)
            chain(nc.vector.tensor_copy(keep["mod_cols"][:], cols[:, 0:4 * DC]))
            chain.close()

        @block.tensor
        def _(pe):
            pe.wait_ge(silu_ready, 1)
            with pe.Fori(0, NCH // BUFS) as r:
                for b in range(BUFS):
                    pe.wait_ge(w_in_sem[b], (r + 1) * 16)
                    pe.wait_ge(row_copied, r * BUFS + b + 1)
                    for c in range(DC):
                        mm = nc.tensor.matmul(rows[b % 2][0:2, :], silu[:, 2 * c:2 * c + 2], wm[b][:, c, :],
                                              start=(c == 0), stop=(c == DC - 1))
                    mm.then_inc(row_done, 1)
            pe.wait_ge(mod_ready, 1)
            pe.wait_ge(keep["ident_loaded"], 16)
            for c in range(2 * DC):
                mm = nc.tensor.transpose(cols[:, 2 * c:2 * c + 2], mod[:, c * P:(c + 1) * P],
                                         keep["ident"][0:2, 0:2])
            mm.then_inc(cols_done, 1)



def projection(nc, io, keep):
    ORDER = (0, 1, 3, 4, 2)
    WIDTH = (512, 512, 512, 512, 256)
    with ExitStack() as ctx:
        def sb(name, shape, dt=F32):
            return ctx.enter_context(nc.sbuf_tensor(name, shape, dt))

        def sem(name):
            return ctx.enter_context(nc.semaphore(name))

        xt = [sb(f"xt{b}", [P, DC, P]) for b in range(2)]
        h1t = [sb(f"h1t{b}", [P, DC, P]) for b in range(2)]
        proj = [sb(f"proj{b}", [P, INW]) for b in range(2)]
        trig = [sb(f"trig{b}", [P, 2 * HALF]) for b in range(2)]
        rot_c = sb("rot_c", [P, 16, 2, HALF])
        rot_s = sb("rot_s", [P, 16, 2, HALF])
        qk_t = [sb(f"qk_t{b}", [P, 13, P]) for b in range(2)]
        acc = [ctx.enter_context(nc.psum_tensor(f"acc{c}", [P, 512], F32)) for c in range(5)]
        tr = [ctx.enter_context(nc.psum_tensor(f"tr{c}", [P, 4, P], F32)) for c in range(2)]

        x_loaded = [sem(f"p_x{b}") for b in range(2)]
        h1_ready = sem("p_h1_ready")
        proj_done = sem("p_proj_done")
        proj_copied = sem("p_proj_copied")
        rotated = sem("p_rotated")
        turned = sem("p_turned")
        q_copied = sem("p_q_copied")
        k_copied = sem("p_k_copied")
        stored = [sem(f"p_stored{b}") for b in range(2)]
        block = ctx.enter_context(nc.Block())
        STORES = 5

        def pairs(eng, emit):
            for seq, (tile0, tiles) in enumerate(SEQS):
                with eng.Fori(tile0 // 2, (tile0 + tiles) // 2) as i:
                    for b in range(2):
                        emit(seq, tile0, i, b)

        @block.sync
        def _(sp):
            def emit(seq, tile0, i, b):
                sp.wait_ge(h1_ready, i * 2 + b + 2)
                hold(sp)
                sp.dma_start(xt[b][:], io["x_t"][i * 2 + b]).then_inc(x_loaded[b], 16)
                sp.dma_start(trig[b][:], io["trig"][i * 2 + b]).then_inc(x_loaded[b], 16)
            pairs(sp, emit)

        @block.scalar
        def _(act):
            for b in range(2):
                act.sem_inc(stored[b], 16)
            act.sem_inc(proj_copied, 5)
            act.sem_inc(q_copied, 1)

            def emit(seq, tile0, i, b):
                t = i * 2 + b
                act.wait_ge(stored[b], (i * STORES + 1) * 16)
                for o, c in enumerate(ORDER):
                    act.wait_ge(proj_done, t * 5 + o + 1)
                    w = WIDTH[c]
                    nc.scalar.mul(proj[b][:, c * 512:c * 512 + w], acc[c][:, 0:w],
                                  -HD ** -0.5 if c in (0, 3) else 1.0).then_inc(proj_copied, 1)
                    if o >= 3:
                        g = o - 3
                        act.wait_ge(turned, t * 4 + 2 * g + 1)
                        nc.scalar.mul(qk_t[b][:, 4 * g:4 * g + 4, :], tr[0][:], 1.0).then_inc(q_copied, 1)
                act.wait_ge(proj_copied, t * 5 + 10)
                act.wait_ge(q_copied, t * 2 + 3)
                act.wait_ge(k_copied, t * 2 + 3)
                hold(act)
                slot = t + first_slot(tile0) - tile0
                act.dma_start(io["qt"][t], qk_t[b][:, 0:8, :]).then_inc(stored[b], 16)
                act.dma_start(io["kt"][seq][:, :, bass.ds((t - tile0) * P, P)], qk_t[b][:, 8:12, :]
                              ).then_inc(stored[b], 16)
                act.dma_start(io["kb"][slot], qk_t[b][:, 12, :]).then_inc(stored[b], 16)
                act.dma_start(io["vb"][slot], proj[b][:, KVB + P:INW]).then_inc(stored[b], 16)
                act.dma_start(io["va"][seq][t - tile0], proj[b][:, VA:QB]).then_inc(stored[b], 16)
            pairs(act, emit)
            for b in range(2):
                act.wait_ge(stored[b], 16 * (STORES * TILES // 2 + 1))

        @block.vector
        def _(dve):
            chain = Chain(dve, keep["vector_chain"])
            dve.sem_inc(h1_ready, 2)
            dve.sem_inc(k_copied, 1)

            def h1(seq, i, b):
                dve.wait_ge(x_loaded[b], (i + 1) * 32)
                for c in range(DC):
                    mc = keep["mod_cols"]
                    n = chain(nc.vector.tensor_scalar(
                        h1t[b][:, c, :], xt[b][:, c, :], mc[:, 2 * (DC + c) + seq:2 * (DC + c) + seq + 1],
                        mc[:, 2 * c + seq:2 * c + seq + 1], ALU.mult, ALU.add))
                chain.wait()
                dve.sem_inc(h1_ready, 1)

            def emit(seq, i, b):
                t = i * 2 + b
                for g, (first, heads, pieces) in enumerate(((QA, 16, 2), (QB, 10, 4))):
                    dve.wait_ge(proj_copied, t * 5 + 5 + pieces)
                    v = proj[b][:, first:first + heads * HD].rearrange("p (h d) -> p h d", d=HD)
                    v = v[:, :, 0:2 * HALF].rearrange("p h (e d) -> p h e d", e=2)
                    cos = trig[b][:, 0:HALF].unsqueeze(1).unsqueeze(1).to_broadcast([P, heads, 2, HALF])
                    sin = trig[b][:, HALF:2 * HALF].unsqueeze(1).to_broadcast([P, heads, HALF])
                    rc, rs = rot_c[:, 0:heads], rot_s[:, 0:heads]
                    chain(nc.vector.tensor_tensor(rc, v, cos, ALU.mult))
                    chain(nc.vector.tensor_tensor(rs[:, :, 0, :], v[:, :, 1, :], sin, ALU.mult))
                    chain(nc.vector.tensor_tensor(rs[:, :, 1, :], v[:, :, 0, :], sin, ALU.mult))
                    chain.wait()
                    chain(nc.vector.tensor_tensor(v[:, :, 0, :], rc[:, :, 0, :], rs[:, :, 0, :], ALU.subtract))
                    chain(nc.vector.tensor_tensor(v[:, :, 1, :], rc[:, :, 1, :], rs[:, :, 1, :], ALU.add))
                    chain.wait()
                    dve.sem_inc(rotated, 1)
                if b == 0:
                    h1(seq, i, 1)
                elif not (isinstance(i, int) and i == TILES // 2 - 1):
                    h1(1, i + 1, 0)
                for g in range(2):
                    dve.wait_ge(turned, t * 4 + 2 * g + 2)
                    w = 4 if g == 0 else 1
                    nc.vector.tensor_copy(qk_t[b][:, 8 + 4 * g:8 + 4 * g + w, :], tr[1][:, 0:w, :]
                                          ).then_inc(k_copied, 1)
                chain.close()

            h1(0, 0, 0)
            for b in range(2):
                emit(0, 0, b)
            with dve.Fori(1, TILES // 2 - 1) as i:
                for b in range(2):
                    emit(1, i, b)
            for b in range(2):
                emit(1, TILES // 2 - 1, b)

        @block.tensor
        def _(pe):
            pe.wait_ge(keep["w_in_loaded"], 32)

            def emit(seq, tile0, i, b):
                t = i * 2 + b
                pe.wait_ge(h1_ready, t + 3)
                turns = ((QA, 4, 0), (KA, 4, 1), (QB, 4, 0), (KVB, 1, 1))
                for o, c in enumerate(ORDER):
                    pe.wait_ge(proj_copied, t * 5 + o + 1)
                    w = WIDTH[c]
                    for k in range(DC):
                        rhs = (keep["w_in_a"][:, k, c * 512:c * 512 + w] if c < 4
                               else keep["w_in_b"][:, k, :])
                        mm = nc.tensor.matmul(acc[c][:, 0:w], h1t[b][:, k, :], rhs,
                                              start=(k == 0), stop=(k == DC - 1))
                    mm.then_inc(proj_done, 1)
                    if o >= 3:
                        g = o - 3
                        pe.wait_ge(rotated, t * 2 + 1 + g)
                        for col, chunks, bank in turns[2 * g:2 * g + 2]:
                            pe.wait_ge((q_copied, k_copied)[bank], t * 2 + 1 + g)
                            for k in range(chunks):
                                mm = nc.tensor.transpose(
                                    tr[bank][:, k, :], proj[b][:, col + k * P:col + (k + 1) * P], keep["ident"][:])
                            mm.then_inc(turned, 1)
            pairs(pe, emit)



def attention(nc, io, keep, seq):
    tile0, tiles = SEQS[seq]
    S = tiles * P
    KT = S // P
    side = seq == 1
    DOWN, UP = 8, 4
    PER = 2 * TOPK
    CONSTS = 96 if side else 64
    M_AT, MIX_AT, READ_AT, LN_AT, H2_AT = 2, (3, 4, 5, 6), 7, 9, 12
    with ExitStack() as ctx:
        def sb(name, shape, dt=F32):
            return ctx.enter_context(nc.sbuf_tensor(f"a{seq}_{name}", shape, dt))

        def sem(name):
            return ctx.enter_context(nc.semaphore(f"a{seq}_{name}"))

        def ps(name, shape):
            return ctx.enter_context(nc.psum_tensor(f"a{seq}_{name}", shape, F32))

        k_t = sb("k_t", [P, 4, S])
        v_a = sb("v_a", [P, KT, 512])
        q_t = sb("q_t", [P, 8, P])
        mask_a = sb("mask_a", [P, S])
        mask_b = sb("mask_b", [P, 3 * P])
        k_b = sb("k_b", [P, 3, P])
        v_b = sb("v_b", [P, 3, P])
        rows = sb("rows", [P, 3, D])
        ln = sb("ln", [P, 2, D])
        sink, neg_sink = sb("sink", [P, BH]), sb("neg_sink", [P, BH])
        prob = [sb(f"prob{b}", [P, S if S > 384 else 384]) for b in range(2)]
        prob_t = [sb(f"prob_t{b}", [P, max(KT, 3), P]) for b in range(2)]
        heads_out = sb("heads_out", [P, D])
        merged = sb("merged", [P, D])
        merged_t = sb("merged_t", [P, DC, P])
        if side:
            free = keep["w_in_a"][:].rearrange("p c n -> p (c n)").rearrange("p (s d) -> p s d", d=D)
            down, up = free[:, 0:DOWN, :], free[:, DOWN:DOWN + UP, :]
            h2_p = [free[:, DOWN + UP + t, :] for t in range(2)]
            x_in, heads_raw = free[:, DOWN + UP + 2, :], free[:, DOWN + UP + 3, :]
            idx_down = [sb(f"idx_down{t}", [P, TOPK], U32) for t in range(2)]
            idx_up = [sb(f"idx_up{t}", [P, TOPK], U32) for t in range(2)]
            dots = [sb(f"dots{t}", [P, TOPK]) for t in range(2)]
            acts = [sb(f"acts{t}", [P, TOPK]) for t in range(2)]
            wgt = [sb(f"wgt{t}", [P, TOPK]) for t in range(2)]
            down_in = [sem(f"down_in{k}") for k in range(DOWN)]
            up_in = [sem(f"up_in{k}") for k in range(UP)]
            dotted, upped, activated = sem("dotted"), sem("upped"), sem("activated")
        else:
            x_in, heads_raw = sb("x_in", [P, D])[:], sb("heads_raw", [P, D])[:]
            gn = sb("gn", [P, DC])
        x2 = sb("x2", [P, D])
        z = merged[:]
        h2 = merged
        neg_m = sb("neg_m", [P, HEADS])
        den = sb("den", [P, HEADS])
        sink_e = sb("sink_e", [P, BH])
        r_den = sb("r_den", [P, HEADS])
        sq = sb("sq", [P, 8])
        rr = sb("rr", [P, 4])
        stats = sb("stats", [P, 12])
        mv = sb("mv", [P, 2])
        lr = sb("lr", [P, 4])
        eps = sb("eps", [P, 2])

        score = [ps(f"score{b}", [P, 1024]) for b in range(2)]
        turn = ps("turn", [P, 8, P])
        out_ps = [ps(f"out{b}", [P, 512]) for b in range(2)]

        const_in = sem("const_in")
        kv_in = sem("kv_in")
        qa_in, qb_in, win_in, x_sem = sem("qa_in"), sem("qb_in"), sem("win_in"), sem("x_in_s")
        maska_in, maskb_in = sem("maska_in"), sem("maskb_in")
        scored, masked, exped = sem("scored"), sem("masked"), sem("exped")
        turned, copied = sem("turned"), sem("copied")
        summed, head_done = sem("summed"), sem("head_done")
        squared, merged_ready, merged_turned = sem("squared"), sem("merged_ready"), sem("merged_turned")
        merged_copied, den_ready = sem("merged_copied"), sem("den_ready")
        mixed, mix_read, stat_ready, rooted = sem("mixed"), sem("mix_read"), sem("stat_ready"), sem("rooted")
        x2_ready, h2_ready, h2_turned, h2_copied = (sem("x2_ready"), sem("h2_ready"), sem("h2_turned"),
                                                    sem("h2_copied"))
        stored = sem("stored")
        eps_ready = sem("eps_ready")
        block = ctx.enter_context(nc.Block())

        def keys_of(h):
            return KT if h >= BH else 3

        def tiled(eng, body):
            body(0, True, False)
            if tiles > 2:
                with eng.Fori(1, tiles - 1) as i:
                    body(i, False, False)
            body(tiles - 1, False, True)

        def before(i, h, n):
            return (i, h - n) if h >= n else (i - 1, h - n + HEADS)

        @block.sync
        def _(sp):
            sp.dma_start(sink[:], io["attn_sink"].partition_broadcast(P)).then_inc(const_in, 16)

            def wait(semaphore, value):
                sp.wait_ge(semaphore, value)
                hold(sp)

            def load(i, first, last):
                t = i + tile0
                slot = i + first_slot(tile0)
                if not first:
                    wait(scored, i * HEADS - AH)
                sp.dma_start(q_t[:, 4:8, :], io["qt"][t][:, 4:8, :]).then_inc(qb_in, 16)
                sp.dma_start(k_b[:], io["kb"][bass.ds(slot - 1, 3)].rearrange("s p k -> p s k")
                             ).then_inc(win_in, 16)
                if not first:
                    wait(masked, i * HEADS - AH + 2)
                sp.dma_start(mask_b[:], io["mask_b"][t]).then_inc(maskb_in, 16)
                if not first:
                    wait(summed, i * HEADS - AH + 2)
                sp.dma_start(v_b[:], io["vb"][bass.ds(slot - 1, 3)].rearrange("s p k -> p s k")
                             ).then_inc(win_in, 16)
                if first:
                    sp.dma_start(k_t[:], io["kt"][seq]).then_inc(kv_in, 16)
                else:
                    wait(scored, i * HEADS)
                sp.dma_start(q_t[:, 0:4, :], io["qt"][t][:, 0:4, :]).then_inc(qa_in, 16)
                if not first:
                    wait(masked, i * HEADS + 2)
                sp.dma_start(mask_a[:], io["mask_a"][i][:, 0:S]).then_inc(maska_in, 16)
                if not first:
                    wait(x2_ready, i)
                    sp.dma_start(x_in, io["x"][t - 1]).then_inc(x_sem, 16)
                    return
                rows_dram = io["mod_rows"][seq:seq + 1, 0:3 * D].rearrange("a n -> (a n)")
                sp.dma_start(v_a[:], io["va"][seq].rearrange("n p c -> p n c")).then_inc(kv_in, 16)
                sp.dma_start(rows[:].rearrange("p a d -> p (a d)"), rows_dram.partition_broadcast(P)
                             ).then_inc(const_in, 16)
                for j in range(2):
                    sp.dma_start(ln[:, j, :], io["ln1"][j].partition_broadcast(P)).then_inc(const_in, 16)
                if side:
                    for p in range(2):
                        sp.dma_start(h2_p[p], io["h2"][p]).then_inc(const_in, 16)
                else:
                    sp.dma_start(gn[:], io["gn"]).then_inc(keep["w_out_loaded"], 16)
                    sp.dma_start(keep["w_out"][:], io["w_out"].rearrange("(c p) n -> p c n", p=P)
                                 ).then_inc(keep["w_out_loaded"], 16)
                    sp.dma_start(keep["w_in_a"][:], io["w_query"].rearrange("(c p) n -> p c n", p=P)
                                 ).then_inc(keep["w_query_loaded"], 16)

            tiled(sp, load)
            sp.wait_ge(x2_ready, tiles)
            sp.dma_start(x_in, io["x"][tile0 + tiles - 1]).then_inc(x_sem, 16)
            if side:
                w_query = io["w_query"].rearrange("(c p) n -> p c n", p=P)
                sp.wait_ge(dotted, tiles * PER + DOWN)
                for lo, hi in ((0, 4), (6, 7)):
                    sp.dma_start(keep["w_in_a"][:, lo:hi, :], w_query[:, lo:hi, :]).then_inc(
                        keep["w_query_loaded"], 16)
                sp.wait_ge(upped, tiles * PER + UP)
                sp.dma_start(keep["w_in_a"][:, 4:6, :], w_query[:, 4:6, :]).then_inc(keep["w_query_loaded"], 16)

        @block.gpsimd
        def _(pool):
            chain = Chain(pool, keep["gpsimd_chain"])

            def tail(j):
                pool.wait_ge(x2_ready, j + 2)
                pool.wait_ge(h2_turned, j + 1)
                pool.wait_ge(stored, (j + 1) * 48)
                chain.then(nc.gpsimd.tensor_tensor(h2[:], x2[:], rows[:, 2, :], ALU.mult))
                chain.then(nc.gpsimd.tensor_tensor(h2[:], h2[:], rows[:, 1, :], ALU.add))
                pool.sem_inc(h2_ready, 1)

            def take_idx(dst, i, p):
                chain.then(nc.gpsimd.tensor_copy(dst[p][:], keep["idx_all"][:, bass.ds((i * 2 + p) * TOPK, TOPK)]))

            def gather(ring, table, index, landed):
                hold(pool)
                pool.indirect_dma_start(ring, None, table, bass.IndirectOffsetOnAxis(ap=index, axis=0)
                                        ).then_inc(landed, 16)

            def gather_down(i, h):
                for k in range(2 * h, 2 * h + 2):
                    pool.wait_ge(dotted, i * PER + k + 1)
                    gather(down[:, k % DOWN, :], io["down"], idx_down[h // 8][:, k % TOPK:k % TOPK + 1],
                           down_in[k % DOWN])

            def gather_up(i, h):
                for k in range(2 * h, 2 * h + 2):
                    pool.wait_ge(upped, i * PER + k - TOPK + 1)
                    gather(up[:, k % UP, :], io["up"], idx_up[1 - h // 8][:, k % TOPK:k % TOPK + 1],
                           up_in[k % UP])

            def body(i, first):
                for h in range(HEADS):
                    if h == 4:
                        take_idx(idx_down, i, 1)
                        take_idx(idx_up, i, 0)
                    gather_down(i, h)
                    if not (first and h < 8):
                        gather_up(i, h)
                    if h == 12:
                        take_idx(idx_up, i, 1)
                        if i is not None:
                            take_next(i)
                    if not first and h == H2_AT - 1:
                        tail(i - 1)
                chain.close()

            def take_next(i):
                if not (isinstance(i, int) and i == tiles - 1):
                    take_idx(idx_down, i + 1, 0)

            pool.wait_ge(const_in, CONSTS)
            if side:
                take_idx(idx_down, 0, 0)
                chain.close()
                body(0, True)
                with pool.Fori(1, tiles - 1) as i:
                    body(i, False)
                body(tiles - 1, False)
                for h in range(8):
                    gather_up(tiles, h)
                tail(tiles - 1)
            else:
                with pool.Fori(0, tiles - 1) as j:
                    tail(j)
                    chain.close()
                tail(tiles - 1)
            chain.close()

        @block.scalar
        def _(act):
            act.wait_ge(const_in, CONSTS)
            act.wait_ge(eps_ready, 1)
            act.sem_inc(copied, 1)
            act.sem_inc(stored, 48)

            def copy_probs(i, h):
                g = i * HEADS + h
                n = keys_of(h)
                act.wait_ge(turned, g + 1)
                act.wait_ge(summed, g + 1)
                nc.scalar.copy(prob_t[h % 2][:, 0:n, :], turn[:, 0:n, :]).then_inc(copied, 1)

            def copy_turned(count, n, j, dst_sem):
                act.wait_ge(count, n)
                act.wait_ge(stored, (j + 1) * 48)
                nc.scalar.copy(merged_t[:], turn[:]).then_inc(dst_sem, 1)

            def finish_head(i, h):
                g = i * HEADS + h
                col = (AH + b_head(h) if h < BH else h - BH) * HD
                act.wait_ge(den_ready, g + 1)
                act.wait_ge(summed, g + 3)
                nc.scalar.activation(heads_out[:, col:col + HD], out_ps[h % 2][:, 0:HD], ACT.Copy,
                                     scale=r_den[:, h:h + 1]).then_inc(head_done, 1)

            def activate(i, p):
                act.wait_ge(dotted, i * PER + (p + 1) * TOPK + DOWN)
                nc.scalar.activation(acts[p][:], dots[p][:], ACT.Gelu).then_inc(activated, 1)

            def square(j):
                act.wait_ge(head_done, (j + 1) * HEADS)
                nc.scalar.copy(heads_raw, heads_out[:]).then_inc(squared, 1)
                act.wait_ge(stored, (j + 1) * 48)
                act.wait_ge(squared, j * 4 + 1)
                for b in range(2):
                    nc.scalar.activation(merged[:, b * 512:(b + 1) * 512],
                                         heads_raw[:, b * 512:(b + 1) * 512], ACT.Square,
                                         accum_out=sq[:, b:b + 1]).then_inc(squared, 1)
                act.wait_ge(squared, j * 4 + 3)
                nc.scalar.activation(sq[:, 2:4], sq[:, 0:2], ACT.Sqrt, bias=eps[:, 0:1], scale=1.0 / 512
                                     ).then_inc(squared, 1)

            def body(i, first, last):
                for h in range(HEADS):
                    g = i * HEADS + h
                    act.wait_ge(masked, g + 3)
                    w = keys_of(h) * P
                    if h < BH:
                        s_at = b_head(h)
                        nc.scalar.activation(sink_e[:, h:h + 1], sink[:, s_at:s_at + 1], ACT.Exp,
                                             bias=neg_m[:, h:h + 1])
                    nc.scalar.activation(prob[h % 2][:, 0:w], prob[h % 2][:, 0:w], ACT.Exp,
                                         bias=neg_m[:, h:h + 1], scale=-1.0, accum_out=den[:, h:h + 1]
                                         ).then_inc(exped, 1)
                    if side and h == 0 and not first:
                        activate(i - 1, 1)
                    if side and h == 8:
                        activate(i, 0)
                    if not (first and h < 1):
                        copy_probs(*before(i, h, 1))
                    if not first and h == M_AT + 1:
                        copy_turned(merged_turned, i, i - 1, merged_copied)
                    if not (first and h < 2):
                        finish_head(*before(i, h, 2))
                    if not first and h == 1:
                        square(i - 1)
                    if not first and h == READ_AT + 1:
                        root(i - 1)
                    if not first and h == H2_AT + 1:
                        after_h2(i - 1)

            def root(j):
                act.wait_ge(stat_ready, j + 1)
                nc.scalar.activation(lr[:, 0:1], mv[:, 1:2], ACT.Sqrt, bias=eps[:, 1:2], scale=1.0
                                     ).then_inc(rooted, 1)

            def after_h2(j):
                copy_turned(h2_turned, j + 2, j, h2_copied)
                act.wait_ge(h2_ready, j + 1)
                nc.scalar.mul(x2[:], x2[:], ALPHA).then_inc(h2_copied, 1)
                act.wait_ge(h2_copied, (j + 1) * 2)
                hold(act)
                act.dma_start(io["h2"][j + tile0], h2[:]).then_inc(stored, 16)
                act.dma_start(io["x2a"][j + tile0], x2[:]).then_inc(stored, 16)
                act.dma_start(io["h2t"][j + tile0], merged_t[:]).then_inc(stored, 16)

            tiled(act, body)
            last = tiles - 1
            copy_probs(last, HEADS - 1)
            finish_head(last, HEADS - 2)
            finish_head(last, HEADS - 1)
            square(last)
            if side:
                activate(last, 1)
            copy_turned(merged_turned, last + 1, last, merged_copied)
            root(last)
            after_h2(last)
            act.wait_ge(stored, 48 * (tiles + 1))

        @block.vector
        def _(dve):
            chain = Chain(dve, keep["vector_chain"])
            chain(nc.vector.memset(eps[:, 0:1], RMS_EPS))
            chain(nc.vector.memset(eps[:, 1:2], LN_EPS))
            chain.wait()
            dve.sem_inc(eps_ready, 1)
            dve.sem_inc(masked, 2)
            if side:
                dve.sem_inc(dotted, DOWN)
                dve.sem_inc(upped, UP)
                for p in range(2):
                    chain(nc.vector.memset(keep["sums"][p][:], 0.0))
            dve.sem_inc(x2_ready, 1)
            dve.wait_ge(const_in, CONSTS)
            chain.then(nc.vector.tensor_scalar(neg_sink[:], sink[:], -1.0, None, ALU.mult))

            def newton(dst, root, var, tmp):
                chain.then(nc.vector.reciprocal(dst, root))
                chain.then(nc.vector.tensor_tensor(tmp, dst, dst, ALU.mult))
                chain.then(nc.vector.tensor_tensor(tmp, tmp, var, ALU.mult))
                chain.then(nc.vector.tensor_scalar(tmp, tmp, -0.5, 1.5, ALU.mult, ALU.add))
                chain.then(nc.vector.tensor_tensor(dst, dst, tmp, ALU.mult))

            def mask(i, h):
                g = i * HEADS + h
                w = keys_of(h) * P
                dve.wait_ge(scored, g + 1)
                if h == 0:
                    dve.wait_ge(maskb_in, (i + 1) * 16)
                if h == BH:
                    dve.wait_ge(maska_in, (i + 1) * 16)
                if h < BH:
                    m, most = mask_b[:], neg_sink[:, b_head(h):b_head(h) + 1]
                else:
                    m, most = mask_a[:], 3.0e38
                hold(dve)
                nc.vector.tensor_tensor_reduce(
                    prob[h % 2][:, 0:w], score[h % 2][:, 0:w], m, 1.0, most, ALU.add, ALU.min,
                    neg_m[:, h:h + 1]).then_inc(masked, 1)

            def denominator(i, h):
                g = i * HEADS + h
                dve.wait_ge(exped, g + 1)
                if h < BH:
                    chain.then(nc.vector.tensor_tensor(den[:, h:h + 1], den[:, h:h + 1],
                                                       sink_e[:, h:h + 1], ALU.add))
                nc.vector.reciprocal(r_den[:, h:h + 1], den[:, h:h + 1]).then_inc(den_ready, 1)

            def dot_row(i, k):
                row, p = down[:, k % DOWN, :], k // TOPK
                dve.wait_ge(down_in[k % DOWN], (i * (PER // DOWN) + k // DOWN + 1) * 16)
                nc.vector.tensor_tensor_reduce(row, row, h2_p[p], 1.0, 0.0, ALU.mult, ALU.add,
                                               dots[p][:, k % TOPK:k % TOPK + 1]).then_inc(dotted, 1)

            def add_row(i, k):
                p = 1 - k // TOPK
                n = i * PER + k - TOPK
                total = keep["sums"][p][:]
                dve.wait_ge(up_in[k % UP], (i * (PER // UP) + (k - TOPK) // UP + 1) * 16)
                dve.wait_ge(upped, n + UP)
                nc.vector.scalar_tensor_tensor(out=total, in0=up[:, k % UP, :],
                                               scalar=wgt[p][:, k % TOPK:k % TOPK + 1], in1=total,
                                               op0=ALU.mult, op1=ALU.add).then_inc(upped, 1)

            def weigh(i, p):
                dve.wait_ge(activated, i * 2 + p + 1)
                chain.then(nc.vector.tensor_tensor(
                    wgt[p][:], acts[p][:], keep["gate_all"][:, bass.ds((i * 2 + p) * TOPK, TOPK)], ALU.mult))

            def merge(j):
                dve.wait_ge(squared, j * 4 + 4)
                chain.then(nc.vector.tensor_scalar(sq[:, 4:6], sq[:, 0:2], 1.0 / 512, RMS_EPS,
                                                   ALU.mult, ALU.add))
                newton(rr[:, 0:2], sq[:, 2:4], sq[:, 4:6], rr[:, 2:4])
                for b in range(2):
                    chain(nc.vector.tensor_scalar(merged[:, b * 512:(b + 1) * 512],
                                                  heads_raw[:, b * 512:(b + 1) * 512], rr[:, b:b + 1], None,
                                                  ALU.mult))
                chain.wait()
                dve.sem_inc(merged_ready, 1)

            def weigh_w_out(k):
                dve.wait_ge(keep["w_out_loaded"], 32)
                nc.vector.tensor_scalar(keep["w_out"][:, k, :], keep["w_out"][:, k, :], gn[:, k:k + 1], None,
                                        ALU.mult).then_inc(keep["w_out_weighed"], 1)

            def mix(j):
                dve.wait_ge(mixed, j + 1)
                for c in range(2):
                    chain(nc.vector.tensor_tensor(z[:, c * 512:(c + 1) * 512], score[c][:, 512:1024],
                                                  rows[:, 0, c * 512:(c + 1) * 512], ALU.mult))
                chain.wait()
                dve.sem_inc(mix_read, 1)
                dve.wait_ge(x_sem, (j + 1) * 16)
                chain.then(nc.vector.scalar_tensor_tensor(out=z, in0=x_in, scalar=ALPHA, in1=z,
                                                          op0=ALU.mult, op1=ALU.add))
                for b in range(2):
                    chain(nc.vector.bn_stats(stats[:, 6 * b:6 * b + 6], z[:, b * 512:(b + 1) * 512]))
                chain.wait()
                nc.vector.bn_aggr(mv[:], stats[:]).then_inc(stat_ready, 1)

            def layer_norm(j):
                dve.wait_ge(rooted, j + 1)
                dve.wait_ge(stat_ready, j + 1)
                chain.then(nc.vector.tensor_scalar(lr[:, 1:2], mv[:, 1:2], LN_EPS, None, ALU.add))
                newton(lr[:, 2:3], lr[:, 0:1], lr[:, 1:2], lr[:, 3:4])
                dve.wait_ge(stored, (j + 1) * 48)
                chain.then(nc.vector.tensor_scalar(x2[:], z, mv[:, 0:1], lr[:, 2:3],
                                                   ALU.subtract, ALU.mult))
                chain.then(nc.vector.tensor_tensor(x2[:], x2[:], ln[:, 0, :], ALU.mult))
                nc.vector.tensor_tensor(x2[:], x2[:], ln[:, 1, :], ALU.add).then_inc(x2_ready, 1)

            def body(i, first, last):
                for h in range(HEADS):
                    mask(i, h)
                    if not first and h == M_AT:
                        merge(i - 1)
                    if not first and h == READ_AT:
                        mix(i - 1)
                    if not (first and h < 1):
                        denominator(*before(i, h, 1))
                    if side:
                        for k in range(2 * h, 2 * h + 2):
                            dot_row(i, k)
                        if h == 0 and not first:
                            weigh(i - 1, 1)
                        if h == 8:
                            weigh(i, 0)
                        for k in range(2 * h, 2 * h + 2):
                            if not (first and h < 8):
                                add_row(i, k)
                    if seq == 0 and first and h >= 8:
                        weigh_w_out(h - 8)
                    if not first and h == LN_AT:
                        layer_norm(i - 1)
                chain.close()

            if side:
                chain.close()
            tiled(dve, body)
            last = tiles - 1
            denominator(last, HEADS - 1)
            if side:
                weigh(last, 1)
            merge(last)
            def add_rows(lo, hi):
                for k in range(lo, hi) if side else ():
                    add_row(tiles, k)

            add_rows(0, 10)
            mix(last)
            add_rows(10, 12)
            layer_norm(last)
            add_rows(12, TOPK)
            if side:
                dve.wait_ge(upped, tiles * PER + UP)
            chain.close()

        @block.tensor
        def _(pe):
            ident = keep["ident"]
            pe.sem_inc(summed, 2)
            pe.sem_inc(h2_turned, 1)

            def scores(i, h):
                g = i * HEADS + h
                pe.wait_ge(masked, g + 1)
                lo = (h % 2) * HD
                w = keys_of(h) * P
                q = q_t[lo:lo + HD, 4 + h // 2 if h < BH else (h - BH) // 2, :]
                if h == 0:
                    pe.wait_ge(qb_in, (i + 1) * 16)
                    pe.wait_ge(win_in, (i + 1) * 32)
                if h == BH:
                    pe.wait_ge(qa_in, (i + 1) * 16)
                    pe.wait_ge(kv_in, 32)
                for c in range(0, w, 512):
                    n = min(512, w - c)
                    rhs = k_t[lo:lo + HD, (h - BH) // 2, c:c + n] if h >= BH else \
                        k_b[lo:lo + HD].rearrange("p j k -> p (j k)")
                    mm = nc.tensor.matmul(score[h % 2][:, c:c + n], q, rhs, start=True, stop=True)
                mm.then_inc(scored, 1)

            def turn_probs(i, h):
                g = i * HEADS + h
                pe.wait_ge(exped, g + 1)
                pe.wait_ge(copied, g + 1)
                for k in range(keys_of(h)):
                    mm = nc.tensor.transpose(turn[:, k, :], prob[h % 2][:, k * P:(k + 1) * P], ident[:])
                mm.then_inc(turned, 1)

            def sum_values(i, h):
                g = i * HEADS + h
                pe.wait_ge(copied, g + 2)
                if not (isinstance(i, int) and i == 0 and h < 2):
                    pe.wait_ge(head_done, g - 1)
                n = keys_of(h)
                for k in range(n):
                    if h < BH:
                        v = v_b[:, k, h % 2 * HD:(h % 2 + 1) * HD]
                    else:
                        v = v_a[:, k, (h - BH) * HD:(h - BH + 1) * HD]
                    mm = nc.tensor.matmul(out_ps[h % 2][:, 0:HD], prob_t[h % 2][:, k, :], v,
                                          start=(k == 0), stop=(k == n - 1))
                mm.then_inc(summed, 1)

            def turn_rows(src, count):
                for k in range(DC):
                    mm = nc.tensor.transpose(turn[:, k, :], src[:, k * P:(k + 1) * P], ident[:])
                mm.then_inc(count, 1)

            def turn_merged(j, g):
                pe.wait_ge(merged_ready, j + 1)
                pe.wait_ge(copied, g)
                turn_rows(merged, merged_turned)

            def mix(j, parts):
                pe.wait_ge(merged_copied, j + 1)
                pe.wait_ge(keep["w_out_weighed"], DC)
                for part in parts:
                    c = part // 2
                    for k in range(part % 2 * DC // 2, (part % 2 + 1) * DC // 2):
                        mm = nc.tensor.matmul(score[c][:, 512:1024], merged_t[:, k, :],
                                              keep["w_out"][:, k, c * 512:(c + 1) * 512],
                                              start=(k == 0), stop=(k == DC - 1))
                if part == 3:
                    mm.then_inc(mixed, 1)

            def turn_h2(j, g):
                pe.wait_ge(h2_ready, j + 1)
                pe.wait_ge(mixed, j + 1)
                pe.wait_ge(copied, g)
                turn_rows(h2, h2_turned)

            def body(i, first, last):
                g0 = i * HEADS
                for h in range(HEADS):
                    if h + 1 < HEADS:
                        if not first and h + 1 == BH:
                            pe.wait_ge(mix_read, i)
                        scores(i, h + 1)
                    elif not last:
                        scores(i + 1, 0)
                    if not first and h == M_AT + 1:
                        pe.wait_ge(merged_copied, i)
                    if not first and h == H2_AT + 1:
                        pe.wait_ge(h2_copied, i * 2)
                    turn_probs(i, h)
                    if not (first and h < 1):
                        sum_values(*before(i, h, 1))
                    if not first and h == M_AT:
                        turn_merged(i - 1, g0 + h + 2)
                    if not first and h in MIX_AT:
                        mix(i - 1, (h - MIX_AT[0],))
                    if not first and h == H2_AT:
                        turn_h2(i - 1, g0 + h + 2)

            scores(0, 0)
            tiled(pe, body)
            last = tiles - 1
            sum_values(last, HEADS - 1)
            turn_merged(last, tiles * HEADS + 1)
            pe.wait_ge(masked, tiles * HEADS + 2)
            mix(last, range(4))
            turn_h2(last, tiles * HEADS + 1)



class Retrieval:

    QW = 2 * N_KEYS
    LOW = -3.0e38

    def __init__(self, nc, keep, lanes, sb, sem, ps):
        self.nc, self.keep = nc, keep
        self.keys = sb("keys", [P, PH * self.QW])
        self.iota = sb("iota", [P, TOPK])
        self.h2t = sb("h2t", [P, DC, P])
        self.q, self.q_t = sb("q", [P, self.QW]), sb("q_t", [P, 2, P])
        self.sc = [sb(f"sc{b}", [P, 2, N_KEYS]) for b in range(2 * lanes)]
        each = lambda name, shape, dt=F32: [sb(f"{name}{b}", shape, dt) for b in range(lanes)]
        self.sc2 = each("sc2_", [P, 2, N_KEYS])
        self.top = each("top", [P, 2, TOPK])
        self.top_i, self.top_f = each("top_i", [P, 2, TOPK], U32), each("top_f", [P, 2, TOPK])
        self.cand, self.cand2 = each("cand", [P, TOPK, TOPK]), each("cand2_", [P, TOPK, TOPK])
        self.best = [sb(f"best{b}", [P, TOPK]) for b in range(2)]
        self.best_i = each("best_i", [P, TOPK], U32)
        self.pair_i, self.pair_f = each("pair_i", [P, 2, TOPK], U32), each("pair_f", [P, 2, TOPK])
        self.hot, self.hot2 = each("hot", [P, 2, TOPK, TOPK]), each("hot2_", [P, 2, TOPK, TOPK])
        self.key_f = each("key_f", [P, 2, TOPK])
        self.neg_b = [sb(f"neg_b{b}", [P, 1]) for b in range(2)]
        self.gate_e = [sb(f"gate_e{b}", [P, TOPK]) for b in range(2)]
        self.gate_s = [sb(f"gate_s{b}", [P, 1]) for b in range(2)]
        self.gate_r = sb("gate_r", [P, 1])
        self.q_ps, self.qt_ps, self.sc_ps = ps("q_ps", [P, 512]), ps("qt_ps", [P, 4, P]), ps("sc_ps", [P, 4, P])
        self.const_in, self.h2t_in = sem("r_const_in"), sem("h2t_in")
        self.q_done, self.q_copied = sem("q_done"), sem("q_copied")
        self.qt_done, self.qt_copied = sem("qt_done"), sem("qt_copied")
        self.sc_done, self.sc_copied = sem("sc_done"), sem("sc_copied")
        self.best_ready, self.gated, self.idx_ready = sem("best_ready"), sem("gated"), sem("idx_ready")

    def load(self, sp, io, tile):
        sp.dma_start(self.h2t[:], io["h2t"][tile]).then_inc(self.h2t_in, 16)
        sp.dma_start(self.keys[:], io["keys_t"]).then_inc(self.const_in, 16)
        sp.dma_start(self.iota[:], io["iota"]).then_inc(self.const_in, 16)

    def query(self, pe, m, e, tiles_in):
        nc, w_query = self.nc, self.keep["w_in_a"]
        pe.wait_ge(self.h2t_in, tiles_in * 16)
        pe.wait_ge(self.q_copied, m + 1)
        for k in range(DC):
            mm = nc.tensor.matmul(self.q_ps[:, 0:self.QW], self.h2t[:, k, :],
                                  w_query[:, k, bass.ds(e * self.QW, self.QW)],
                                  start=(k == 0), stop=(k == DC - 1))
        mm.then_inc(self.q_done, 1)
        pe.wait_ge(self.q_copied, m + 2)
        for h in range(2):
            mm = nc.tensor.transpose(self.qt_ps[:, h, :], self.q[:, h * P:(h + 1) * P], self.keep["ident"][:])
        mm.then_inc(self.qt_done, 1)
        pe.wait_ge(self.qt_copied, m + 1)
        pe.wait_ge(self.sc_copied, m + 1)
        for h in range(2):
            mm = nc.tensor.matmul(self.sc_ps[:, h, :], self.q_t[:, h, :],
                                  self.keys[:, bass.ds(e * self.QW + h * N_KEYS, N_KEYS)], start=True, stop=True)
        mm.then_inc(self.sc_done, 1)

    def start_act(self, act):
        act.sem_inc(self.q_copied, 1)
        act.sem_inc(self.sc_copied, 1)

    def move_query(self, act, m, b):
        nc = self.nc
        act.wait_ge(self.q_done, m + 1)
        nc.scalar.copy(self.q[:], self.q_ps[:, 0:self.QW]).then_inc(self.q_copied, 1)
        act.wait_ge(self.qt_done, m + 1)
        nc.scalar.copy(self.q_t[:], self.qt_ps[:, 0:2, :]).then_inc(self.qt_copied, 1)
        act.wait_ge(self.sc_done, m + 1)
        act.wait_ge(self.idx_ready, m + 1)
        nc.scalar.copy(self.sc[b][:], self.sc_ps[:, 0:2, :]).then_inc(self.sc_copied, 1)

    def gates(self, act, m, b):
        act.wait_ge(self.best_ready, m + 1)
        self.nc.scalar.activation(self.gate_e[b][:], self.best[b][:], ACT.Exp, bias=self.neg_b[b][:, 0:1],
                                  accum_out=self.gate_s[b][:, 0:1]).then_inc(self.gated, 1)

    def pick(self, dve, chain, m, work, idx_free=None):
        nc, top, top_i, LOW = self.nc, self.top, self.top_i, self.LOW
        lanes = [(n, self.best[b], self.sc[s], self.sc2[n], idx, self.neg_b[b]) for n, (b, s, idx) in enumerate(work)]
        flat, flat2 = ([v[:].rearrange("p a b -> p (a b)") for v in w] for w in (self.cand, self.cand2))
        halves = [(h, lane) for lane in lanes for h in range(2)]
        dve.wait_ge(self.sc_copied, m + 2)
        hold(dve)
        for h, (n, best, sc, sc2, idx, neg_b) in halves:
            chain(nc.vector.max(top[n][:, h, 0:8], sc[:, h, :]))
        chain.wait()
        for h, (n, best, sc, sc2, idx, neg_b) in halves:
            chain(nc.vector.match_replace(sc2[:, h, :], top[n][:, h, 0:8], sc[:, h, :], LOW))
        chain.wait()
        for h, (n, best, sc, sc2, idx, neg_b) in halves:
            chain(nc.vector.max(top[n][:, h, 8:16], sc2[:, h, :]))
        for h, (n, best, sc, sc2, idx, neg_b) in halves:
            chain(nc.vector.max_index(top_i[n][:, h, 0:8], top[n][:, h, 0:8], sc[:, h, :]))
        chain.wait()
        for n, *_ in lanes:
            chain(nc.vector.tensor_tensor(self.cand[n][:], top[n][:, 0, :].unsqueeze(2).to_broadcast([P, TOPK, TOPK]),
                                          top[n][:, 1, :].unsqueeze(1).to_broadcast([P, TOPK, TOPK]), ALU.add))
        for h, (n, best, sc, sc2, idx, neg_b) in halves:
            chain(nc.vector.max_index(top_i[n][:, h, 8:16], top[n][:, h, 8:16], sc2[:, h, :]))
        chain.wait()
        for n, best, *_ in lanes:
            chain(nc.vector.max(best[:, 0:8], flat[n]))
            chain(nc.vector.tensor_copy(self.top_f[n][:], top_i[n][:]))
        chain.wait()
        for n, best, sc, sc2, idx, neg_b in lanes:
            chain(nc.vector.match_replace(flat2[n], best[:, 0:8], flat[n], LOW))
            chain(nc.vector.max_index(self.best_i[n][:, 0:8], best[:, 0:8], flat[n]))
            chain(nc.vector.tensor_scalar(neg_b[:, 0:1], best[:, 0:1], -1.0, None, ALU.mult))
        chain.wait()
        for n, best, *_ in lanes:
            chain(nc.vector.max(best[:, 8:16], flat2[n]))
        chain.wait()
        dve.sem_inc(self.best_ready, len(lanes))
        for n, best, *_ in lanes:
            chain(nc.vector.max_index(self.best_i[n][:, 8:16], best[:, 8:16], flat2[n]))
        chain.wait()
        for n, *_ in lanes:
            chain(nc.vector.tensor_scalar(self.pair_i[n][:, 0, :], self.best_i[n][:], 4, None, ALU.logical_shift_right))
            chain(nc.vector.tensor_scalar(self.pair_i[n][:, 1, :], self.best_i[n][:], TOPK - 1, None, ALU.bitwise_and))
        chain.wait()
        for n, *_ in lanes:
            chain(nc.vector.tensor_copy(self.pair_f[n][:], self.pair_i[n][:]))
        chain.wait()
        shape = [P, 2, TOPK, TOPK]
        for n, *_ in lanes:
            chain(nc.vector.tensor_tensor(
                self.hot[n][:], self.pair_f[n][:].unsqueeze(3).to_broadcast(shape),
                self.iota[:].unsqueeze(1).unsqueeze(1).to_broadcast(shape), ALU.is_equal))
        chain.wait()
        for n, *_ in lanes:
            chain(nc.vector.tensor_tensor(self.hot2[n][:], self.hot[n][:],
                                          self.top_f[n][:].unsqueeze(2).to_broadcast(shape), ALU.mult))
        chain.wait()
        for n, *_ in lanes:
            chain(nc.vector.tensor_reduce(self.key_f[n][:], self.hot2[n][:], AX_X, ALU.add))
        chain.wait()
        if idx_free:
            idx_free()
        for n, best, sc, sc2, idx, neg_b in lanes:
            nc.vector.scalar_tensor_tensor(out=idx, in0=self.key_f[n][:, 0, :], scalar=float(N_KEYS),
                                           in1=self.key_f[n][:, 1, :], op0=ALU.mult, op1=ALU.add
                                           ).then_inc(self.idx_ready, 1)


def prompt_retrieval(nc, io, keep):
    tiles = SEQS[0][1]
    with ExitStack() as ctx:
        def sb(name, shape, dt=F32):
            return ctx.enter_context(nc.sbuf_tensor(f"r_{name}", shape, dt))

        def sem(name):
            return ctx.enter_context(nc.semaphore(f"r_{name}"))

        def ps(name, shape):
            return ctx.enter_context(nc.psum_tensor(f"r_{name}", shape, F32))

        rt = Retrieval(nc, keep, 2, sb, sem, ps)
        idx = [sb(f"idx{b}", [P, TOPK], U32) for b in range(2)]
        block = ctx.enter_context(nc.Block())

        QUADS = tiles * PH // 4

        @block.sync
        def _(sp):
            rt.load(sp, io, 0)
            sp.wait_ge(rt.q_done, PH)
            sp.dma_start(rt.h2t[:], io["h2t"][1]).then_inc(rt.h2t_in, 16)

        @block.tensor
        def _(pe):
            pe.wait_ge(rt.const_in, 32)
            pe.wait_ge(keep["w_query_loaded"], 16)
            for t in range(tiles):
                with pe.Fori(0, PH) as e:
                    rt.query(pe, t * PH + e, e, t + 1)

        @block.scalar
        def _(act):
            rt.start_act(act)

            def quad(q, last):
                for pair in range(2):
                    for b in range(2) if not (last and pair == 1) else ():
                        n = pair * 2 + b + 2
                        rt.move_query(act, q * 4 + n, n % 4)
                    for b in range(2):
                        rt.gates(act, q * 4 + pair * 2 + b, b)

            for b in range(2):
                rt.move_query(act, b, b)
            with act.Fori(0, QUADS - 1) as q:
                quad(q, False)
            quad(QUADS - 1, True)

        @block.vector
        def _(dve):
            chain = Chain(dve, keep["vector_chain"])
            dve.sem_inc(rt.idx_ready, 4)
            dve.wait_ge(rt.const_in, 32)

            def pair_of(q, pair, tile):
                e = q * 4 + pair * 2
                m = tile * PH + e
                rt.pick(dve, chain, m + 1, [(b, pair * 2 + b, idx[b][:]) for b in range(2)])
                dve.wait_ge(rt.idx_ready, m + 6)
                for b in range(2):
                    at = ((e + b) * tiles + tile) * TOPK
                    chain(nc.vector.tensor_copy(keep["idx_all"][:, bass.ds(at, TOPK)], idx[b][:]))
                dve.wait_ge(rt.gated, m + 2)
                for b in range(2):
                    chain(nc.vector.reciprocal(rt.gate_s[b][:, 0:1], rt.gate_s[b][:, 0:1]))
                chain.wait()
                for b in range(2):
                    at = ((e + b) * tiles + tile) * TOPK
                    chain(nc.vector.tensor_scalar(keep["gate_all"][:, bass.ds(at, TOPK)], rt.gate_e[b][:],
                                                  rt.gate_s[b][:, 0:1], None, ALU.mult))
                chain.wait()

            for tile in range(tiles):
                with dve.Fori(0, PH // 4) as q:
                    for pair in range(2):
                        pair_of(q, pair, tile)
                    chain.close()



def experts(nc, io, keep):
    RING = 8
    tile0, tiles = SEQS[1]
    prompt_tiles = SEQS[0][1]
    with ExitStack() as ctx:
        def sb(name, shape, dt=F32):
            return ctx.enter_context(nc.sbuf_tensor(f"e_{name}", shape, dt))

        def sem(name):
            return ctx.enter_context(nc.semaphore(f"e_{name}"))

        def ps(name, shape):
            return ctx.enter_context(nc.psum_tensor(f"e_{name}", shape, F32))

        ident = keep["ident"]
        rt = Retrieval(nc, keep, 1, sb, sem, ps)
        ln = sb("ln", [P, 2, D])
        eps = sb("eps", [P, 1])
        h2 = sb("h2", [P, D])
        x2a = sb("x2a", [P, D])
        gate2 = sb("gate2", [P, D])
        z = sb("z", [P, D])
        y = sb("y", [P, D])
        down = sb("down", [P, RING, D])
        up = sb("up", [P, RING, D])
        idx = [sb(f"idx{b}", [P, TOPK], U32) for b in range(2)]
        dots = [sb(f"dots{b}", [P, TOPK]) for b in range(2)]
        acts = [sb(f"acts{b}", [P, TOPK]) for b in range(2)]
        wgt = sb("wgt", [P, TOPK])
        diag = [sb(f"diag{b}", [P, TOPK, P]) for b in range(2)]
        stats, mv, lr = sb("stats", [P, 12]), sb("mv", [P, 2]), sb("lr", [P, 4])

        acc = ps("acc", [P, D])

        const_in = sem("const_in")
        h2_in, res_in = sem("h2_in"), sem("res_in")
        down_in = [sem(f"down_in{s}") for s in range(RING)]
        up_in = [sem(f"up_in{s}") for s in range(RING)]
        dotted, activated = sem("dotted"), sem("activated")
        diag_ready, upped = sem("diag_ready"), sem("upped")
        stat_ready, rooted, y_ready, y_stored = sem("stat_ready"), sem("rooted"), sem("y_ready"), sem("y_stored")
        set_up = sem("set_up")
        block = ctx.enter_context(nc.Block())

        def first(n):
            return isinstance(n, int) and n == 0

        def steps(eng, step):
            step(0, 0, 0, 1, 0, True)

            def heads(t, last):
                with eng.Fori(0, PH // 2 - 1) as p:
                    for e in range(2):
                        step(t * PH + p * 2 + e + 1, 1 - e, t, p * 2 + e + 2, t, False)
                step(t * PH + PH - 1, 1, t, None if last else 0, t + 1, False)

            with eng.Fori(0, tiles - 1) as t:
                heads(t, False)
                step(t * PH + PH, 0, t + 1, 1, t + 1, True)
            heads(tiles - 1, True)

        @block.sync
        def _(sp):
            sp.dma_start(keep["w_in_a"][:, DC - 1, :], io["w_query"][(DC - 1) * P:, :]).then_inc(
                keep["w_query_loaded"], 16)
            rt.load(sp, io, tile0)
            sp.dma_start(h2[:], io["h2"][tile0]).then_inc(h2_in, 16)
            for j in range(2):
                sp.dma_start(ln[:, j, :], io["ln2"][j].partition_broadcast(P)).then_inc(const_in, 16)

            for j in range(prompt_tiles + 1):
                if j:
                    sp.wait_ge(stat_ready, j)
                sp.dma_start(x2a[:], io["x2a"][j]).then_inc(res_in, 16)
                sp.dma_start(gate2[:], io["gate2"][j].partition_broadcast(P)).then_inc(res_in, 16)
                if j:
                    sp.wait_ge(y_ready, j)
                    sp.dma_start(io["y"][j - 1], y[:]).then_inc(y_stored, 16)

            def tile(t, last):
                if not last:
                    sp.wait_ge(rt.q_done, t * PH + PH)
                    hold(sp)
                    sp.dma_start(rt.h2t[:], io["h2t"][t + tile0 + 1]).then_inc(rt.h2t_in, 16)
                    sp.wait_ge(dotted, (t * PH + PH) * TOPK + RING)
                    hold(sp)
                    sp.dma_start(h2[:], io["h2"][t + tile0 + 1]).then_inc(h2_in, 16)
                    sp.wait_ge(stat_ready, t + tile0 + 1)
                    hold(sp)
                    sp.dma_start(x2a[:], io["x2a"][t + tile0 + 1]).then_inc(res_in, 16)
                    sp.dma_start(gate2[:], io["gate2"][t + tile0 + 1].partition_broadcast(P)).then_inc(res_in, 16)
                sp.wait_ge(y_ready, t + tile0 + 1)
                hold(sp)
                sp.dma_start(io["y"][t + tile0], y[:]).then_inc(y_stored, 16)

            with sp.Fori(0, tiles - 1) as t:
                tile(t, False)
            tile(tiles - 1, True)
            sp.wait_ge(y_stored, 16 * (TILES + 1))

        @block.gpsimd
        def _(pool):
            def gather(ring, table, index, landed):
                pool.indirect_dma_start(ring, None, table, bass.IndirectOffsetOnAxis(ap=index, axis=0)
                                        ).then_inc(landed, 16)

            def step(n, b, t, e_next, t_next, start):
                pool.wait_ge(rt.idx_ready, n + 3)
                hold(pool)
                for s in range(TOPK):
                    pool.wait_ge(dotted, n * TOPK + s + 1)
                    hold(pool)
                    gather(down[:, s % RING, :], io["down"], idx[b][:, s:s + 1], down_in[s % RING])
                for s in range(TOPK):
                    pool.wait_ge(upped, n * TOPK + s + 1 + 2 * TOPK - RING)
                    hold(pool)
                    gather(up[:, s % RING, :], io["up"], idx[b][:, s:s + 1], up_in[s % RING])
            steps(pool, step)

        @block.scalar
        def _(act):
            rt.start_act(act)
            act.wait_ge(set_up, 1)

            def step(n, b, t, e_next, t_next, start):
                if e_next is not None:
                    rt.move_query(act, n + 1, 1 - b)
                act.wait_ge(dotted, (n + 1) * TOPK + RING)
                nc.scalar.activation(acts[b][:], dots[b][:], ACT.Gelu).then_inc(activated, 1)
                if e_next is not None:
                    rt.gates(act, n + 1, 1 - b)
                if start and not first(n):
                    root(t + tile0 - 1)

            def root(t):
                act.wait_ge(stat_ready, t + 1)
                nc.scalar.activation(lr[:, 0:1], mv[:, 1:2], ACT.Sqrt, bias=eps[:, 0:1], scale=1.0
                                     ).then_inc(rooted, 1)

            rt.move_query(act, 0, 0)
            rt.gates(act, 0, 0)
            for t in range(prompt_tiles):
                root(t)
            steps(act, step)
            root(TILES - 1)

        @block.vector
        def _(dve):
            chain = Chain(dve, keep["vector_chain"])
            chain(nc.vector.memset(eps[:], LN_EPS))
            chain.close()
            dve.sem_inc(set_up, 1)
            dve.sem_inc(dotted, RING)
            dve.sem_inc(rt.idx_ready, 2)
            dve.wait_ge(const_in, 32)
            dve.wait_ge(rt.const_in, 32)

            def retrieve(m, b):
                rt.pick(dve, chain, m, [(b, b, idx[b][:])], lambda: dve.wait_ge(upped, (m + 1) * TOPK))

            def step(n, b, t, e_next, t_next, start):
                dve.wait_ge(h2_in, (t + 1) * 16)
                for s in range(TOPK):
                    row = down[:, s % RING, :]
                    dve.wait_ge(down_in[s % RING], (n * 2 + s // RING + 1) * 16)
                    nc.vector.tensor_tensor_reduce(row, row, h2[:], 1.0, 0.0, ALU.mult, ALU.add,
                                                   dots[b][:, s:s + 1]).then_inc(dotted, 1)
                if start and not first(n):
                    summed_in_psum(t - 1)
                    residual(t + tile0 - 1, acc[:])
                dve.wait_ge(rt.gated, n + 1)
                chain.then(nc.vector.reciprocal(rt.gate_r[:], rt.gate_s[b][:, 0:1]))
                dve.wait_ge(activated, n + 1)
                dve.wait_ge(upped, (n + 1) * TOPK)
                chain.then(nc.vector.scalar_tensor_tensor(out=wgt[:], in0=rt.gate_e[b][:], scalar=rt.gate_r[:, 0:1],
                                                          in1=acts[b][:], op0=ALU.mult, op1=ALU.mult))
                chain.then(nc.vector.tensor_tensor(
                    diag[b][:], ident[:].unsqueeze(1).to_broadcast([P, TOPK, P]),
                    wgt[:].unsqueeze(2).to_broadcast([P, TOPK, P]), ALU.mult))
                dve.sem_inc(diag_ready, 1)
                if e_next is not None:
                    retrieve(n + 1, 1 - b)
                if start and not first(n):
                    layer_norm(t + tile0 - 1)
                chain.close()

            def summed_in_psum(t):
                dve.wait_ge(upped, (t * PH + PH) * TOPK + 2 * TOPK)

            def residual(t, experts_sum):
                dve.wait_ge(res_in, (t + 1) * 32)
                chain.then(nc.vector.tensor_tensor(z[:], experts_sum, gate2[:], ALU.mult))
                chain.then(nc.vector.tensor_tensor(z[:], z[:], x2a[:], ALU.add))
                for h in range(2):
                    chain(nc.vector.bn_stats(stats[:, 6 * h:6 * h + 6], z[:, h * 512:(h + 1) * 512]))
                chain.wait()
                chain.then(nc.vector.bn_aggr(mv[:], stats[:]))
                dve.sem_inc(stat_ready, 1)

            def layer_norm(t):
                chain(nc.vector.tensor_scalar(lr[:, 1:2], mv[:, 1:2], LN_EPS, None, ALU.add))
                chain.wait()
                dve.wait_ge(rooted, t + 1)
                r, tmp = lr[:, 2:3], lr[:, 3:4]
                chain.then(nc.vector.reciprocal(r, lr[:, 0:1]))
                chain.then(nc.vector.tensor_tensor(tmp, r, r, ALU.mult))
                chain.then(nc.vector.tensor_tensor(tmp, tmp, lr[:, 1:2], ALU.mult))
                chain.then(nc.vector.tensor_scalar(tmp, tmp, -0.5, 1.5, ALU.mult, ALU.add))
                chain.then(nc.vector.tensor_tensor(r, r, tmp, ALU.mult))
                chain.then(nc.vector.tensor_scalar(z[:], z[:], mv[:, 0:1], r, ALU.subtract, ALU.mult))
                chain.then(nc.vector.tensor_tensor(z[:], z[:], ln[:, 0, :], ALU.mult))
                dve.wait_ge(y_stored, (t + 1) * 16)
                chain.then(nc.vector.tensor_tensor(y[:], z[:], ln[:, 1, :], ALU.add))
                dve.sem_inc(y_ready, 1)

            dve.sem_inc(y_stored, 16)
            retrieve(0, 0)
            for t in range(prompt_tiles):
                residual(t, keep["sums"][t][:])
                layer_norm(t)
            chain.close()
            steps(dve, step)
            summed_in_psum(tiles - 1)
            residual(TILES - 1, acc[:])
            layer_norm(TILES - 1)
            chain.close()

        @block.tensor
        def _(pe):
            pe.sem_inc(upped, 2 * TOPK)
            pe.wait_ge(rt.const_in, 32)
            pe.wait_ge(keep["w_query_loaded"], 16 * 5)

            def step(n, b, t, e_next, t_next, start):
                if e_next is not None:
                    rt.query(pe, n + 1, e_next, t_next + 1)
                pe.wait_ge(diag_ready, n + 1)
                for s in range(TOPK):
                    pe.wait_ge(up_in[s % RING], (n * 2 + s // RING + 1) * 16)
                    for c in range(2):
                        mm = nc.tensor.matmul(acc[:, c * 512:(c + 1) * 512], diag[b][:, s, :],
                                              up[:, s % RING, c * 512:(c + 1) * 512], start=start and s == 0,
                                              stop=e_next is None and s == TOPK - 1,
                                              skip_group_check=True)
                    mm.then_inc(upped, 1)

            rt.query(pe, 0, 0, 1)
            steps(pe, step)



def program(nc, io):
    with ExitStack() as outer:
        def sb(name, shape, stack=outer):
            return stack.enter_context(nc.sbuf_tensor(name, shape, F32))

        keep = {n: outer.enter_context(nc.semaphore(n)) for n in
                ("ident_loaded", "w_in_loaded", "w_out_loaded", "w_out_weighed", "w_query_loaded",
                 "vector_chain", "gpsimd_chain")}
        keep["ident"] = sb("ident_sb", [P, P])
        keep["mod_cols"] = sb("mod_cols", [P, 4 * DC])
        keep["sums"] = [sb(f"sums{t}", [P, D]) for t in range(2)]
        keep["w_in_a"] = sb("w_in_a", [P, DC, 2048])
        with ExitStack() as early:
            with ExitStack() as first:
                keep["w_in_b"] = sb("w_in_b", [P, DC, INW - 2048], first)
                modulation(nc, io, keep)
                projection(nc, io, keep)
            keep["w_out"] = sb("w_out_sb", [P, DC, D], early)
            keep["idx_all"] = early.enter_context(nc.sbuf_tensor("idx_all", [P, 2 * PH * TOPK], U32))
            keep["gate_all"] = sb("gate_all", [P, 2 * PH * TOPK], early)
            attention(nc, io, keep, 0)
            prompt_retrieval(nc, io, keep)
            attention(nc, io, keep, 1)
        experts(nc, io, keep)



def shape_constants():
    i = np.arange(1024)[:, None]
    j = np.arange(1024)[None, :]
    off = np.abs(i - j)
    count = (off <= 64).astype(np.float64) + ((off <= 256) & (off % 4 == 0)) + (off % 16 == 0)
    mask_a = np.where(count > 0, -np.log(np.maximum(count, 1)), BIG).astype(np.float32).reshape(8, P, 1024)
    mask_b = np.full((TILES, P, 3 * P), BIG, np.float32)
    trig = np.zeros((TILES, P, 2 * HALF), np.float32)
    inv = (np.float32(500000.0) ** (-np.arange(HALF, dtype=np.float32) * np.float32(2.0) / np.float32(16))
           ).astype(np.float32)
    for tile0, tiles in SEQS:
        for t in range(tiles):
            q = t * P + np.arange(P)[:, None]
            k = (t - 1) * P + np.arange(3 * P)[None, :]
            mask_b[tile0 + t][(np.abs(q - k) <= 128) & (k >= 0) & (k < tiles * P)] = 0.0
            ang = (q.astype(np.float32) * inv[None, :]).astype(np.float64)
            trig[tile0 + t] = np.concatenate([np.cos(ang), np.sin(ang)], 1).astype(np.float32)
    return {"mask_a": mask_a, "mask_b": mask_b, "trig": trig, "ident": np.eye(P, dtype=np.float32),
            "iota": np.tile(np.arange(TOPK, dtype=np.float32), (P, 1))}


def lay_out(x_prompt, x_sample, c_prompt, c_sample, w_mod, b_mod, w_in, attn_sink, gn_a, gn_b, w_out,
            ln1_g, ln1_b, w_query, sub_keys, expert_down, expert_up, ln2_g, ln2_b):
    x = np.concatenate([np.asarray(x_prompt)[0], np.asarray(x_sample)[0]], 0).reshape(TILES, P, D)
    c = np.stack([np.asarray(c_prompt)[0], np.asarray(c_sample)[0]])
    w = np.array(w_in[0])
    q_b = w[:, QB:KVB].reshape(D, BH, HD)[:, [b_head(j) for j in range(BH)]].reshape(D, BH * HD)
    w = np.concatenate([w[:, :QB], q_b, w[:, KVB:]], 1)
    data = {
        "x": x,
        "x_t": x.reshape(TILES, P, DC, P).transpose(0, 3, 2, 1),
        "c_t": c.reshape(2, DC, P).transpose(2, 1, 0).reshape(P, 2 * DC),
        "w_mod": w_mod[0], "b_mod": b_mod[0], "w_in": w, "attn_sink": attn_sink[0],
        "gn": np.concatenate([gn_a[0], gn_b[0]]).reshape(DC, P).T, "w_out": w_out[0],
        "ln1": np.stack([ln1_g[0], ln1_b[0]]), "w_query": w_query[0],
        "keys_t": np.asarray(sub_keys)[0].transpose(3, 0, 1, 2).reshape(P, PH * 2 * N_KEYS),
        "down": expert_down[0], "up": expert_up[0], "ln2": np.stack([ln2_g[0], ln2_b[0]]),
    }
    data.update(shape_constants())
    return {"in_" + n: np.ascontiguousarray(a) for n, a in data.items()}


SCRATCH = {
    "mod_rows": (2, 4 * D), "qt": (TILES, P, 8, P), "kt0": (P, 4, 256), "kt1": (P, 4, 1024),
    "va0": (2, P, 512), "va1": (8, P, 512), "kb": (SLOTS, P, P), "vb": (SLOTS, P, P),
    "gate2": (TILES, D), "h2": (TILES, P, D), "x2a": (TILES, P, D), "h2t": (TILES, P, DC, P),
}


def declare_and_program(nc, arrays):
    io = {n[3:]: nc.dram_tensor(n, a.shape, F32, kind="ExternalInput").ap() for n, a in arrays.items()}
    for n, shape in SCRATCH.items():
        io[n] = nc.dram_tensor("scratch_" + n, shape, F32, kind="Internal").ap()
    io["kt"], io["va"] = (io["kt0"], io["kt1"]), (io["va0"], io["va1"])
    io["y"] = nc.dram_tensor("y", (TILES, P, D), F32, kind="ExternalOutput").ap()
    program(nc, io)


def kernel(**inputs):
    import concourse.bacc as bacc
    from concourse.bass_utils import run_bass_kernel_spmd

    arrays = lay_out(**inputs)
    nc = bacc.Bacc("TRN2", target_bir_lowering=False, num_devices=1)
    declare_and_program(nc, arrays)
    r = run_bass_kernel_spmd(nc, [arrays], core_ids=[0])
    y = r.results[0]["y"].reshape(TILES * P, D)
    return y[:2 * P].reshape(1, 2 * P, D), y[2 * P:].reshape(1, 8 * P, D)
```

```python
from contextlib import ExitStack

import numpy as np

import concourse.bass as bass
from concourse import mybir

P = 128
D = 1024
DC = D // P
SEQS = ((0, 2), (2, 8))
TILES = 10
HD = 64
HALF = 8
AH, BH, BKV = 8, 8, 2
HEADS = AH + BH
QA, KA, VA, QB, KVB = 0, 512, 1024, 1536, 2048
INW = 2304
N_KEYS = 128
PH = 8
TOPK = 16
SLOTS = 14
BIG = 1.0e30
ALPHA = 2.0 ** 0.25
LN_EPS = 1e-5
RMS_EPS = 1e-6

ALU = mybir.AluOpType
ACT = mybir.ActivationFunctionType
F32 = mybir.dt.float32
U32 = mybir.dt.uint32
AX_X = mybir.AxisListType.X


def first_slot(tile0):
    return 1 if tile0 == 0 else 5


def b_head(j):
    return j // 2 + (BH // BKV) * (j % 2)


def hold(eng):
    eng.nop(nofuse=True)


class Chain:

    def __init__(self, eng, sem):
        self.eng, self.sem, self.n = eng, sem, 0

    def __call__(self, ins):
        ins.then_inc(self.sem, 1)
        self.n += 1
        return self.n

    def wait(self, n=None):
        self.eng.wait_ge(self.sem, self.n if n is None else n)

    def then(self, ins):
        self(ins)
        self.wait()

    def close(self):
        if self.n:
            self.wait()
            self.eng.sem_clear(self.sem)
        self.n = 0



def modulation(nc, io, keep):
    CH, BUFS = 512, 4
    NCH = 6 * D // CH
    with ExitStack() as ctx:
        def sb(name, shape, dt=F32):
            return ctx.enter_context(nc.sbuf_tensor(name, shape, dt))

        def sem(name):
            return ctx.enter_context(nc.semaphore(name))

        wm = [sb(f"wm{b}", [P, DC, CH]) for b in range(BUFS)]
        c_t = sb("c_t", [P, 2 * DC])
        neg_e = sb("neg_e", [P, 2 * DC])
        sig = sb("sig", [P, 2 * DC])
        silu = sb("silu", [P, 2 * DC])
        bias = sb("bias", [2, 6 * D])
        mod = sb("mod", [2, 6 * D])
        zeros = sb("zeros", [P, P])
        rows = [ctx.enter_context(nc.psum_tensor(f"rows{b}", [P, CH], F32)) for b in range(2)]
        cols = ctx.enter_context(nc.psum_tensor("cols", [P, 512], F32))

        small_in = sem("m_small_in")
        w_in_sem = [sem(f"m_w{b}") for b in range(BUFS)]
        exped = sem("m_exped")
        silu_ready = sem("m_silu_ready")
        row_done = sem("m_row_done")
        row_copied = sem("m_row_copied")
        mod_ready = sem("m_mod_ready")
        cols_done = sem("m_cols_done")
        zeroed = sem("m_zeroed")
        stored = sem("m_stored")
        block = ctx.enter_context(nc.Block())
        w_mod = io["w_mod"].rearrange("(c p) n -> p c n", p=P)

        @block.sync
        def _(sp):
            sp.dma_start(keep["ident"][:], io["ident"]).then_inc(keep["ident_loaded"], 16)
            sp.dma_start(c_t[:], io["c_t"]).then_inc(small_in, 16)
            sp.dma_start(bias[:], io["b_mod"].partition_broadcast(2)).then_inc(small_in, 16)
            for b in range(BUFS):
                sp.dma_start(wm[b][:], w_mod[:, :, b * CH:(b + 1) * CH]).then_inc(w_in_sem[b], 16)
            with sp.Fori(1, NCH // BUFS) as r:
                for b in range(BUFS):
                    sp.wait_ge(row_done, (r - 1) * BUFS + b + 1)
                    hold(sp)
                    sp.dma_start(wm[b][:], w_mod[:, :, bass.ds((r * BUFS + b) * CH, CH)]).then_inc(
                        w_in_sem[b], 16)
            sp.wait_ge(zeroed, 1)
            for slot in (0, 3, 4, 13):
                sp.dma_start(io["kb"][slot], zeros[:]).then_inc(stored, 16)
                sp.dma_start(io["vb"][slot], zeros[:]).then_inc(stored, 16)
            w_in = io["w_in"].rearrange("(c p) n -> p c n", p=P)
            sp.dma_start(keep["w_in_a"][:, :, 0:VA], w_in[:, :, 0:VA]).then_inc(keep["w_in_first"], 16)
            sp.dma_start(keep["w_in_a"][:, :, VA:], w_in[:, :, VA:2048]).then_inc(keep["w_in_loaded"], 16)
            sp.dma_start(keep["w_in_b"][:], w_in[:, :, 2048:INW]).then_inc(keep["w_in_loaded"], 16)
            sp.wait_ge(mod_ready, 1)
            sp.dma_start(io["mod_rows"], mod[:, 2 * D:6 * D]).then_inc(stored, 16)
            sp.wait_ge(stored, 16 * 9)

        @block.scalar
        def _(act):
            act.wait_ge(small_in, 32)
            nc.scalar.activation(neg_e[:], c_t[:], ACT.Exp, scale=-1.0).then_inc(exped, 1)

        @block.vector
        def _(dve):
            chain = Chain(dve, keep["vector_chain"])
            dve.sem_inc(row_copied, 2)
            nc.vector.memset(zeros[:], 0.0).then_inc(zeroed, 1)
            chain(nc.vector.memset(keep["eps"][:, 0:1], RMS_EPS))
            chain(nc.vector.memset(keep["eps"][:, 1:2], LN_EPS))
            dve.wait_ge(exped, 1)
            chain.then(nc.vector.tensor_scalar(neg_e[:], neg_e[:], 1.0, None, ALU.add))
            chain.then(nc.vector.reciprocal(sig[:], neg_e[:]))
            nc.vector.tensor_tensor(silu[:], c_t[:], sig[:], ALU.mult).then_inc(silu_ready, 1)
            with dve.Fori(0, NCH // 2) as r:
                for b in range(2):
                    j = r * 2 + b
                    dve.wait_ge(row_done, j + 1)
                    nc.vector.tensor_tensor(mod[:, bass.ds(j * CH, CH)], rows[b][0:2, :],
                                            bias[:, bass.ds(j * CH, CH)], ALU.add).then_inc(row_copied, 1)
            dve.wait_ge(row_copied, 2 + NCH)
            chain(nc.vector.tensor_scalar(mod[:, D:3 * D], mod[:, D:3 * D], 1.0, None, ALU.add))
            chain.then(nc.vector.tensor_scalar(mod[:, 4 * D:6 * D], mod[:, 4 * D:6 * D], 1.0, None, ALU.add))
            dve.sem_inc(mod_ready, 1)
            dve.wait_ge(cols_done, 1)
            chain(nc.vector.tensor_copy(keep["mod_cols"][:], cols[:, 0:4 * DC]))
            chain.close()

        @block.tensor
        def _(pe):
            pe.wait_ge(silu_ready, 1)
            with pe.Fori(0, NCH // BUFS) as r:
                for b in range(BUFS):
                    pe.wait_ge(w_in_sem[b], (r + 1) * 16)
                    pe.wait_ge(row_copied, r * BUFS + b + 1)
                    for c in range(DC):
                        mm = nc.tensor.matmul(rows[b % 2][0:2, :], silu[:, 2 * c:2 * c + 2], wm[b][:, c, :],
                                              start=(c == 0), stop=(c == DC - 1))
                    mm.then_inc(row_done, 1)
            pe.wait_ge(mod_ready, 1)
            pe.wait_ge(keep["ident_loaded"], 16)
            for c in range(2 * DC):
                mm = nc.tensor.transpose(cols[:, 2 * c:2 * c + 2], mod[:, c * P:(c + 1) * P],
                                         keep["ident"][0:2, 0:2])
            mm.then_inc(cols_done, 1)



PROJ_CHUNK, ATT_CHUNK = 8, 12
assert 4 * PROJ_CHUNK + 8 * ATT_CHUNK == PH * TOPK


class SideRows:

    def __init__(self, nc, keep, sb, chunk, first, done, down, up, h2, down_ring, up_ring):
        self.nc, self.keep, self.chunk, self.first = nc, keep, chunk, first
        self.down, self.up, self.h2, self.down_ring, self.up_ring = down, up, h2, down_ring, up_ring
        assert 2 * chunk % down_ring == 0 and 2 * chunk % up_ring == 0
        self.idx_down = [sb(f"idx_down{t}", [P, chunk], U32) for t in range(2)]
        self.idx_up = [sb(f"idx_up{t}", [P, chunk], U32) for t in range(2)]
        self.dots, self.acts, self.wgt = ([sb(f"{n}{t}", [P, chunk]) for t in range(2)]
                                          for n in ("dots", "acts", "wgt"))
        self.down_in, self.up_in = keep["down_in"], keep["up_in"]
        self.dotted, self.upped, self.activated = keep["side_dotted"], keep["side_upped"], keep["side_activated"]
        self.dotted_done, self.upped_done, self.activated_done = done

    def place(self, p, j):
        return bass.ds(j * self.chunk + (p * PH * TOPK + self.first), self.chunk)

    def row(self, p, j, k):
        return j * (2 * self.chunk) + (p * self.chunk + k)

    def slot(self, p, k, ring):
        return (p * self.chunk + k) % ring

    def landed(self, way, p, j, k, ring):
        n = p * self.chunk + k
        return j * (2 * self.chunk // ring * 16) + (n // ring + 1) * 16 + self.keep[way][n % ring]

    def take_down(self, pool, chain, p, j):
        if not (isinstance(j, int) and j == 0):
            pool.wait_ge(self.dotted, self.dotted_done + self.down_ring + self.row(p, j - 1, self.chunk))
            hold(pool)
        chain.then(self.nc.gpsimd.tensor_copy(self.idx_down[p][:], self.keep["idx_all"][:, self.place(p, j)]))

    def take_up(self, pool, chain, p, j):
        if not (isinstance(j, int) and j == 0):
            pool.wait_ge(self.upped, self.upped_done + self.up_ring + self.row(p, j - 1, self.chunk))
            hold(pool)
        chain.then(self.nc.gpsimd.tensor_copy(self.idx_up[p][:], self.keep["idx_all"][:, self.place(p, j)]))

    def gather_down(self, pool, io, p, j, k):
        slot = self.slot(p, k, self.down_ring)
        pool.wait_ge(self.dotted, self.dotted_done + self.row(p, j, k) + 1)
        hold(pool)
        pool.indirect_dma_start(self.down[:, slot, :], None, io["down"], bass.IndirectOffsetOnAxis(
            ap=self.idx_down[p][:, k:k + 1], axis=0)).then_inc(self.down_in[slot], 16)

    def gather_up(self, pool, io, p, j, k):
        slot = self.slot(p, k, self.up_ring)
        pool.wait_ge(self.upped, self.upped_done + self.row(p, j, k) + 1)
        hold(pool)
        pool.indirect_dma_start(self.up[:, slot, :], None, io["up"], bass.IndirectOffsetOnAxis(
            ap=self.idx_up[p][:, k:k + 1], axis=0)).then_inc(self.up_in[slot], 16)

    def activate(self, act, p, j):
        act.wait_ge(self.dotted, self.dotted_done + self.down_ring + self.row(p, j, self.chunk))
        self.nc.scalar.activation(self.acts[p][:], self.dots[p][:], ACT.Gelu).then_inc(self.activated, 1)

    def start(self, dve):
        dve.sem_inc(self.dotted, self.down_ring)
        dve.sem_inc(self.upped, self.up_ring)

    def dot_row(self, dve, p, j, k):
        slot = self.slot(p, k, self.down_ring)
        dve.wait_ge(self.down_in[slot], self.landed("down_landed", p, j, k, self.down_ring))
        self.nc.vector.tensor_tensor_reduce(self.down[:, slot, :], self.down[:, slot, :], self.h2[p], 1.0, 0.0,
                                            ALU.mult, ALU.add, self.dots[p][:, k:k + 1]).then_inc(self.dotted, 1)

    def weigh(self, dve, chain, p, j):
        dve.wait_ge(self.activated, self.activated_done + j * 2 + p + 1)
        chain.then(self.nc.vector.tensor_tensor(self.wgt[p][:], self.acts[p][:],
                                                self.keep["gate_all"][:, self.place(p, j)], ALU.mult))

    def add_row(self, dve, p, j, k):
        slot = self.slot(p, k, self.up_ring)
        total = self.keep["sums"][p][:]
        dve.wait_ge(self.up_in[slot], self.landed("up_landed", p, j, k, self.up_ring))
        dve.wait_ge(self.upped, self.upped_done + self.up_ring + self.row(p, j, k))
        self.nc.vector.scalar_tensor_tensor(out=total, in0=self.up[:, slot, :], scalar=self.wgt[p][:, k:k + 1],
                                            in1=total, op0=ALU.mult, op1=ALU.add).then_inc(self.upped, 1)

    def finish(self, dve, chain, pairs):
        dve.wait_ge(self.upped, self.upped_done + self.up_ring + self.row(0, pairs, 0))
        chain.close()

    def count(self, pairs):
        for way, ring in (("down_landed", self.down_ring), ("up_landed", self.up_ring)):
            for slot in range(ring):
                self.keep[way][slot] += self.row(0, pairs, 0) // ring * 16



def projection(nc, io, keep, seq):
    tile0, tiles = SEQS[seq]
    side = seq == 1
    ORDER = (0, 1, 3, 4, 2)
    WIDTH = (512, 512, 512, 512, 256)
    with ExitStack() as ctx:
        def sb(name, shape, dt=F32):
            return ctx.enter_context(nc.sbuf_tensor(f"p{seq}_{name}", shape, dt))

        def sem(name):
            return ctx.enter_context(nc.semaphore(f"p{seq}_{name}"))

        xt = [sb(f"xt{b}", [P, DC, P]) for b in range(2)]
        h1t = [sb(f"h1t{b}", [P, DC, P]) for b in range(2)]
        proj = [sb(f"proj{b}", [P, INW]) for b in range(2)]
        trig = [sb(f"trig{b}", [P, 2 * HALF]) for b in range(2)]
        rot_c = sb("rot_c", [P, 16, 2, HALF])
        rot_s = sb("rot_s", [P, 16, 2, HALF])
        qk_t = [sb(f"qk_t{b}", [P, 13, P]) for b in range(2)]
        if side:
            h2_p = [sb(f"h2_p{t}", [P, D])[:] for t in range(2)]
            rows = SideRows(nc, keep, sb, PROJ_CHUNK, 0, (0, 0, 0), sb("down", [P, 4, D])[:],
                            sb("up", [P, 4, D])[:], h2_p, 4, 4)
        acc = [ctx.enter_context(nc.psum_tensor(f"p{seq}_acc{c}", [P, 512], F32)) for c in range(5)]
        tr = [ctx.enter_context(nc.psum_tensor(f"p{seq}_tr{c}", [P, 4, P], F32)) for c in range(2)]

        x_loaded = [sem(f"x{b}") for b in range(2)]
        h1_ready = sem("h1_ready")
        proj_done = sem("proj_done")
        proj_copied = sem("proj_copied")
        rotated = sem("rotated")
        turned = sem("turned")
        q_copied = sem("q_copied")
        k_copied = sem("k_copied")
        stored = [sem(f"stored{b}") for b in range(2)]
        block = ctx.enter_context(nc.Block())
        STORES = 5

        def pairs(eng, emit):
            if tiles > 2:
                for b in range(2):
                    emit(0, b, False)
                with eng.Fori(1, tiles // 2 - 1) as i:
                    for b in range(2):
                        emit(i, b, False)
            for b in range(2):
                emit(tiles // 2 - 1, b, b == 1)

        @block.sync
        def _(sp):
            def emit(i, b, last):
                sp.wait_ge(h1_ready, i * 2 + b + 2)
                hold(sp)
                sp.dma_start(xt[b][:], io["x_t"][i * 2 + b + tile0]).then_inc(x_loaded[b], 16)
                sp.dma_start(trig[b][:], io["trig"][i * 2 + b + tile0]).then_inc(x_loaded[b], 16)
                if side and b == 0 and isinstance(i, int) and i == 0:
                    for p in range(2):
                        sp.dma_start(h2_p[p], io["h2"][p]).then_inc(keep["h2_prompt_in"], 16)
                    w_in = io["w_in"].rearrange("(c p) n -> p c n", p=P)
                    sp.dma_start(keep["w_in_b"][:], w_in[:, :, 2048:INW]).then_inc(keep["w_in_loaded"], 16)

            pairs(sp, emit)

        if side:
            @block.gpsimd
            def _(pool):
                chain = Chain(pool, keep["gpsimd_chain"])

                def emit(i, b, last):
                    more = not (b == 0 and isinstance(i, int) and i == 0)
                    before = (1 - b, i if b else i - 1)
                    rows.take_down(pool, chain, b, i)
                    if more:
                        rows.take_up(pool, chain, *before)
                    for k in range(PROJ_CHUNK):
                        rows.gather_down(pool, io, b, i, k)
                        if more:
                            rows.gather_up(pool, io, *before, k)
                    chain.close()
                pairs(pool, emit)
                rows.take_up(pool, chain, 1, tiles // 2 - 1)
                for k in range(PROJ_CHUNK):
                    rows.gather_up(pool, io, 1, tiles // 2 - 1, k)
                chain.close()

        @block.scalar
        def _(act):
            for b in range(2):
                act.sem_inc(stored[b], 16)
            act.sem_inc(proj_copied, 5)
            act.sem_inc(q_copied, 1)

            def emit(i, b, last):
                t = i * 2 + b
                act.wait_ge(stored[b], (i * STORES + 1) * 16)
                for o, c in enumerate(ORDER):
                    act.wait_ge(proj_done, t * 5 + o + 1)
                    w = WIDTH[c]
                    nc.scalar.mul(proj[b][:, c * 512:c * 512 + w], acc[c][:, 0:w],
                                  -HD ** -0.5 if c in (0, 3) else 1.0).then_inc(proj_copied, 1)
                    if side and o == 0 and not (b == 0 and isinstance(i, int) and i == 0):
                        rows.activate(act, 1 - b, i if b else i - 1)
                    if o >= 3:
                        g = o - 3
                        act.wait_ge(turned, t * 4 + 2 * g + 1)
                        nc.scalar.mul(qk_t[b][:, 4 * g:4 * g + 4, :], tr[0][:], 1.0).then_inc(q_copied, 1)
                act.wait_ge(proj_copied, t * 5 + 10)
                act.wait_ge(q_copied, t * 2 + 3)
                act.wait_ge(k_copied, t * 2 + 3)
                hold(act)
                slot = t + first_slot(tile0)
                act.dma_start(io["qt"][t + tile0], qk_t[b][:, 0:8, :]).then_inc(stored[b], 16)
                act.dma_start(io["kt"][seq][:, :, bass.ds(t * P, P)], qk_t[b][:, 8:12, :]
                              ).then_inc(stored[b], 16)
                act.dma_start(io["kb"][slot], qk_t[b][:, 12, :]).then_inc(stored[b], 16)
                act.dma_start(io["vb"][slot], proj[b][:, KVB + P:INW]).then_inc(stored[b], 16)
                act.dma_start(io["va"][seq][t], proj[b][:, VA:QB]).then_inc(stored[b], 16)
            pairs(act, emit)
            if side:
                rows.activate(act, 1, tiles // 2 - 1)
            for b in range(2):
                act.wait_ge(stored[b], 16 * (STORES * tiles // 2 + 1))

        @block.vector
        def _(dve):
            chain = Chain(dve, keep["vector_chain"])
            dve.sem_inc(h1_ready, 2)
            dve.sem_inc(k_copied, 1)

            def h1(i, b):
                dve.wait_ge(x_loaded[b], (i + 1) * 32)
                for c in range(DC):
                    mc = keep["mod_cols"]
                    n = chain(nc.vector.tensor_scalar(
                        h1t[b][:, c, :], xt[b][:, c, :], mc[:, 2 * (DC + c) + seq:2 * (DC + c) + seq + 1],
                        mc[:, 2 * c + seq:2 * c + seq + 1], ALU.mult, ALU.add))
                chain.wait()
                dve.sem_inc(h1_ready, 1)

            def emit(i, b, last):
                t = i * 2 + b
                more = side and not (b == 0 and isinstance(i, int) and i == 0)

                def side_rows(order):
                    for what in order.split() if side else ():
                        if what[0] == "d":
                            rows.dot_row(dve, b, i, int(what[1]))
                        elif more:
                            rows.add_row(dve, *before, int(what[1]))

                before = (1 - b, i if b else i - 1)
                side_rows("d0 d1 d2 d3")
                for g, (first, heads, pieces) in enumerate(((QA, 16, 2), (QB, 10, 4))):
                    dve.wait_ge(proj_copied, t * 5 + 5 + pieces)
                    v = proj[b][:, first:first + heads * HD].rearrange("p (h d) -> p h d", d=HD)
                    v = v[:, :, 0:2 * HALF].rearrange("p h (e d) -> p h e d", e=2)
                    cos = trig[b][:, 0:HALF].unsqueeze(1).unsqueeze(1).to_broadcast([P, heads, 2, HALF])
                    sin = trig[b][:, HALF:2 * HALF].unsqueeze(1).to_broadcast([P, heads, HALF])
                    rc, rs = rot_c[:, 0:heads], rot_s[:, 0:heads]
                    chain(nc.vector.tensor_tensor(rc, v, cos, ALU.mult))
                    chain(nc.vector.tensor_tensor(rs[:, :, 0, :], v[:, :, 1, :], sin, ALU.mult))
                    chain(nc.vector.tensor_tensor(rs[:, :, 1, :], v[:, :, 0, :], sin, ALU.mult))
                    chain.wait()
                    chain(nc.vector.tensor_tensor(v[:, :, 0, :], rc[:, :, 0, :], rs[:, :, 0, :], ALU.subtract))
                    chain(nc.vector.tensor_tensor(v[:, :, 1, :], rc[:, :, 1, :], rs[:, :, 1, :], ALU.add))
                    chain.wait()
                    dve.sem_inc(rotated, 1)
                    if g == 0:
                        if more:
                            rows.weigh(dve, chain, *before)
                        side_rows("u0 u1 d4 d5")
                if b == 0:
                    h1(i, 1)
                elif not last:
                    h1(i + 1, 0)
                for g in range(2):
                    dve.wait_ge(turned, t * 4 + 2 * g + 2)
                    w = 4 if g == 0 else 1
                    nc.vector.tensor_copy(qk_t[b][:, 8 + 4 * g:8 + 4 * g + w, :], tr[1][:, 0:w, :]
                                          ).then_inc(k_copied, 1)
                side_rows("u2 u3 d6 u4 d7 u5 u6 u7")
                chain.close()

            h1(0, 0)
            if side:
                rows.start(dve)
                for p in range(2):
                    chain(nc.vector.memset(keep["sums"][p][:], 0.0))
                chain.wait()
                dve.wait_ge(keep["h2_prompt_in"], 32)
            pairs(dve, emit)
            if side:
                rows.weigh(dve, chain, 1, tiles // 2 - 1)
                for k in range(PROJ_CHUNK):
                    rows.add_row(dve, 1, tiles // 2 - 1, k)
                rows.finish(dve, chain, tiles // 2)

        @block.tensor
        def _(pe):
            pe.wait_ge(keep["w_in_first"], 16 * (seq + 1))

            def emit(i, b, last):
                t = i * 2 + b
                pe.wait_ge(h1_ready, t + 3)
                turns = ((QA, 4, 0), (KA, 4, 1), (QB, 4, 0), (KVB, 1, 1))
                for o, c in enumerate(ORDER):
                    pe.wait_ge(proj_copied, t * 5 + o + 1)
                    w = WIDTH[c]
                    if o == 2:
                        pe.wait_ge(keep["w_in_loaded"], 32 * (seq + 1))
                    for k in range(DC):
                        rhs = (keep["w_in_a"][:, k, c * 512:c * 512 + w] if c < 4
                               else keep["w_in_b"][:, k, :])
                        mm = nc.tensor.matmul(acc[c][:, 0:w], h1t[b][:, k, :], rhs,
                                              start=(k == 0), stop=(k == DC - 1))
                    mm.then_inc(proj_done, 1)
                    if o >= 3:
                        g = o - 3
                        pe.wait_ge(rotated, t * 2 + 1 + g)
                        for col, chunks, bank in turns[2 * g:2 * g + 2]:
                            pe.wait_ge((q_copied, k_copied)[bank], t * 2 + 1 + g)
                            for k in range(chunks):
                                mm = nc.tensor.transpose(
                                    tr[bank][:, k, :], proj[b][:, col + k * P:col + (k + 1) * P], keep["ident"][:])
                            mm.then_inc(turned, 1)
            pairs(pe, emit)
        if side:
            rows.count(tiles // 2)



def attention(nc, io, keep, seq):
    tile0, tiles = SEQS[seq]
    S = tiles * P
    KT = S // P
    side = seq == 1
    DOWN, UP = 8, 4
    PAIRS = SEQS[1][1] // 2
    CONSTS = 48
    M_AT, MIX_AT, READ_AT, LN_AT, H2_AT = 2, (3, 4, 5, 6), 7, 9, 12
    with ExitStack() as ctx:
        def sb(name, shape, dt=F32):
            return ctx.enter_context(nc.sbuf_tensor(f"a{seq}_{name}", shape, dt))

        def sem(name):
            return ctx.enter_context(nc.semaphore(f"a{seq}_{name}"))

        def ps(name, shape):
            return ctx.enter_context(nc.psum_tensor(f"a{seq}_{name}", shape, F32))

        k_t = sb("k_t", [P, 4, S])
        v_a = sb("v_a", [P, KT, 512])
        q_t = sb("q_t", [P, 8, P])
        mask_a = sb("mask_a", [P, S])
        mask_b = sb("mask_b", [P, 3 * P])
        k_b = sb("k_b", [P, 3, P])
        v_b = sb("v_b", [P, 3, P])
        rows = sb("rows", [P, 3, D])
        ln = sb("ln", [P, 2, D])
        sink, neg_sink = sb("sink", [P, BH]), sb("neg_sink", [P, BH])
        prob = [sb(f"prob{b}", [P, S if S > 384 else 384]) for b in range(2)]
        prob_t = [sb(f"prob_t{b}", [P, max(KT, 3), P]) for b in range(2)]
        heads_out = sb("heads_out", [P, D])
        merged = sb("merged", [P, D])
        merged_t = sb("merged_t", [P, DC, P])
        if side:
            free = keep["w_in_a"][:].rearrange("p c n -> p (c n)").rearrange("p (s d) -> p s d", d=D)
            down, up = free[:, 0:DOWN, :], free[:, DOWN:DOWN + UP, :]
            h2_p = [free[:, DOWN + UP + t, :] for t in range(2)]
            x_in, heads_raw = free[:, DOWN + UP + 2, :], free[:, DOWN + UP + 3, :]
            earlier = 2 * PAIRS * PROJ_CHUNK
            side_rows = SideRows(nc, keep, sb, ATT_CHUNK, PAIRS * PROJ_CHUNK, (earlier + 4, earlier + 4, 2 * PAIRS),
                                 down, up, h2_p, DOWN, UP)
        else:
            x_in, heads_raw = sb("x_in", [P, D])[:], sb("heads_raw", [P, D])[:]
            gn = sb("gn", [P, DC])
        x2 = sb("x2", [P, D])
        z = merged[:]
        h2 = merged
        neg_m = sb("neg_m", [P, HEADS])
        den = sb("den", [P, HEADS])
        sink_e = sb("sink_e", [P, BH])
        r_den = sb("r_den", [P, HEADS])
        sq = sb("sq", [P, 8])
        rr = sb("rr", [P, 4])
        stats = sb("stats", [P, 12])
        mv = sb("mv", [P, 2])
        lr = sb("lr", [P, 4])
        eps = keep["eps"]

        score = [ps(f"score{b}", [P, 1024]) for b in range(2)]
        turn = ps("turn", [P, 8, P])
        out_ps = [ps(f"out{b}", [P, 512]) for b in range(2)]

        const_in = sem("const_in")
        kv_in = sem("kv_in")
        qa_in, qb_in, win_in, x_sem = sem("qa_in"), sem("qb_in"), sem("win_in"), sem("x_in_s")
        maska_in, maskb_in = sem("maska_in"), sem("maskb_in")
        scored, masked, exped = sem("scored"), sem("masked"), sem("exped")
        turned, copied = sem("turned"), sem("copied")
        summed, head_done = sem("summed"), sem("head_done")
        squared, merged_ready, merged_turned = sem("squared"), sem("merged_ready"), sem("merged_turned")
        merged_copied, den_ready = sem("merged_copied"), sem("den_ready")
        mixed, mix_read, stat_ready, rooted = sem("mixed"), sem("mix_read"), sem("stat_ready"), sem("rooted")
        x2_ready, h2_ready, h2_turned, h2_copied = (sem("x2_ready"), sem("h2_ready"), sem("h2_turned"),
                                                    sem("h2_copied"))
        stored = sem("stored")
        block = ctx.enter_context(nc.Block())

        def keys_of(h):
            return KT if h >= BH else 3

        def tiled(eng, body):
            body(0, True, False)
            if tiles > 2:
                with eng.Fori(1, tiles - 1) as i:
                    body(i, False, False)
            body(tiles - 1, False, True)

        def rows_of(h):
            return range(h % 8 * ATT_CHUNK // 8, (h % 8 + 1) * ATT_CHUNK // 8)

        def chunk_before(i, h):
            return (1, i - 1) if h < 8 else (0, i)

        def before(i, h, n):
            return (i, h - n) if h >= n else (i - 1, h - n + HEADS)

        @block.sync
        def _(sp):
            sp.dma_start(sink[:], io["attn_sink"].partition_broadcast(P)).then_inc(maskb_in, 16)

            def wait(semaphore, value):
                sp.wait_ge(semaphore, value)
                hold(sp)

            def load(i, first, last):
                t = i + tile0
                slot = i + first_slot(tile0)
                if not first:
                    wait(scored, i * HEADS - AH)
                sp.dma_start(q_t[:, 4:8, :], io["qt"][t][:, 4:8, :]).then_inc(qb_in, 16)
                sp.dma_start(k_b[:], io["kb"][bass.ds(slot - 1, 3)].rearrange("s p k -> p s k")
                             ).then_inc(win_in, 16)
                if not first:
                    wait(masked, i * HEADS - AH + 2)
                sp.dma_start(mask_b[:], io["mask_b"][t]).then_inc(maskb_in, 16)
                if not first:
                    wait(summed, i * HEADS - AH + 2)
                sp.dma_start(v_b[:], io["vb"][bass.ds(slot - 1, 3)].rearrange("s p k -> p s k")
                             ).then_inc(win_in, 16)
                if first:
                    sp.dma_start(k_t[:], io["kt"][seq]).then_inc(kv_in, 16)
                else:
                    wait(scored, i * HEADS)
                sp.dma_start(q_t[:, 0:4, :], io["qt"][t][:, 0:4, :]).then_inc(qa_in, 16)
                if not first:
                    wait(masked, i * HEADS + 2)
                sp.dma_start(mask_a[:], io["mask_a"][i][:, 0:S]).then_inc(maska_in, 16)
                if not first:
                    wait(x2_ready, i)
                    sp.dma_start(x_in, io["x"][t - 1]).then_inc(x_sem, 16)
                    return
                rows_dram = io["mod_rows"][seq:seq + 1, 0:3 * D].rearrange("a n -> (a n)")
                sp.dma_start(v_a[:], io["va"][seq].rearrange("n p c -> p n c")).then_inc(kv_in, 16)
                sp.dma_start(rows[:].rearrange("p a d -> p (a d)"), rows_dram.partition_broadcast(P)
                             ).then_inc(const_in, 16)
                for j in range(2):
                    sp.dma_start(ln[:, j, :], io["ln1"][j].partition_broadcast(P)).then_inc(const_in, 16)
                if side:
                    for p in range(2):
                        sp.dma_start(h2_p[p], io["h2"][p]).then_inc(keep["h2_prompt_in"], 16)
                else:
                    sp.dma_start(gn[:], io["gn"]).then_inc(keep["w_out_loaded"], 16)
                    sp.dma_start(keep["w_out"][:], io["w_out"].rearrange("(c p) n -> p c n", p=P)
                                 ).then_inc(keep["w_out_loaded"], 16)

            tiled(sp, load)
            if not side:
                sp.dma_start(keep["keys"][:], io["keys_t"]).then_inc(keep["w_query_loaded"], 16)
                sp.dma_start(keep["w_in_a"][:], io["w_query"].rearrange("(c p) n -> p c n", p=P)
                             ).then_inc(keep["w_query_loaded"], 16)
            sp.wait_ge(x2_ready, tiles)
            sp.dma_start(x_in, io["x"][tile0 + tiles - 1]).then_inc(x_sem, 16)
            if side:
                w_query = io["w_query"].rearrange("(c p) n -> p c n", p=P)
                sp.wait_ge(side_rows.dotted, side_rows.dotted_done + DOWN + side_rows.row(0, tiles, 0))
                for lo, hi in ((0, 4), (6, 7)):
                    sp.dma_start(keep["w_in_a"][:, lo:hi, :], w_query[:, lo:hi, :]).then_inc(
                        keep["w_query_loaded"], 16)

        @block.gpsimd
        def _(pool):
            chain = Chain(pool, keep["gpsimd_chain"])

            def tail(j):
                pool.wait_ge(x2_ready, j + 2)
                pool.wait_ge(h2_turned, j + 1)
                pool.wait_ge(stored, (j + 1) * 48)
                chain.then(nc.gpsimd.tensor_tensor(h2[:], x2[:], rows[:, 2, :], ALU.mult))
                chain.then(nc.gpsimd.tensor_tensor(h2[:], h2[:], rows[:, 1, :], ALU.add))
                pool.sem_inc(h2_ready, 1)

            def body(i, first, last):
                for h in range(HEADS):
                    if h == 4:
                        side_rows.take_down(pool, chain, 1, i)
                        side_rows.take_up(pool, chain, 0, i)
                    for k in rows_of(h):
                        side_rows.gather_down(pool, io, h // 8, i, k)
                    for k in rows_of(h) if not (first and h < 8) else ():
                        side_rows.gather_up(pool, io, *chunk_before(i, h), k)
                    if h == 12:
                        side_rows.take_up(pool, chain, 1, i)
                        if not last:
                            side_rows.take_down(pool, chain, 0, i + 1)
                    if not first and h == H2_AT - 1:
                        tail(i - 1)
                chain.close()

            pool.wait_ge(const_in, CONSTS)
            if side:
                side_rows.take_down(pool, chain, 0, 0)
                chain.close()
                tiled(pool, body)
                for k in range(ATT_CHUNK):
                    side_rows.gather_up(pool, io, 1, tiles - 1, k)
                tail(tiles - 1)
            else:
                with pool.Fori(0, tiles - 1) as j:
                    tail(j)
                    chain.close()
                tail(tiles - 1)
            chain.close()

        @block.scalar
        def _(act):
            act.sem_inc(copied, 1)
            act.sem_inc(stored, 48)

            def copy_probs(i, h):
                g = i * HEADS + h
                n = keys_of(h)
                act.wait_ge(turned, g + 1)
                act.wait_ge(summed, g + 1)
                nc.scalar.copy(prob_t[h % 2][:, 0:n, :], turn[:, 0:n, :]).then_inc(copied, 1)

            def copy_turned(count, n, j, dst_sem):
                act.wait_ge(count, n)
                act.wait_ge(stored, (j + 1) * 48)
                nc.scalar.copy(merged_t[:], turn[:]).then_inc(dst_sem, 1)

            def finish_head(i, h):
                g = i * HEADS + h
                col = (AH + b_head(h) if h < BH else h - BH) * HD
                act.wait_ge(den_ready, g + 1)
                act.wait_ge(summed, g + 3)
                nc.scalar.activation(heads_out[:, col:col + HD], out_ps[h % 2][:, 0:HD], ACT.Copy,
                                     scale=r_den[:, h:h + 1]).then_inc(head_done, 1)

            def square(j):
                act.wait_ge(head_done, (j + 1) * HEADS)
                nc.scalar.copy(heads_raw, heads_out[:]).then_inc(squared, 1)
                act.wait_ge(stored, (j + 1) * 48)
                act.wait_ge(squared, j * 4 + 1)
                for b in range(2):
                    nc.scalar.activation(merged[:, b * 512:(b + 1) * 512],
                                         heads_raw[:, b * 512:(b + 1) * 512], ACT.Square,
                                         accum_out=sq[:, b:b + 1]).then_inc(squared, 1)
                act.wait_ge(squared, j * 4 + 3)
                nc.scalar.activation(sq[:, 2:4], sq[:, 0:2], ACT.Sqrt, bias=eps[:, 0:1], scale=1.0 / 512
                                     ).then_inc(squared, 1)

            def body(i, first, last):
                for h in range(HEADS):
                    g = i * HEADS + h
                    act.wait_ge(masked, g + 3)
                    w = keys_of(h) * P
                    if h < BH:
                        s_at = b_head(h)
                        nc.scalar.activation(sink_e[:, h:h + 1], sink[:, s_at:s_at + 1], ACT.Exp,
                                             bias=neg_m[:, h:h + 1])
                    nc.scalar.activation(prob[h % 2][:, 0:w], prob[h % 2][:, 0:w], ACT.Exp,
                                         bias=neg_m[:, h:h + 1], scale=-1.0, accum_out=den[:, h:h + 1]
                                         ).then_inc(exped, 1)
                    if side and h % 8 == 0 and not (first and h == 0):
                        side_rows.activate(act, *chunk_before(i, h))
                    if not (first and h < 1):
                        copy_probs(*before(i, h, 1))
                    if not first and h == M_AT + 1:
                        copy_turned(merged_turned, i, i - 1, merged_copied)
                    if not (first and h < 2):
                        finish_head(*before(i, h, 2))
                    if not first and h == 1:
                        square(i - 1)
                    if not first and h == READ_AT + 1:
                        root(i - 1)
                    if not first and h == H2_AT + 1:
                        after_h2(i - 1)

            def root(j):
                act.wait_ge(stat_ready, j + 1)
                nc.scalar.activation(lr[:, 0:1], mv[:, 1:2], ACT.Sqrt, bias=eps[:, 1:2], scale=1.0
                                     ).then_inc(rooted, 1)

            def after_h2(j):
                copy_turned(h2_turned, j + 2, j, h2_copied)
                act.wait_ge(h2_ready, j + 1)
                nc.scalar.mul(x2[:], x2[:], ALPHA).then_inc(h2_copied, 1)
                act.wait_ge(h2_copied, (j + 1) * 2)
                hold(act)
                act.dma_start(io["h2"][j + tile0], h2[:]).then_inc(stored, 16)
                act.dma_start(io["x2a"][j + tile0], x2[:]).then_inc(stored, 16)
                act.dma_start(io["h2t"][j + tile0], merged_t[:]).then_inc(stored, 16)

            tiled(act, body)
            last = tiles - 1
            copy_probs(last, HEADS - 1)
            finish_head(last, HEADS - 2)
            finish_head(last, HEADS - 1)
            square(last)
            if side:
                side_rows.activate(act, 1, last)
            copy_turned(merged_turned, last + 1, last, merged_copied)
            root(last)
            after_h2(last)
            act.wait_ge(stored, 48 * (tiles + 1))

        @block.vector
        def _(dve):
            chain = Chain(dve, keep["vector_chain"])
            dve.sem_inc(masked, 2)
            if side:
                side_rows.start(dve)
            dve.sem_inc(x2_ready, 1)
            dve.wait_ge(maskb_in, 32)
            chain.then(nc.vector.tensor_scalar(neg_sink[:], sink[:], -1.0, None, ALU.mult))

            def newton(dst, root, var, tmp):
                chain.then(nc.vector.reciprocal(dst, root))
                chain.then(nc.vector.tensor_tensor(tmp, dst, dst, ALU.mult))
                chain.then(nc.vector.tensor_tensor(tmp, tmp, var, ALU.mult))
                chain.then(nc.vector.tensor_scalar(tmp, tmp, -0.5, 1.5, ALU.mult, ALU.add))
                chain.then(nc.vector.tensor_tensor(dst, dst, tmp, ALU.mult))

            def mask(i, h):
                g = i * HEADS + h
                w = keys_of(h) * P
                dve.wait_ge(scored, g + 1)
                if h == 0:
                    dve.wait_ge(maskb_in, (i + 2) * 16)
                if h == BH:
                    dve.wait_ge(maska_in, (i + 1) * 16)
                if h < BH:
                    m, most = mask_b[:], neg_sink[:, b_head(h):b_head(h) + 1]
                else:
                    m, most = mask_a[:], 3.0e38
                hold(dve)
                nc.vector.tensor_tensor_reduce(
                    prob[h % 2][:, 0:w], score[h % 2][:, 0:w], m, 1.0, most, ALU.add, ALU.min,
                    neg_m[:, h:h + 1]).then_inc(masked, 1)

            def denominator(i, h):
                g = i * HEADS + h
                dve.wait_ge(exped, g + 1)
                if h < BH:
                    chain.then(nc.vector.tensor_tensor(den[:, h:h + 1], den[:, h:h + 1],
                                                       sink_e[:, h:h + 1], ALU.add))
                nc.vector.reciprocal(r_den[:, h:h + 1], den[:, h:h + 1]).then_inc(den_ready, 1)

            def merge(j):
                dve.wait_ge(squared, j * 4 + 4)
                chain.then(nc.vector.tensor_scalar(sq[:, 4:6], sq[:, 0:2], 1.0 / 512, RMS_EPS,
                                                   ALU.mult, ALU.add))
                newton(rr[:, 0:2], sq[:, 2:4], sq[:, 4:6], rr[:, 2:4])
                for b in range(2):
                    chain(nc.vector.tensor_scalar(merged[:, b * 512:(b + 1) * 512],
                                                  heads_raw[:, b * 512:(b + 1) * 512], rr[:, b:b + 1], None,
                                                  ALU.mult))
                chain.wait()
                dve.sem_inc(merged_ready, 1)

            def weigh_w_out(k):
                dve.wait_ge(keep["w_out_loaded"], 32)
                nc.vector.tensor_scalar(keep["w_out"][:, k, :], keep["w_out"][:, k, :], gn[:, k:k + 1], None,
                                        ALU.mult).then_inc(keep["w_out_weighed"], 1)

            def mix(j):
                dve.wait_ge(mixed, j + 1)
                for c in range(2):
                    chain(nc.vector.tensor_tensor(z[:, c * 512:(c + 1) * 512], score[c][:, 512:1024],
                                                  rows[:, 0, c * 512:(c + 1) * 512], ALU.mult))
                chain.wait()
                dve.sem_inc(mix_read, 1)
                dve.wait_ge(x_sem, (j + 1) * 16)
                chain.then(nc.vector.scalar_tensor_tensor(out=z, in0=x_in, scalar=ALPHA, in1=z,
                                                          op0=ALU.mult, op1=ALU.add))
                for b in range(2):
                    chain(nc.vector.bn_stats(stats[:, 6 * b:6 * b + 6], z[:, b * 512:(b + 1) * 512]))
                chain.wait()
                nc.vector.bn_aggr(mv[:], stats[:]).then_inc(stat_ready, 1)

            def layer_norm(j):
                dve.wait_ge(rooted, j + 1)
                dve.wait_ge(stat_ready, j + 1)
                chain.then(nc.vector.tensor_scalar(lr[:, 1:2], mv[:, 1:2], LN_EPS, None, ALU.add))
                newton(lr[:, 2:3], lr[:, 0:1], lr[:, 1:2], lr[:, 3:4])
                dve.wait_ge(stored, (j + 1) * 48)
                chain.then(nc.vector.tensor_scalar(x2[:], z, mv[:, 0:1], lr[:, 2:3],
                                                   ALU.subtract, ALU.mult))
                chain.then(nc.vector.tensor_tensor(x2[:], x2[:], ln[:, 0, :], ALU.mult))
                nc.vector.tensor_tensor(x2[:], x2[:], ln[:, 1, :], ALU.add).then_inc(x2_ready, 1)

            def body(i, first, last):
                for h in range(HEADS):
                    mask(i, h)
                    if not first and h == M_AT:
                        merge(i - 1)
                    if not first and h == READ_AT:
                        mix(i - 1)
                    if not (first and h < 1):
                        denominator(*before(i, h, 1))
                    if first and h == 8:
                        dve.wait_ge(const_in, CONSTS)
                    if side and first and h == 0:
                        dve.wait_ge(keep["h2_prompt_in"], 64)
                    if side:
                        for k in rows_of(h):
                            side_rows.dot_row(dve, h // 8, i, k)
                        if not (first and h < 8):
                            if h % 8 == 0:
                                side_rows.weigh(dve, chain, *chunk_before(i, h))
                            for k in rows_of(h):
                                side_rows.add_row(dve, *chunk_before(i, h), k)
                    if seq == 0 and first and h >= 8:
                        weigh_w_out(h - 8)
                    if not first and h == LN_AT:
                        layer_norm(i - 1)
                chain.close()

            if side:
                chain.close()
            tiled(dve, body)
            last = tiles - 1
            denominator(last, HEADS - 1)
            if side:
                side_rows.weigh(dve, chain, 1, last)
            merge(last)
            def add_rows(lo, hi):
                for k in range(lo, hi) if side else ():
                    side_rows.add_row(dve, 1, last, k)

            add_rows(0, 8)
            mix(last)
            add_rows(8, 10)
            layer_norm(last)
            add_rows(10, ATT_CHUNK)
            if side:
                side_rows.finish(dve, chain, tiles)
            chain.close()

        @block.tensor
        def _(pe):
            ident = keep["ident"]
            pe.sem_inc(summed, 2)
            pe.sem_inc(h2_turned, 1)

            def scores(i, h):
                g = i * HEADS + h
                pe.wait_ge(masked, g + 1)
                lo = (h % 2) * HD
                w = keys_of(h) * P
                q = q_t[lo:lo + HD, 4 + h // 2 if h < BH else (h - BH) // 2, :]
                if h == 0:
                    pe.wait_ge(qb_in, (i + 1) * 16)
                    pe.wait_ge(win_in, (i + 1) * 32)
                if h == BH:
                    pe.wait_ge(qa_in, (i + 1) * 16)
                    pe.wait_ge(kv_in, 32)
                for c in range(0, w, 512):
                    n = min(512, w - c)
                    rhs = k_t[lo:lo + HD, (h - BH) // 2, c:c + n] if h >= BH else \
                        k_b[lo:lo + HD].rearrange("p j k -> p (j k)")
                    mm = nc.tensor.matmul(score[h % 2][:, c:c + n], q, rhs, start=True, stop=True)
                mm.then_inc(scored, 1)

            def turn_probs(i, h):
                g = i * HEADS + h
                pe.wait_ge(exped, g + 1)
                pe.wait_ge(copied, g + 1)
                for k in range(keys_of(h)):
                    mm = nc.tensor.transpose(turn[:, k, :], prob[h % 2][:, k * P:(k + 1) * P], ident[:])
                mm.then_inc(turned, 1)

            def sum_values(i, h):
                g = i * HEADS + h
                pe.wait_ge(copied, g + 2)
                if not (isinstance(i, int) and i == 0 and h < 2):
                    pe.wait_ge(head_done, g - 1)
                n = keys_of(h)
                for k in range(n):
                    if h < BH:
                        v = v_b[:, k, h % 2 * HD:(h % 2 + 1) * HD]
                    else:
                        v = v_a[:, k, (h - BH) * HD:(h - BH + 1) * HD]
                    mm = nc.tensor.matmul(out_ps[h % 2][:, 0:HD], prob_t[h % 2][:, k, :], v,
                                          start=(k == 0), stop=(k == n - 1))
                mm.then_inc(summed, 1)

            def turn_rows(src, count):
                for k in range(DC):
                    mm = nc.tensor.transpose(turn[:, k, :], src[:, k * P:(k + 1) * P], ident[:])
                mm.then_inc(count, 1)

            def turn_merged(j, g):
                pe.wait_ge(merged_ready, j + 1)
                pe.wait_ge(copied, g)
                turn_rows(merged, merged_turned)

            def mix(j, parts):
                pe.wait_ge(merged_copied, j + 1)
                pe.wait_ge(keep["w_out_weighed"], DC)
                for part in parts:
                    c = part // 2
                    for k in range(part % 2 * DC // 2, (part % 2 + 1) * DC // 2):
                        mm = nc.tensor.matmul(score[c][:, 512:1024], merged_t[:, k, :],
                                              keep["w_out"][:, k, c * 512:(c + 1) * 512],
                                              start=(k == 0), stop=(k == DC - 1))
                if part == 3:
                    mm.then_inc(mixed, 1)

            def turn_h2(j, g):
                pe.wait_ge(h2_ready, j + 1)
                pe.wait_ge(mixed, j + 1)
                pe.wait_ge(copied, g)
                turn_rows(h2, h2_turned)

            def body(i, first, last):
                g0 = i * HEADS
                for h in range(HEADS):
                    if h + 1 < HEADS:
                        if not first and h + 1 == BH:
                            pe.wait_ge(mix_read, i)
                        scores(i, h + 1)
                    elif not last:
                        scores(i + 1, 0)
                    if not first and h == M_AT + 1:
                        pe.wait_ge(merged_copied, i)
                    if not first and h == H2_AT + 1:
                        pe.wait_ge(h2_copied, i * 2)
                    turn_probs(i, h)
                    if not (first and h < 1):
                        sum_values(*before(i, h, 1))
                    if not first and h == M_AT:
                        turn_merged(i - 1, g0 + h + 2)
                    if not first and h in MIX_AT:
                        mix(i - 1, (h - MIX_AT[0],))
                    if not first and h == H2_AT:
                        turn_h2(i - 1, g0 + h + 2)

            scores(0, 0)
            tiled(pe, body)
            last = tiles - 1
            sum_values(last, HEADS - 1)
            turn_merged(last, tiles * HEADS + 1)
            pe.wait_ge(masked, tiles * HEADS + 2)
            mix(last, range(4))
            turn_h2(last, tiles * HEADS + 1)
        if side:
            side_rows.count(tiles)



class Retrieval:

    QW = 2 * N_KEYS
    LOW = -3.0e38

    def __init__(self, nc, keep, lanes, sb, sem, ps):
        self.nc, self.keep = nc, keep
        self.keys = keep["keys"] if "keys" in keep else sb("keys", [P, PH * self.QW])
        self.iota = sb("iota", [P, TOPK])
        self.h2t = sb("h2t", [P, DC, P])
        self.q, self.q_t = sb("q", [P, self.QW]), sb("q_t", [P, 2, P])
        self.sc = [sb(f"sc{b}", [P, 2, N_KEYS]) for b in range(2 * lanes)]
        each = lambda name, shape, dt=F32: [sb(f"{name}{b}", shape, dt) for b in range(lanes)]
        self.sc2 = each("sc2_", [P, 2, N_KEYS])
        self.top = each("top", [P, 2, TOPK])
        self.top_i, self.top_f = each("top_i", [P, 2, TOPK], U32), each("top_f", [P, 2, TOPK])
        self.cand, self.cand2 = each("cand", [P, TOPK, TOPK]), each("cand2_", [P, TOPK, TOPK])
        self.best = [sb(f"best{b}", [P, TOPK]) for b in range(2)]
        self.best_i = each("best_i", [P, TOPK], U32)
        self.pair_i, self.pair_f = each("pair_i", [P, 2, TOPK], U32), each("pair_f", [P, 2, TOPK])
        self.hot, self.hot2 = each("hot", [P, 2, TOPK, TOPK]), each("hot2_", [P, 2, TOPK, TOPK])
        self.key_f = each("key_f", [P, 2, TOPK])
        self.neg_b = [sb(f"neg_b{b}", [P, 1]) for b in range(2)]
        self.gate_e = [sb(f"gate_e{b}", [P, TOPK]) for b in range(2)]
        self.gate_s = [sb(f"gate_s{b}", [P, 1]) for b in range(2)]
        self.gate_r = sb("gate_r", [P, 1])
        self.q_ps, self.qt_ps, self.sc_ps = ps("q_ps", [P, 512]), ps("qt_ps", [P, 4, P]), ps("sc_ps", [P, 4, P])
        self.const_in, self.h2t_in = sem("r_const_in"), sem("h2t_in")
        self.q_done, self.q_copied = sem("q_done"), sem("q_copied")
        self.qt_done, self.qt_copied = sem("qt_done"), sem("qt_copied")
        self.sc_done, self.sc_copied = sem("sc_done"), sem("sc_copied")
        self.best_ready, self.gated, self.idx_ready = sem("best_ready"), sem("gated"), sem("idx_ready")

    def load(self, sp, io, tile):
        sp.dma_start(self.h2t[:], io["h2t"][tile]).then_inc(self.h2t_in, 16)
        if "keys" not in self.keep:
            sp.dma_start(self.keys[:], io["keys_t"]).then_inc(self.const_in, 16)
        sp.dma_start(self.iota[:], io["iota"]).then_inc(self.const_in, 16)

    def query(self, pe, m, e, tiles_in):
        nc, w_query = self.nc, self.keep["w_in_a"]
        pe.wait_ge(self.h2t_in, tiles_in * 16)
        pe.wait_ge(self.q_copied, m + 1)
        for k in range(DC):
            mm = nc.tensor.matmul(self.q_ps[:, 0:self.QW], self.h2t[:, k, :],
                                  w_query[:, k, bass.ds(e * self.QW, self.QW)],
                                  start=(k == 0), stop=(k == DC - 1))
        mm.then_inc(self.q_done, 1)
        pe.wait_ge(self.q_copied, m + 2)
        for h in range(2):
            mm = nc.tensor.transpose(self.qt_ps[:, h, :], self.q[:, h * P:(h + 1) * P], self.keep["ident"][:])
        mm.then_inc(self.qt_done, 1)
        pe.wait_ge(self.qt_copied, m + 1)
        pe.wait_ge(self.sc_copied, m + 1)
        for h in range(2):
            mm = nc.tensor.matmul(self.sc_ps[:, h, :], self.q_t[:, h, :],
                                  self.keys[:, bass.ds(e * self.QW + h * N_KEYS, N_KEYS)], start=True, stop=True)
        mm.then_inc(self.sc_done, 1)

    def start_act(self, act):
        act.sem_inc(self.q_copied, 1)
        act.sem_inc(self.sc_copied, 1)

    def move_query(self, act, m, b):
        nc = self.nc
        act.wait_ge(self.q_done, m + 1)
        nc.scalar.copy(self.q[:], self.q_ps[:, 0:self.QW]).then_inc(self.q_copied, 1)
        act.wait_ge(self.qt_done, m + 1)
        nc.scalar.copy(self.q_t[:], self.qt_ps[:, 0:2, :]).then_inc(self.qt_copied, 1)
        act.wait_ge(self.sc_done, m + 1)
        act.wait_ge(self.idx_ready, m + 1)
        nc.scalar.copy(self.sc[b][:], self.sc_ps[:, 0:2, :]).then_inc(self.sc_copied, 1)

    def gates(self, act, m, b):
        act.wait_ge(self.best_ready, m + 1)
        self.nc.scalar.activation(self.gate_e[b][:], self.best[b][:], ACT.Exp, bias=self.neg_b[b][:, 0:1],
                                  accum_out=self.gate_s[b][:, 0:1]).then_inc(self.gated, 1)

    def pick(self, dve, chain, m, work, idx_free=None):
        nc, top, top_i, LOW = self.nc, self.top, self.top_i, self.LOW
        lanes = [(n, self.best[b], self.sc[s], self.sc2[n], idx, self.neg_b[b]) for n, (b, s, idx) in enumerate(work)]
        flat, flat2 = ([v[:].rearrange("p a b -> p (a b)") for v in w] for w in (self.cand, self.cand2))
        halves = [(h, lane) for lane in lanes for h in range(2)]
        dve.wait_ge(self.sc_copied, m + 2)
        hold(dve)
        for h, (n, best, sc, sc2, idx, neg_b) in halves:
            chain(nc.vector.max(top[n][:, h, 0:8], sc[:, h, :]))
        chain.wait()
        for h, (n, best, sc, sc2, idx, neg_b) in halves:
            chain(nc.vector.match_replace(sc2[:, h, :], top[n][:, h, 0:8], sc[:, h, :], LOW))
        chain.wait()
        for h, (n, best, sc, sc2, idx, neg_b) in halves:
            chain(nc.vector.max(top[n][:, h, 8:16], sc2[:, h, :]))
        for h, (n, best, sc, sc2, idx, neg_b) in halves:
            chain(nc.vector.max_index(top_i[n][:, h, 0:8], top[n][:, h, 0:8], sc[:, h, :]))
        chain.wait()
        for n, *_ in lanes:
            chain(nc.vector.tensor_tensor(self.cand[n][:], top[n][:, 0, :].unsqueeze(2).to_broadcast([P, TOPK, TOPK]),
                                          top[n][:, 1, :].unsqueeze(1).to_broadcast([P, TOPK, TOPK]), ALU.add))
        for h, (n, best, sc, sc2, idx, neg_b) in halves:
            chain(nc.vector.max_index(top_i[n][:, h, 8:16], top[n][:, h, 8:16], sc2[:, h, :]))
        chain.wait()
        for n, best, *_ in lanes:
            chain(nc.vector.max(best[:, 0:8], flat[n]))
            chain(nc.vector.tensor_copy(self.top_f[n][:], top_i[n][:]))
        chain.wait()
        for n, best, sc, sc2, idx, neg_b in lanes:
            chain(nc.vector.match_replace(flat2[n], best[:, 0:8], flat[n], LOW))
            chain(nc.vector.max_index(self.best_i[n][:, 0:8], best[:, 0:8], flat[n]))
            chain(nc.vector.tensor_scalar(neg_b[:, 0:1], best[:, 0:1], -1.0, None, ALU.mult))
        chain.wait()
        for n, best, *_ in lanes:
            chain(nc.vector.max(best[:, 8:16], flat2[n]))
        chain.wait()
        dve.sem_inc(self.best_ready, len(lanes))
        for n, best, *_ in lanes:
            chain(nc.vector.max_index(self.best_i[n][:, 8:16], best[:, 8:16], flat2[n]))
        chain.wait()
        for n, *_ in lanes:
            chain(nc.vector.tensor_scalar(self.pair_i[n][:, 0, :], self.best_i[n][:], 4, None, ALU.logical_shift_right))
            chain(nc.vector.tensor_scalar(self.pair_i[n][:, 1, :], self.best_i[n][:], TOPK - 1, None, ALU.bitwise_and))
        chain.wait()
        for n, *_ in lanes:
            chain(nc.vector.tensor_copy(self.pair_f[n][:], self.pair_i[n][:]))
        chain.wait()
        shape = [P, 2, TOPK, TOPK]
        for n, *_ in lanes:
            chain(nc.vector.tensor_tensor(
                self.hot[n][:], self.pair_f[n][:].unsqueeze(3).to_broadcast(shape),
                self.iota[:].unsqueeze(1).unsqueeze(1).to_broadcast(shape), ALU.is_equal))
        chain.wait()
        for n, *_ in lanes:
            chain(nc.vector.tensor_tensor(self.hot2[n][:], self.hot[n][:],
                                          self.top_f[n][:].unsqueeze(2).to_broadcast(shape), ALU.mult))
        chain.wait()
        for n, *_ in lanes:
            chain(nc.vector.tensor_reduce(self.key_f[n][:], self.hot2[n][:], AX_X, ALU.add))
        chain.wait()
        if idx_free:
            idx_free()
        for n, best, sc, sc2, idx, neg_b in lanes:
            nc.vector.scalar_tensor_tensor(out=idx, in0=self.key_f[n][:, 0, :], scalar=float(N_KEYS),
                                           in1=self.key_f[n][:, 1, :], op0=ALU.mult, op1=ALU.add
                                           ).then_inc(self.idx_ready, 1)


def prompt_retrieval(nc, io, keep):
    tiles = SEQS[0][1]
    with ExitStack() as ctx:
        def sb(name, shape, dt=F32):
            return ctx.enter_context(nc.sbuf_tensor(f"r_{name}", shape, dt))

        def sem(name):
            return ctx.enter_context(nc.semaphore(f"r_{name}"))

        def ps(name, shape):
            return ctx.enter_context(nc.psum_tensor(f"r_{name}", shape, F32))

        rt = Retrieval(nc, keep, 2, sb, sem, ps)
        idx = [sb(f"idx{b}", [P, TOPK], U32) for b in range(2)]
        block = ctx.enter_context(nc.Block())

        QUADS = tiles * PH // 4

        @block.sync
        def _(sp):
            rt.load(sp, io, 0)
            sp.wait_ge(rt.q_done, PH)
            sp.dma_start(rt.h2t[:], io["h2t"][1]).then_inc(rt.h2t_in, 16)
            sp.wait_ge(rt.q_done, tiles * PH)
            w_in = io["w_in"].rearrange("(c p) n -> p c n", p=P)
            sp.dma_start(keep["w_in_a"][:, :, 0:VA], w_in[:, :, 0:VA]).then_inc(keep["w_in_first"], 16)
            sp.dma_start(keep["w_in_a"][:, :, VA:], w_in[:, :, VA:2048]).then_inc(keep["w_in_loaded"], 16)

        @block.tensor
        def _(pe):
            pe.wait_ge(keep["w_query_loaded"], 32)
            for t in range(tiles):
                with pe.Fori(0, PH) as e:
                    rt.query(pe, t * PH + e, e, t + 1)

        @block.scalar
        def _(act):
            rt.start_act(act)

            def quad(q, last):
                for pair in range(2):
                    for b in range(2) if not (last and pair == 1) else ():
                        n = pair * 2 + b + 2
                        rt.move_query(act, q * 4 + n, n % 4)
                    for b in range(2):
                        rt.gates(act, q * 4 + pair * 2 + b, b)

            for b in range(2):
                rt.move_query(act, b, b)
            with act.Fori(0, QUADS - 1) as q:
                quad(q, False)
            quad(QUADS - 1, True)

        @block.vector
        def _(dve):
            chain = Chain(dve, keep["vector_chain"])
            dve.sem_inc(rt.idx_ready, 4)
            dve.wait_ge(rt.const_in, 16)

            def pair_of(q, pair, tile):
                e = q * 4 + pair * 2
                m = tile * PH + e
                rt.pick(dve, chain, m + 1, [(b, pair * 2 + b, idx[b][:]) for b in range(2)])
                dve.wait_ge(rt.idx_ready, m + 6)
                for b in range(2):
                    at = (e + b) * TOPK + tile * PH * TOPK
                    chain(nc.vector.tensor_copy(keep["idx_all"][:, bass.ds(at, TOPK)], idx[b][:]))
                dve.wait_ge(rt.gated, m + 2)
                for b in range(2):
                    chain(nc.vector.reciprocal(rt.gate_s[b][:, 0:1], rt.gate_s[b][:, 0:1]))
                chain.wait()
                for b in range(2):
                    at = (e + b) * TOPK + tile * PH * TOPK
                    chain(nc.vector.tensor_scalar(keep["gate_all"][:, bass.ds(at, TOPK)], rt.gate_e[b][:],
                                                  rt.gate_s[b][:, 0:1], None, ALU.mult))
                chain.wait()

            for tile in range(tiles):
                with dve.Fori(0, PH // 4) as q:
                    for pair in range(2):
                        pair_of(q, pair, tile)
                    chain.close()



def experts(nc, io, keep):
    RING = 8
    tile0, tiles = SEQS[1]
    prompt_tiles = SEQS[0][1]
    with ExitStack() as ctx:
        def sb(name, shape, dt=F32):
            return ctx.enter_context(nc.sbuf_tensor(f"e_{name}", shape, dt))

        def sem(name):
            return ctx.enter_context(nc.semaphore(f"e_{name}"))

        def ps(name, shape):
            return ctx.enter_context(nc.psum_tensor(f"e_{name}", shape, F32))

        ident = keep["ident"]
        rt = Retrieval(nc, keep, 1, sb, sem, ps)
        ln = sb("ln", [P, 2, D])
        eps = keep["eps"]
        h2 = sb("h2", [P, D])
        x2a = sb("x2a", [P, D])
        gate2 = sb("gate2", [P, D])
        z = sb("z", [P, D])
        y = sb("y", [P, D])
        down = sb("down", [P, RING, D])
        up = sb("up", [P, RING, D])
        idx = [sb(f"idx{b}", [P, TOPK], U32) for b in range(2)]
        dots = [sb(f"dots{b}", [P, TOPK]) for b in range(2)]
        acts = [sb(f"acts{b}", [P, TOPK]) for b in range(2)]
        wgt = sb("wgt", [P, TOPK])
        diag = [sb(f"diag{b}", [P, TOPK, P]) for b in range(2)]
        stats, mv, lr = sb("stats", [P, 12]), sb("mv", [P, 2]), sb("lr", [P, 4])

        acc = ps("acc", [P, D])
        h2_ps = ps("h2_ps", [P, D])

        const_in = sem("const_in")
        h2_in, h2_moved, res_in, gate2_in = sem("h2_in"), sem("h2_moved"), sem("res_in"), sem("gate2_in")
        down_in, up_in = keep["down_in"], keep["up_in"]
        dotted, activated = sem("dotted"), sem("activated")
        diag_ready, upped = sem("diag_ready"), sem("upped")
        stat_ready, rooted, y_ready, y_stored = sem("stat_ready"), sem("rooted"), sem("y_ready"), sem("y_stored")
        w_query_rest = sem("w_query_rest")
        block = ctx.enter_context(nc.Block())

        def first(n):
            return isinstance(n, int) and n == 0

        def steps(eng, step):
            step(0, 0, 0, 1, 0, True)

            def heads(t, last):
                with eng.Fori(0, PH // 2 - 1) as p:
                    for e in range(2):
                        step(t * PH + p * 2 + e + 1, 1 - e, t, p * 2 + e + 2, t, False)
                step(t * PH + PH - 1, 1, t, None if last else 0, t + 1, False)

            with eng.Fori(0, tiles - 1) as t:
                heads(t, False)
                step(t * PH + PH, 0, t + 1, 1, t + 1, True)
            heads(tiles - 1, True)

        @block.sync
        def _(sp):
            w_query = io["w_query"].rearrange("(c p) n -> p c n", p=P)
            late = ((4, 6), (7, 8))
            for lo, hi in late:
                sp.dma_start(keep["w_in_a"][:, lo:hi, 0:rt.QW], w_query[:, lo:hi, 0:rt.QW]).then_inc(
                    keep["w_query_loaded"], 16)
            rt.load(sp, io, tile0)
            for lo, hi in late:
                sp.dma_start(keep["w_in_a"][:, lo:hi, rt.QW:], w_query[:, lo:hi, rt.QW:]).then_inc(
                    w_query_rest, 16)
            sp.dma_start(h2[:], io["h2"][tile0]).then_inc(h2_in, 16)
            for j in range(2):
                sp.dma_start(ln[:, j, :], io["ln2"][j].partition_broadcast(P)).then_inc(const_in, 16)

            def load_gate2(seq):
                sp.dma_start(gate2[:], io["mod_rows"][seq:seq + 1, 3 * D:4 * D].rearrange("a n -> (a n)")
                             .partition_broadcast(P)).then_inc(gate2_in, 16)

            load_gate2(0)
            for j in range(prompt_tiles + 1):
                if j:
                    sp.wait_ge(stat_ready, j)
                sp.dma_start(x2a[:], io["x2a"][j]).then_inc(res_in, 16)
                if j == prompt_tiles:
                    load_gate2(1)
                if j:
                    sp.wait_ge(y_ready, j)
                    sp.dma_start(io["y"][j - 1], y[:]).then_inc(y_stored, 16)

            def tile(t, last):
                if not last:
                    sp.wait_ge(rt.q_done, t * PH + PH)
                    hold(sp)
                    sp.dma_start(rt.h2t[:], io["h2t"][t + tile0 + 1]).then_inc(rt.h2t_in, 16)
                    sp.wait_ge(h2_moved, t + 1)
                    hold(sp)
                    sp.dma_start(h2[:], io["h2"][t + tile0 + 1]).then_inc(h2_in, 16)
                    sp.wait_ge(stat_ready, t + tile0 + 1)
                    hold(sp)
                    sp.dma_start(x2a[:], io["x2a"][t + tile0 + 1]).then_inc(res_in, 16)
                sp.wait_ge(y_ready, t + tile0 + 1)
                hold(sp)
                sp.dma_start(io["y"][t + tile0], y[:]).then_inc(y_stored, 16)

            with sp.Fori(0, tiles - 1) as t:
                tile(t, False)
            tile(tiles - 1, True)
            sp.wait_ge(y_stored, 16 * (TILES + 1))

        @block.gpsimd
        def _(pool):
            def gather(ring, table, index, landed):
                pool.indirect_dma_start(ring, None, table, bass.IndirectOffsetOnAxis(ap=index, axis=0)
                                        ).then_inc(landed, 16)

            def step(n, b, t, e_next, t_next, start):
                pool.wait_ge(rt.idx_ready, n + 3)
                hold(pool)
                for s in range(TOPK):
                    pool.wait_ge(dotted, n * TOPK + s + 1)
                    hold(pool)
                    gather(down[:, s % RING, :], io["down"], idx[b][:, s:s + 1], down_in[s % RING])
                for s in range(TOPK):
                    pool.wait_ge(upped, n * TOPK + s + 1 + 2 * TOPK - RING)
                    hold(pool)
                    gather(up[:, s % RING, :], io["up"], idx[b][:, s:s + 1], up_in[s % RING])
            steps(pool, step)

        @block.scalar
        def _(act):
            rt.start_act(act)

            def step(n, b, t, e_next, t_next, start):
                if e_next is not None:
                    rt.move_query(act, n + 1, 1 - b)
                act.wait_ge(dotted, (n + 1) * TOPK + RING)
                nc.scalar.activation(acts[b][:], dots[b][:], ACT.Gelu).then_inc(activated, 1)
                if isinstance(e_next, int) and e_next == 0:
                    move_h2(t + 1)
                if e_next is not None:
                    rt.gates(act, n + 1, 1 - b)
                if start and not first(n):
                    root(t + tile0 - 1)

            def root(t):
                act.wait_ge(stat_ready, t + 1)
                nc.scalar.activation(lr[:, 0:1], mv[:, 1:2], ACT.Sqrt, bias=eps[:, 1:2], scale=1.0
                                     ).then_inc(rooted, 1)

            def move_h2(t):
                act.wait_ge(h2_in, (t + 1) * 16)
                nc.scalar.copy(h2_ps[:], h2[:]).then_inc(h2_moved, 1)

            rt.move_query(act, 0, 0)
            move_h2(0)
            rt.gates(act, 0, 0)
            for t in range(prompt_tiles):
                root(t)
            steps(act, step)
            root(TILES - 1)

        @block.vector
        def _(dve):
            chain = Chain(dve, keep["vector_chain"])
            dve.sem_inc(dotted, RING)
            dve.sem_inc(rt.idx_ready, 2)
            dve.wait_ge(const_in, 32)
            dve.wait_ge(rt.const_in, 32)

            def retrieve(m, b):
                rt.pick(dve, chain, m, [(b, b, idx[b][:])], lambda: dve.wait_ge(upped, (m + 1) * TOPK))

            def step(n, b, t, e_next, t_next, start):
                dve.wait_ge(h2_moved, t + 1)
                for s in range(TOPK):
                    row = down[:, s % RING, :]
                    dve.wait_ge(down_in[s % RING], n * 32 + (s // RING + 1) * 16 + keep["down_landed"][s % RING])
                    nc.vector.tensor_tensor_reduce(row, row, h2_ps[:], 1.0, 0.0, ALU.mult, ALU.add,
                                                   dots[b][:, s:s + 1]).then_inc(dotted, 1)
                if start and not first(n):
                    summed_in_psum(t - 1)
                    residual(t + tile0 - 1, acc[:])
                dve.wait_ge(rt.gated, n + 1)
                chain.then(nc.vector.reciprocal(rt.gate_r[:], rt.gate_s[b][:, 0:1]))
                dve.wait_ge(activated, n + 1)
                dve.wait_ge(upped, (n + 1) * TOPK)
                chain.then(nc.vector.scalar_tensor_tensor(out=wgt[:], in0=rt.gate_e[b][:], scalar=rt.gate_r[:, 0:1],
                                                          in1=acts[b][:], op0=ALU.mult, op1=ALU.mult))
                for half in range(2):
                    at = slice(half * TOPK // 2, (half + 1) * TOPK // 2)
                    nc.vector.tensor_tensor(
                        diag[b][:, at, :], ident[:].unsqueeze(1).to_broadcast([P, TOPK // 2, P]),
                        wgt[:, at].unsqueeze(2).to_broadcast([P, TOPK // 2, P]), ALU.mult).then_inc(diag_ready, 1)
                if e_next is not None:
                    retrieve(n + 1, 1 - b)
                if start and not first(n):
                    layer_norm(t + tile0 - 1)
                chain.close()

            def summed_in_psum(t):
                dve.wait_ge(upped, (t * PH + PH) * TOPK + 2 * TOPK)

            def residual(t, experts_sum):
                dve.wait_ge(res_in, (t + 1) * 16)
                dve.wait_ge(gate2_in, 16 if isinstance(t, int) and t < prompt_tiles else 32)
                chain.then(nc.vector.tensor_tensor(z[:], experts_sum, gate2[:], ALU.mult))
                chain.then(nc.vector.tensor_tensor(z[:], z[:], x2a[:], ALU.add))
                for h in range(2):
                    chain(nc.vector.bn_stats(stats[:, 6 * h:6 * h + 6], z[:, h * 512:(h + 1) * 512]))
                chain.wait()
                chain.then(nc.vector.bn_aggr(mv[:], stats[:]))
                dve.sem_inc(stat_ready, 1)

            def layer_norm(t):
                chain(nc.vector.tensor_scalar(lr[:, 1:2], mv[:, 1:2], LN_EPS, None, ALU.add))
                chain.wait()
                dve.wait_ge(rooted, t + 1)
                r, tmp = lr[:, 2:3], lr[:, 3:4]
                chain.then(nc.vector.reciprocal(r, lr[:, 0:1]))
                chain.then(nc.vector.tensor_tensor(tmp, r, r, ALU.mult))
                chain.then(nc.vector.tensor_tensor(tmp, tmp, lr[:, 1:2], ALU.mult))
                chain.then(nc.vector.tensor_scalar(tmp, tmp, -0.5, 1.5, ALU.mult, ALU.add))
                chain.then(nc.vector.tensor_tensor(r, r, tmp, ALU.mult))
                chain.then(nc.vector.tensor_scalar(z[:], z[:], mv[:, 0:1], r, ALU.subtract, ALU.mult))
                chain.then(nc.vector.tensor_tensor(z[:], z[:], ln[:, 0, :], ALU.mult))
                dve.wait_ge(y_stored, (t + 1) * 16)
                chain.then(nc.vector.tensor_tensor(y[:], z[:], ln[:, 1, :], ALU.add))
                dve.sem_inc(y_ready, 1)

            dve.sem_inc(y_stored, 16)
            retrieve(0, 0)
            for t in range(prompt_tiles):
                residual(t, keep["sums"][t][:])
                layer_norm(t)
            chain.close()
            steps(dve, step)
            summed_in_psum(tiles - 1)
            residual(TILES - 1, acc[:])
            layer_norm(TILES - 1)
            chain.close()

        @block.tensor
        def _(pe):
            pe.sem_inc(upped, 2 * TOPK)
            pe.wait_ge(rt.const_in, 32)
            pe.wait_ge(keep["w_query_loaded"], 16 * 6)

            def step(n, b, t, e_next, t_next, start):
                if e_next is not None:
                    rt.query(pe, n + 1, e_next, t_next + 1)
                for s in range(TOPK):
                    if s % (TOPK // 2) == 0:
                        pe.wait_ge(diag_ready, n * 2 + s // (TOPK // 2) + 1)
                    pe.wait_ge(up_in[s % RING], n * 32 + (s // RING + 1) * 16 + keep["up_landed"][s % RING])
                    for c in range(2):
                        mm = nc.tensor.matmul(acc[:, c * 512:(c + 1) * 512], diag[b][:, s, :],
                                              up[:, s % RING, c * 512:(c + 1) * 512], start=start and s == 0,
                                              stop=e_next is None and s == TOPK - 1,
                                              skip_group_check=True)
                    mm.then_inc(upped, 1)

            rt.query(pe, 0, 0, 1)
            pe.wait_ge(w_query_rest, 32)
            steps(pe, step)



def program(nc, io):
    with ExitStack() as outer:
        def sb(name, shape, stack=outer):
            return stack.enter_context(nc.sbuf_tensor(name, shape, F32))

        keep = {n: outer.enter_context(nc.semaphore(n)) for n in
                ("ident_loaded", "w_in_first", "w_in_loaded", "w_out_loaded", "w_out_weighed", "w_query_loaded",
                 "h2_prompt_in", "side_dotted", "side_upped", "side_activated",
                 "vector_chain", "gpsimd_chain")}
        for n in ("down_in", "up_in"):
            keep[n] = [outer.enter_context(nc.semaphore(f"{n}{s}")) for s in range(8)]
        keep["down_landed"], keep["up_landed"] = [0] * 8, [0] * 8
        keep["ident"] = sb("ident_sb", [P, P])
        keep["eps"] = sb("eps", [P, 2])
        keep["mod_cols"] = sb("mod_cols", [P, 4 * DC])
        keep["sums"] = [sb(f"sums{t}", [P, D]) for t in range(2)]
        keep["w_in_a"] = sb("w_in_a", [P, DC, 2048])
        with ExitStack() as early:
            with ExitStack() as first:
                keep["w_in_b"] = sb("w_in_b", [P, DC, INW - 2048], first)
                modulation(nc, io, keep)
                projection(nc, io, keep, 0)
            keep["w_out"] = sb("w_out_sb", [P, DC, D], early)
            keep["idx_all"] = early.enter_context(nc.sbuf_tensor("idx_all", [P, 2 * PH * TOPK], U32))
            keep["gate_all"] = sb("gate_all", [P, 2 * PH * TOPK], early)
            with ExitStack() as prompt:
                keep["keys"] = sb("keys", [P, 2 * PH * N_KEYS], prompt)
                attention(nc, io, keep, 0)
                prompt_retrieval(nc, io, keep)
                del keep["keys"]
            with ExitStack() as second:
                keep["w_in_b"] = sb("w_in_b_again", [P, DC, INW - 2048], second)
                projection(nc, io, keep, 1)
            attention(nc, io, keep, 1)
        experts(nc, io, keep)



def shape_constants():
    i = np.arange(1024)[:, None]
    j = np.arange(1024)[None, :]
    off = np.abs(i - j)
    count = (off <= 64).astype(np.float64) + ((off <= 256) & (off % 4 == 0)) + (off % 16 == 0)
    mask_a = np.where(count > 0, -np.log(np.maximum(count, 1)), BIG).astype(np.float32).reshape(8, P, 1024)
    mask_b = np.full((TILES, P, 3 * P), BIG, np.float32)
    trig = np.zeros((TILES, P, 2 * HALF), np.float32)
    inv = (np.float32(500000.0) ** (-np.arange(HALF, dtype=np.float32) * np.float32(2.0) / np.float32(16))
           ).astype(np.float32)
    for tile0, tiles in SEQS:
        for t in range(tiles):
            q = t * P + np.arange(P)[:, None]
            k = (t - 1) * P + np.arange(3 * P)[None, :]
            mask_b[tile0 + t][(np.abs(q - k) <= 128) & (k >= 0) & (k < tiles * P)] = 0.0
            ang = (q.astype(np.float32) * inv[None, :]).astype(np.float64)
            trig[tile0 + t] = np.concatenate([np.cos(ang), np.sin(ang)], 1).astype(np.float32)
    return {"mask_a": mask_a, "mask_b": mask_b, "trig": trig, "ident": np.eye(P, dtype=np.float32),
            "iota": np.tile(np.arange(TOPK, dtype=np.float32), (P, 1))}


def lay_out(x_prompt, x_sample, c_prompt, c_sample, w_mod, b_mod, w_in, attn_sink, gn_a, gn_b, w_out,
            ln1_g, ln1_b, w_query, sub_keys, expert_down, expert_up, ln2_g, ln2_b):
    x = np.concatenate([np.asarray(x_prompt)[0], np.asarray(x_sample)[0]], 0).reshape(TILES, P, D)
    c = np.stack([np.asarray(c_prompt)[0], np.asarray(c_sample)[0]])
    w = np.array(w_in[0])
    q_b = w[:, QB:KVB].reshape(D, BH, HD)[:, [b_head(j) for j in range(BH)]].reshape(D, BH * HD)
    w = np.concatenate([w[:, :QB], q_b, w[:, KVB:]], 1)
    data = {
        "x": x,
        "x_t": x.reshape(TILES, P, DC, P).transpose(0, 3, 2, 1),
        "c_t": c.reshape(2, DC, P).transpose(2, 1, 0).reshape(P, 2 * DC),
        "w_mod": w_mod[0], "b_mod": b_mod[0], "w_in": w, "attn_sink": attn_sink[0],
        "gn": np.concatenate([gn_a[0], gn_b[0]]).reshape(DC, P).T, "w_out": w_out[0],
        "ln1": np.stack([ln1_g[0], ln1_b[0]]), "w_query": w_query[0],
        "keys_t": np.asarray(sub_keys)[0].transpose(3, 0, 1, 2).reshape(P, PH * 2 * N_KEYS),
        "down": expert_down[0], "up": expert_up[0], "ln2": np.stack([ln2_g[0], ln2_b[0]]),
    }
    data.update(shape_constants())
    return {"in_" + n: np.ascontiguousarray(a) for n, a in data.items()}


SCRATCH = {
    "mod_rows": (2, 4 * D), "qt": (TILES, P, 8, P), "kt0": (P, 4, 256), "kt1": (P, 4, 1024),
    "va0": (2, P, 512), "va1": (8, P, 512), "kb": (SLOTS, P, P), "vb": (SLOTS, P, P),
    "h2": (TILES, P, D), "x2a": (TILES, P, D), "h2t": (TILES, P, DC, P),
}


def declare_and_program(nc, arrays):
    io = {n[3:]: nc.dram_tensor(n, a.shape, F32, kind="ExternalInput").ap() for n, a in arrays.items()}
    for n, shape in SCRATCH.items():
        io[n] = nc.dram_tensor("scratch_" + n, shape, F32, kind="Internal").ap()
    io["kt"], io["va"] = (io["kt0"], io["kt1"]), (io["va0"], io["va1"])
    io["y"] = nc.dram_tensor("y", (TILES, P, D), F32, kind="ExternalOutput").ap()
    program(nc, io)


def kernel(**inputs):
    import concourse.bacc as bacc
    from concourse.bass_utils import run_bass_kernel_spmd

    arrays = lay_out(**inputs)
    nc = bacc.Bacc("TRN2", target_bir_lowering=False, num_devices=1)
    declare_and_program(nc, arrays)
    r = run_bass_kernel_spmd(nc, [arrays], core_ids=[0])
    y = r.results[0]["y"].reshape(TILES * P, D)
    return y[:2 * P].reshape(1, 2 * P, D), y[2 * P:].reshape(1, 8 * P, D)
```
